# Optimizing a Trainium2 kernel written in Bass

```python
import math
import jax, jax.numpy as jnp
from jax import lax
import numpy as np

D_MODEL = 1024
BATCH = 1
SEQ = 512
DEPTH = 2

N_MIXERS = 2
N_META = 16
N_HEADS = 8
HEAD_DIM = D_MODEL // (2 * N_HEADS)
V_DIM = 2 * HEAD_DIM
CONV_WIDTH = 3
CONV_GROUPS = 8
D_FF = 4 * D_MODEL
Q_BLOCK = 128
RMS_EPS = 1e-6
N_ATTN_LAYERS = (DEPTH + 1) // 2
N_CONV_LAYERS = DEPTH // 2


def _rmsnorm(x, g):
    xf = x.astype(jnp.float32)
    y = xf * lax.rsqrt(jnp.mean(xf * xf, axis=-1, keepdims=True) + RMS_EPS)
    return (y * g.astype(jnp.float32)).astype(x.dtype)

def _alibi_slopes(n_heads):
    return jnp.exp2(-8.0 * jnp.arange(1, n_heads + 1, dtype=jnp.float32) / n_heads)

def _lambda_init(layer_idx):
    return 0.8 - 0.6 * math.exp(-0.3 * layer_idx)

def _query_blocks(total_len):
    blocks = [(0, N_META)]
    start = N_META
    while start < total_len:
        end = min(start + Q_BLOCK, total_len)
        blocks.append((start, end))
        start = end
    return blocks

def _diff_attention(h, w_in, w_out, lam_vec, subln_g, lam_init):
    bsz, L, _ = h.shape
    qkv = jnp.einsum('bld,de->ble', h, w_in)
    q, k, v = jnp.split(qkv, 3, axis=-1)
    q = q.reshape(bsz, L, N_HEADS, 2, HEAD_DIM)
    k = k.reshape(bsz, L, N_HEADS, 2, HEAD_DIM)
    v = v.reshape(bsz, L, N_HEADS, V_DIM)
    lv = lam_vec.astype(jnp.float32)
    lam = jnp.exp(jnp.sum(lv[0] * lv[1])) - jnp.exp(jnp.sum(lv[2] * lv[3])) + lam_init
    slopes = _alibi_slopes(N_HEADS)
    scale = HEAD_DIM ** -0.5
    pos = jnp.arange(L, dtype=jnp.int32)
    outs = []
    for qs, qe in _query_blocks(L):
        s = jnp.einsum('bqhcd,bkhcd->bhcqk', q[:, qs:qe], k[:, :qe]).astype(jnp.float32) * scale
        dist = (pos[qs:qe, None] - pos[None, :qe]).astype(jnp.float32)
        bias = -slopes[:, None, None, None] * dist
        s = jnp.where(dist >= 0, s + bias, -jnp.inf)
        p = jax.nn.softmax(s, axis=-1)
        a = (p[:, :, 0] - lam * p[:, :, 1]).astype(v.dtype)
        outs.append(jnp.einsum('bhqk,bkhe->bqhe', a, v[:, :qe]))
    o = jnp.concatenate(outs, axis=1)
    o = _rmsnorm(o, subln_g) * (1.0 - lam_init)
    return jnp.einsum('ble,ed->bld', o.reshape(bsz, L, N_HEADS * V_DIM), w_out)

def _short_conv(h, w_in, conv_w, w_out):
    bcu = jnp.einsum('bld,de->ble', h, w_in)
    b_gate, c_gate, u = jnp.split(bcu, 3, axis=-1)
    u = c_gate * u
    y = lax.conv_general_dilated(
        u, conv_w[:, None, :].astype(u.dtype), window_strides=(1,),
        padding=[(CONV_WIDTH - 1, 0)], dimension_numbers=('NWC', 'WIO', 'NWC'),
        feature_group_count=D_MODEL)
    return jnp.einsum('bld,de->ble', b_gate * y, w_out)

def _sqrelu_mlp(h, w_up, w_down):
    a = jax.nn.relu(jnp.einsum('bld,df->blf', h, w_up))
    return jnp.einsum('blf,fd->bld', a * a, w_down)

def first_inputs(seed: int = 0) -> dict:
    key = jax.random.key(seed)
    ks = jax.random.split(key, 10)
    x = jax.random.normal(ks[0], (BATCH, SEQ, D_MODEL), jnp.float32)
    meta_tokens = jax.random.normal(ks[1], (N_META, D_MODEL), jnp.float32)
    norm_g = 1.0 + 0.05 * jax.random.normal(ks[2], (DEPTH, 4, D_MODEL), jnp.float32)
    w_in = jax.random.normal(ks[3], (DEPTH, D_MODEL, 3 * D_MODEL), jnp.float32) * D_MODEL ** -0.5
    w_out = jax.random.normal(ks[4], (DEPTH, D_MODEL, D_MODEL), jnp.float32) * D_MODEL ** -0.5
    lambda_params = 0.1 * jax.random.normal(ks[5], (N_ATTN_LAYERS, 4, HEAD_DIM), jnp.float32)
    subln_g = 1.0 + 0.05 * jax.random.normal(ks[6], (N_ATTN_LAYERS, V_DIM), jnp.float32)
    conv_w = jax.random.normal(ks[7], (N_CONV_LAYERS, CONV_WIDTH, D_MODEL), jnp.float32) * CONV_WIDTH ** -0.5
    w_up = jax.random.normal(ks[8], (DEPTH, D_MODEL, D_FF), jnp.float32) * D_MODEL ** -0.5
    w_down = jax.random.normal(ks[9], (DEPTH, D_FF, D_MODEL), jnp.float32) * D_FF ** -0.5
    return {'x': x, 'meta_tokens': meta_tokens, 'norm_g': norm_g, 'w_in': w_in, 'w_out': w_out,
            'lambda_params': lambda_params, 'subln_g': subln_g, 'conv_w': conv_w,
            'w_up': w_up, 'w_down': w_down}

def first_block(x, meta_tokens, norm_g, w_in, w_out, lambda_params, subln_g, conv_w, w_up, w_down):
    bsz = x.shape[0]
    meta = jnp.broadcast_to(meta_tokens[None].astype(x.dtype), (bsz, N_META, D_MODEL))
    hres = jnp.concatenate([meta, x], axis=1)
    for i in range(DEPTH):
        h = _rmsnorm(hres, norm_g[i, 0])
        if i % N_MIXERS == 0:
            m = _diff_attention(h, w_in[i], w_out[i], lambda_params[i // N_MIXERS],
                                subln_g[i // N_MIXERS], _lambda_init(i))
        else:
            m = _short_conv(h, w_in[i], conv_w[i // N_MIXERS], w_out[i])
        hres = hres + _rmsnorm(m, norm_g[i, 1])
        h = _rmsnorm(hres, norm_g[i, 2])
        hres = hres + _rmsnorm(_sqrelu_mlp(h, w_up[i], w_down[i]), norm_g[i, 3])
    return hres[:, N_META:]


DEPTH_2 = 1

CHUNK = 64
D_MIX = D_MODEL
D_POOL = D_MIX // 2
POOL_WINDOWS = (2, 4, 8, 16)
N_POOL_GROUPS = len(POOL_WINDOWS)
POOL_GROUP = D_POOL // N_POOL_GROUPS
D_RWKV = D_MIX - D_POOL
RWKV_HEAD = 64
N_RWKV_HEADS = D_RWKV // RWKV_HEAD
DECAY_LORA = 64
AAA_LORA = 64
D_SHIFT = 3 * D_RWKV + DECAY_LORA + AAA_LORA
D_IN = 2 * D_POOL + D_SHIFT + D_RWKV
NORM_EPS = 1e-6
GN_EPS = 64e-5


def rmsnorm(x, gain):
    x32 = x.astype(jnp.float32)
    inv = lax.rsqrt(jnp.mean(x32 * x32, axis=-1, keepdims=True) + NORM_EPS)
    return (x32 * inv * gain.astype(jnp.float32)).astype(x.dtype)

def multi_scale_pool(u, pool_w, pool_scale):
    B, S, _ = u.shape
    u32 = u.astype(jnp.float32).reshape(B, S, N_POOL_GROUPS, POOL_GROUP)
    cs = jnp.cumsum(u32, axis=1)
    cs0 = jnp.concatenate([jnp.zeros_like(cs[:, :1]), cs], axis=1)
    pos = jnp.arange(S)
    outs = []
    for g, w in enumerate(POOL_WINDOWS):
        hi = cs[:, :, g]
        lo = jnp.concatenate([jnp.zeros((B, w - 1, POOL_GROUP), jnp.float32),
                              cs0[:, :S + 1 - w, g]], axis=1)
        cnt = jnp.minimum(pos + 1, w).astype(jnp.float32)[None, :, None]
        outs.append((hi - lo) / cnt - u32[:, :, g])
    pooled = jnp.stack(outs, axis=2)
    mixed = jnp.einsum('bsgc,gcd->bsgd', pooled, pool_w.astype(jnp.float32))
    return (mixed.reshape(B, S, D_POOL) * pool_scale.astype(jnp.float32)).astype(u.dtype)

def rwkv7_time_mix(feat, w0, w_up, a0, a_up, k_k, k_a, r_k, gn_gain, gn_bias):
    B, S, _ = feat.shape
    H, N = N_RWKV_HEADS, RWKV_HEAD
    f = feat.astype(jnp.float32)
    r = f[..., :D_RWKV]
    k = f[..., D_RWKV:2 * D_RWKV]
    v = f[..., 2 * D_RWKV:3 * D_RWKV]
    w_lr = f[..., 3 * D_RWKV:3 * D_RWKV + DECAY_LORA]
    a_lr = f[..., 3 * D_RWKV + DECAY_LORA:]
    ww = w0.astype(jnp.float32) + jnp.tanh(w_lr) @ w_up.astype(jnp.float32)
    decay = jnp.exp(-jnp.exp(-jax.nn.softplus(-ww) - 0.5))
    a = jax.nn.sigmoid(a0.astype(jnp.float32) + a_lr @ a_up.astype(jnp.float32))
    heads = lambda t: t.reshape(B, S, H, N)
    kk = heads(k * k_k.astype(jnp.float32))
    kk = kk / jnp.maximum(jnp.sqrt(jnp.sum(kk * kk, axis=-1, keepdims=True)), 1e-12)
    k = k * (1.0 + (a - 1.0) * k_a.astype(jnp.float32))
    r, k, v, decay, a = heads(r), heads(k), heads(v), heads(decay), heads(a)

    def step(state, inp):
        r_t, k_t, v_t, w_t, kk_t, a_t = inp
        sa = jnp.einsum('bhvk,bhk->bhv', state, -kk_t)
        state = (state * w_t[:, :, None, :]
                 + sa[..., None] * (kk_t * a_t)[:, :, None, :]
                 + v_t[..., None] * k_t[:, :, None, :])
        y_t = jnp.einsum('bhvk,bhk->bhv', state, r_t)
        return state, y_t

    tm = lambda t: jnp.moveaxis(t, 1, 0)
    state0 = jnp.zeros((B, H, N, N), jnp.float32)
    _, y = lax.scan(step, state0, (tm(r), tm(k), tm(v), tm(decay), tm(kk), tm(a)))
    y = jnp.moveaxis(y, 0, 1)
    mu = jnp.mean(y, axis=-1, keepdims=True)
    var = jnp.mean(jnp.square(y - mu), axis=-1, keepdims=True)
    y = (y - mu) * lax.rsqrt(var + GN_EPS)
    y = y * gn_gain.astype(jnp.float32).reshape(H, N) + gn_bias.astype(jnp.float32).reshape(H, N)
    bonus = jnp.sum(r * k * r_k.astype(jnp.float32), axis=-1, keepdims=True) * v
    return (y + bonus).reshape(B, S, D_RWKV)

def second_inputs(seed: int = 0) -> dict:
    key = jax.random.key(seed)
    ks = jax.random.split(key, 20)
    f32 = jnp.float32
    nrm = lambda k, shape, s: jax.random.normal(k, shape, f32) * s
    x = jax.random.normal(ks[0], (BATCH, SEQ, D_MODEL), f32)
    norm_gain = 1.0 + nrm(ks[1], (DEPTH_2, D_MODEL), 0.05)
    w_in = nrm(ks[2], (DEPTH_2, D_MODEL, D_IN), D_MODEL ** -0.5)
    pool_w = nrm(ks[3], (DEPTH_2, N_POOL_GROUPS, POOL_GROUP, POOL_GROUP), POOL_GROUP ** -0.5)
    pool_scale = 1.0 + nrm(ks[4], (DEPTH_2, D_POOL), 0.05)
    shift_mu = jax.random.uniform(ks[5], (DEPTH_2, D_SHIFT), f32, 0.0, 1.0)
    w0 = jax.random.uniform(ks[6], (DEPTH_2, D_RWKV), f32, -4.0, 2.0)
    w_up = nrm(ks[7], (DEPTH_2, DECAY_LORA, D_RWKV), 0.1)
    a0 = nrm(ks[8], (DEPTH_2, D_RWKV), 0.1)
    a_up = nrm(ks[9], (DEPTH_2, AAA_LORA, D_RWKV), 0.5 * AAA_LORA ** -0.5)
    k_k = 0.85 + nrm(ks[10], (DEPTH_2, D_RWKV), 0.05)
    k_a = 1.0 + nrm(ks[11], (DEPTH_2, D_RWKV), 0.05)
    r_k = nrm(ks[12], (DEPTH_2, N_RWKV_HEADS, RWKV_HEAD), 0.1)
    gn_gain = 1.0 + nrm(ks[13], (DEPTH_2, D_RWKV), 0.05)
    gn_bias = nrm(ks[14], (DEPTH_2, D_RWKV), 0.02)
    w_out = nrm(ks[15], (DEPTH_2, D_MIX, D_MODEL), D_MIX ** -0.5)
    final_gain = 1.0 + nrm(ks[16], (D_MODEL,), 0.05)
    return {"x": x, "norm_gain": norm_gain, "w_in": w_in, "pool_w": pool_w,
            "pool_scale": pool_scale, "shift_mu": shift_mu, "w0": w0, "w_up": w_up,
            "a0": a0, "a_up": a_up, "k_k": k_k, "k_a": k_a, "r_k": r_k,
            "gn_gain": gn_gain, "gn_bias": gn_bias, "w_out": w_out, "final_gain": final_gain}

def second_block(x, norm_gain, w_in, pool_w, pool_scale, shift_mu, w0, w_up, a0, a_up,
              k_k, k_a, r_k, gn_gain, gn_bias, w_out, final_gain):
    for l in range(DEPTH_2):
        h = rmsnorm(x, norm_gain[l])
        z = h @ w_in[l]
        u_a = z[..., :D_POOL]
        g_a = z[..., D_POOL:2 * D_POOL]
        sh = z[..., 2 * D_POOL:2 * D_POOL + D_SHIFT]
        g_b = z[..., 2 * D_POOL + D_SHIFT:]
        sh_prev = jnp.pad(sh, ((0, 0), (1, 0), (0, 0)))[:, :-1]
        sh = sh + shift_mu[l] * (sh_prev - sh)
        y_a = multi_scale_pool(u_a, pool_w[l], pool_scale[l])
        y_b = rwkv7_time_mix(sh, w0[l], w_up[l], a0[l], a_up[l], k_k[l], k_a[l],
                             r_k[l], gn_gain[l], gn_bias[l]).astype(x.dtype)
        y = jnp.concatenate([y_a * jax.nn.silu(g_a), y_b * jax.nn.silu(g_b)], axis=-1)
        x = x + y @ w_out[l]
    return rmsnorm(x, final_gain)


def setup_inputs(seed=0):
    out = dict(first_inputs(seed))
    for name, value in second_inputs(seed + 1).items():
        if name != "x":
            out[name + "_2"] = value
    return out


def reference(
    x, meta_tokens, norm_g, w_in, w_out, lambda_params, subln_g, conv_w, w_up, w_down,
    norm_gain_2, w_in_2, pool_w_2, pool_scale_2, shift_mu_2, w0_2, w_up_2, a0_2, a_up_2, k_k_2,
    k_a_2, r_k_2, gn_gain_2, gn_bias_2, w_out_2, final_gain_2,
):
    x = first_block(
        x, meta_tokens, norm_g, w_in, w_out, lambda_params, subln_g, conv_w, w_up, w_down,
    )
    return second_block(
        x, norm_gain_2, w_in_2, pool_w_2, pool_scale_2, shift_mu_2, w0_2, w_up_2, a0_2, a_up_2,
        k_k_2, k_a_2, r_k_2, gn_gain_2, gn_bias_2, w_out_2, final_gain_2,
    )


_drawn_inputs = setup_inputs


def setup_inputs(seed=0):
    import zlib

    import numpy as np

    out = dict(_drawn_inputs(seed))
    spreads = {}
    factors = {'pool_scale_2': 7.931,
     'a0_2': 6.386,
     'k_k_2': 21.71,
     'k_a_2': 3.415,
     'gn_gain_2': 6.109,
     'gn_bias_2': 28.195}
    for name, (base, spread) in spreads.items():
        noise = np.random.default_rng([zlib.crc32(name.encode()), seed]).standard_normal(out[name].shape)
        drawn = base * np.exp(spread * noise) if base else spread * noise
        out[name] = __import__('jax').numpy.asarray(drawn.astype(out[name].dtype))
    for name, factor in factors.items():
        out[name] = (out[name] * factor).astype(out[name].dtype)
    return out
```

```python
from contextlib import ExitStack
import math

import numpy as np
import concourse.bass as bass
from concourse import mybir

F32 = mybir.dt.float32
F32R = mybir.dt.float32r
ACT = mybir.ActivationFunctionType
ALU = mybir.AluOpType

P = 128
D = 1024
KT = D // P
META, SEQ = 16, 512
TOK = META + SEQ
HEADS = 8
CW = 3
FF_CHUNKS = 4
EPS = 1e-6
LAM_INIT = 0.8 - 0.6 * math.exp(-0.3 * 0)
MASKED = -1e32

ALL = (0, TOK)
NEED = (META - (CW - 1), TOK)
OUT = (META, TOK)
SPLIT = META + SEQ // 2
BANK = 512

V_NORM, V_SUBLN, V_CONV, V_LAM = 0, 64, 65, 89
V_N2 = V_LAM + 256
V_POOL, V_MU = V_N2 + 8, V_N2 + 12
V_W0 = V_MU + 13
V_A0, V_KK, V_KA, V_RK, V_GG, V_GB, V_FG = (V_W0 + 4 * i for i in range(1, 8))
V_END = V_FG + 8
C_IDENT, C_ONES, C_DIST = 0, P, 2 * P
C_BLK = C_DIST + TOK
C_MDL, C_MR, C_ME, C_MD = C_BLK + P, C_BLK + 2 * P, C_BLK + 2 * P + 64, C_BLK + 3 * P
C_RESET = C_MD + 64
C_PFIX = C_RESET + SEQ
C_END = C_PFIX + 4 * 16

HD = 64
CH = 64
SUB = 16
NCH = SEQ // CH
PAIRS = 4
NORM_EPS = 1e-6
GN_EPS = 64e-5
DECAY = math.exp(-0.5)
POOL_W = (2, 4, 8, 16)
PAD = 16


def where(cols):
    a, b = cols
    if b - a <= BANK:
        return [(a, b, BANK, BANK + b - a)], slice(BANK, BANK + b - a)
    off = BANK - SPLIT
    return [(a, SPLIT, a + off, BANK), (SPLIT, b, BANK, b + off)], slice(a + off, b + off)


def program(nc, xT, vecs, consts, mats, weights, out):
    NBLK = weights.shape[0]
    with ExitStack() as whole:
        def sb(name, shape, dt=F32, ctx=whole):
            return ctx.enter_context(nc.sbuf_tensor(name, shape, dt))

        def sem(name):
            return whole.enter_context(nc.semaphore(name))

        hres = sb("hres", [P, KT, TOK])
        vec = sb("vec", [P, V_END])
        con = sb("con", [P, C_END])
        raw = sb("raw", [P, 4, D])
        whi = sb("whi", [P, 2, D], F32R)
        wlo = sb("wlo", [P, 2, D], F32R)
        sq = sb("sq", [P, 2, TOK])
        acc = sb("acc", [P, TOK])
        rms = sb("rms", [P, TOK])
        rstd = sb("rstd", [P, 2, TOK])
        t1 = sb("t1", [P, 2, TOK])
        eps_t = sb("eps_t", [P, 2])
        mat = sb("mat", [P, 2 * SEQ])
        first = ExitStack()
        xh = sb("xh", [P, KT, TOK], F32R, first)
        xl = sb("xl", [P, KT, TOK], F32R, first)
        with ExitStack() as attn:
            qT = sb("qT", [P, HEADS, TOK], F32, attn)
            kT = sb("kT", [P, HEADS, TOK], F32, attn)
            vT = sb("vT", [P, HEADS, TOK], F32, attn)
            o_all = sb("o_all", [P, 5 * HEADS, P], F32, attn)
            biasT = sb("biasT", [P, 2, TOK], F32, attn)
            negs = t1
            prob = sb("prob", [P, 2, 2, TOK], F32, attn)
            aT = sb("aT", [P, 2, 5, P], F32, attn)
            vtok = sb("vtok", [P, 2, 5, P], F32, attn)
            o_sc = aT
            o_sq = sb("o_sq", [P, P], F32, attn)
            nmax = sb("nmax", [P, 2, 40], F32, attn)
            den = sb("den", [P, 2, 40], F32, attn)
            rden = sb("rden", [P, 2, 40], F32, attn)
            coef = sb("coef", [P, 40], F32, attn)
            oss = sb("oss", [P, 40], F32, attn)
            orms = sb("orms", [P, 40], F32, attn)
            orstd = sb("orstd", [P, 40], F32, attn)
            lamt = sb("lamt", [P, 2, 64], F32, attn)
            lamd = sb("lamd", [P, 8], F32, attn)
            gsub = sb("gsub", [P, 1], F32, attn)
        with ExitStack() as mlp:
            ah = sb("ah", [P, 2, KT, TOK - 14], F32R, mlp)
            al = sb("al", [P, 2, KT, TOK - 14], F32R, mlp)
            m = sb("m", [P, KT, TOK - 14], F32, mlp)
            act2 = sb("act2", [P, 2, TOK], F32, mlp)
            cb = sb("cb", [P, 3, TOK - 14], F32, mlp)

        first.close()
        with ExitStack() as tri:
            def mt(name, *shape):
                return sb(name, [P, *(shape or (NCH, CH))], F32, tri)
            DL = [mt(f"DL{x}") for x in range(2)]
            MR = [mt(f"MR{x}") for x in range(2)]
            ET, Dm, Ya, Yb, Wm, at_, PT, Sm = (mt(n) for n in ("ET", "Dm", "Ya", "Yb", "Wm", "at_", "PT", "Sm"))
            PB2, PB4 = mt("PB2", 2, 2, 4, CH), mt("PB4", 2, 2, 4, CH)
            BKt = [mt(f"BKt{x}") for x in range(2)]
            UV = [mt(f"UV{x}") for x in range(2)]
            Sg = mt("Sg", CH)
            tri_end = 21 * 4 * NCH * CH
        second = ExitStack()
        x2h = sb("x2h", [P, KT, TOK], F32R, second)
        x2l = sb("x2l", [P, KT, TOK], F32R, second)
        sb("x2pad", [P, (tri_end - 2 * 4 * KT * TOK) // 4], F32, second)
        z = sb("z", [P, 13, 1 + SEQ], F32, second)
        zu = sb("zu", [P, 4, PAD + SEQ], F32, second)
        gate = sb("gate", [P, 8, SEQ], F32, second)
        tw = sb("tw", [HD, SEQ], F32, second)
        AR = sb("AR", [P, NCH, 2, CH], F32, second)
        BK = sb("BK", [P, NCH, 2, CH], F32, second)
        sg, av, cs, Gp, Gt, Gi, kn, k2 = (sb(n, [P, SEQ], F32, second)
                                          for n in ("sg", "av", "cs", "Gp", "Gt", "Gi", "kn", "k2"))
        second.close()

        G = [whole.enter_context(nc.psum_tensor(f"G{i}", [P, 2 * BANK], F32)) for i in range(2)]
        ST = whole.enter_context(nc.psum_tensor("ST", [P, 2 * BANK], F32))
        PO = whole.enter_context(nc.psum_tensor("PO", [P, BANK], F32))
        PV = whole.enter_context(nc.psum_tensor("PV", [P, BANK], F32))

        inputs_loaded = sem("inputs_loaded")
        w_loaded = [sem(f"w_loaded{i}") for i in range(4)]
        hi_ready = sem("hi_ready"); lo_ready = sem("lo_ready")
        block_done = sem("block_done"); tile_out = sem("tile_out")
        x_hi = sem("x_hi"); x_ready = sem("x_ready")
        a_hi = sem("a_hi"); a_ready = sem("a_ready")
        sq_ready = sem("sq_ready"); sq_used = sem("sq_used")
        psq_ready = sem("psq_ready"); psq_added = sem("psq_added"); post_sum = sem("post_sum")
        rms_ready = sem("rms_ready"); rstd_ready = sem("rstd_ready")
        t1_ready = sem("t1_ready"); h_ready = sem("h_ready")
        sqr_ready = sem("sqr_ready")
        lam_prod = sem("lam_prod"); lam_exp = sem("lam_exp"); lam_ready = sem("lam_ready")
        oss_set = sem("oss_set")
        bias_ready = sem("bias_ready")
        scores_ready = sem("scores_ready"); negs_ready = sem("negs_ready"); prob_ready = sem("prob_ready")
        coef_step = sem("coef_step"); a_done = sem("a_done")
        at_ready = sem("at_ready"); at_copied = sem("at_copied")
        v_turned = sem("v_turned"); v_copied = sem("v_copied")
        o_ready = sem("o_ready"); o_copied = sem("o_copied"); oss_ready = sem("oss_ready")
        orms_ready = sem("orms_ready"); orstd_ready = sem("orstd_ready")
        osc_ready = sem("osc_ready"); ot_ready = sem("ot_ready")
        conv_step = sem("conv_step")
        stored = sem("stored")
        sems = {}

        def S(name):
            if name not in sems:
                sems[name] = sem(name)
            return sems[name]

        def bank(n):
            return (G[0][:, 0:BANK], G[0][:, BANK:], G[1][:, 0:BANK], G[1][:, BANK:], ST[:, 0:BANK], ST[:, BANK:],
                    PO[:], PV[:])[n]

        def chunks(ap):
            return ap.rearrange("p (c t) -> p c t", t=CH)

        def col(v, p):
            return vec[:, v + p:v + p + 1]

        HALF = [slice(0, 4), slice(4, 8)]
        ROW = [slice(0, HD), slice(HD, P)]
        B_IN2, B_O2 = 192, 217

        ident = con[:, C_IDENT:C_IDENT + P]
        ones = con[:, C_ONES:C_ONES + P]

        def gain(layer, n, k):
            if layer == 2:
                return col(V_N2, k)
            c = V_NORM + (layer * 4 + n) * KT + k
            return vec[:, c:c + 1]

        B_QKV, B_AO = 0, 24
        B_MLP = [32, 128]
        B_CI, B_CO = 96, 120
        UP = [0, 8, 24, 40]
        DOWN = [16, 32, 48, 56]

        def blocks(eng, b0, n, body):
            lead = 4 if b0 == 0 else 0
            for j in range(lead):
                body(b0 + j, j, (b0 + j) % 4)
            if n - lead >= 8:
                with eng.Fori(0, (n - lead) // 4) as i:
                    for u in range(4):
                        body(i * 4 + (b0 + lead + u), i * 4 + (lead + u), (b0 + u) % 4)
                lead += (n - lead) // 4 * 4
            for j in range(lead, n):
                body(b0 + j, j, (b0 + j) % 4)

        def tile(buf, j, cols):
            if isinstance(j, int):
                return buf[:, j, cols]
            return buf[:, bass.ds(j, 1), cols]

        def queries(i):
            return (0, META) if i == 0 else (META + P * (i - 1), P)

        def keys(i):
            return [(0, META)] + [(META + P * j, P) for j in range(i)]

        def span(i):
            return META + P * i
        S0 = BANK - META

        block = whole.enter_context(nc.Block())

        @block.sync
        def _(sp):
            sp.dma_start(vec[:], vecs).then_inc(inputs_loaded, 16)
            sp.dma_start(con[:], consts).then_inc(inputs_loaded, 16)
            sp.dma_start(mat[:], mats).then_inc(inputs_loaded, 16)
            sp.dma_start(hres[:], xT.rearrange("(k p) t -> p k t", p=P)).then_inc(inputs_loaded, 16)

            def load(b, j, s):
                if not isinstance(b, int):
                    sp.wait_ge(lo_ready, b - 3)
                elif b >= 4:
                    sp.wait_ge(lo_ready, b - 3)
                src = weights[b] if isinstance(b, int) else weights[bass.ds(b, 1)].rearrange("b p n -> p (b n)")
                sp.dma_start(raw[:, s], src).then_inc(w_loaded[s], 16)
            blocks(sp, 0, NBLK, load)
            for k in range(KT):
                sp.wait_ge(S("out_ready"), k + 1)
                sp.dma_start(out[k * P:(k + 1) * P, :], hres[:, k, META:]).then_inc(stored, 16)
            sp.wait_ge(stored, 16 * KT)

        @block.gpsimd
        def _(pool):
            def low(b, j, s):
                pool.wait_ge(hi_ready, b + 1)
                if not isinstance(b, int) or b >= 2:
                    pool.wait_ge(block_done, b - 1)
                nc.gpsimd.tensor_tensor(wlo[:, s % 2], raw[:, s], whi[:, s % 2].bitcast(F32), ALU.subtract)\
                    .then_inc(lo_ready, 1)
            blocks(pool, 0, NBLK, low)

        @block.scalar
        def _(act):
            def split(b, s):
                if isinstance(b, int):
                    if b >= NBLK:
                        return
                    act.wait_ge(w_loaded[s], 16 * (b // 4 + 1))
                    if b >= 2:
                        act.wait_ge(block_done, b - 1)
                nc.scalar.activation(whi[:, s % 2], raw[:, s], ACT.Copy).then_inc(hi_ready, 1)

            def step(b0, n, evac=None):
                def body(b, j, s):
                    if isinstance(b, int):
                        split(b + 2, (s + 2) % 4)
                    else:
                        i4 = b - s
                        s2 = (s + 2) % 4
                        act.wait_ge(w_loaded[s2], (i4 + 4 * ((s + 2) // 4)) * 4 + 16)
                        act.wait_ge(block_done, b + 1)
                        nc.scalar.activation(whi[:, s2 % 2], raw[:, s2], ACT.Copy).then_inc(hi_ready, 1)
                    if evac:
                        evac(b, j, s)
                blocks(act, b0, n, body)

            def stat_root(s, cols):
                if s % 2 == 0:
                    act.wait_ge(sq_used, 8 * (s // 2 + 1))
                else:
                    act.wait_ge(post_sum, s // 2 + 1)
                if s >= 1:
                    act.wait_ge(rstd_ready, s)
                _, pos = where(cols)
                nc.scalar.activation(rms[:, cols[0]:cols[1]], ST[:, pos], ACT.Sqrt, scale=1.0 / D, bias=eps_t[:, 0:1])\
                    .then_inc(rms_ready, 1)

            def prenorm(f, s, layer, n, cols, h0):
                c = slice(*cols)
                for k in range(KT):
                    if h0 is None:
                        act.wait_ge(inputs_loaded, 64)
                    else:
                        act.wait_ge(h_ready, h0 + k + 1)
                    nc.scalar.activation((x2h if layer == 2 else xh)[:, k, c], hres[:, k, c], ACT.Copy,
                                         scale=gain(layer, n, k)).then_inc(x_hi, 1)
                    if 4 * s + k >= 2:
                        act.wait_ge(sq_used, 4 * s + k - 1)
                    nc.scalar.activation(sq[:, k % 2, c], hres[:, k, c], ACT.Square).then_inc(sq_ready, 1)
                stat_root(s, cols)

            def post_squares(b0, s, cols):
                w = cols[1] - cols[0]

                def evac(b, j, s4):
                    act.wait_ge(tile_out, b + 1)
                    n = 4 * (s - 1) + j
                    if n >= 2:
                        act.wait_ge(psq_added, n - 1)
                    nc.scalar.activation(sq[:, s4 % 2, 0:w], m[:, j, 0:w], ACT.Square).then_inc(psq_ready, 1)
                straight(b0, evac)

            def mlp(layer, cols, s):
                b0 = B_MLP[layer]
                w = cols[1] - cols[0]
                for c in range(FF_CHUNKS + 1):
                    if c < FF_CHUNKS:
                        f = 5 * layer + c
                        n0 = 32 * layer + 8 * c

                        def up(b, j, s4):
                            act.wait_ge(tile_out, b + 1)
                            nc.scalar.activation(tile(ah[:, f % 2], j, slice(0, w)), t1[:, s4 % 2, 0:w], ACT.Square)\
                                .then_inc(a_hi, 1)
                            if 8 * f >= 2:
                                act.wait_ge(a_ready, j + (8 * f - 1))
                            elif isinstance(j, int) and j >= 2:
                                act.wait_ge(a_ready, j - 1)
                            nc.scalar.activation(act2[:, s4 % 2, 0:w], t1[:, s4 % 2, 0:w], ACT.Square)\
                                .then_inc(sqr_ready, 1)
                        straight(b0 + UP[c], up) if f == 0 else step(b0 + UP[c], 8, up)
                    if c >= 1 and c < FF_CHUNKS:
                        step(b0 + DOWN[c - 1], 8)
                    elif c == FF_CHUNKS:
                        post_squares(b0 + DOWN[c - 1], s, cols)

            def straight(b0, evac):
                for j in range(8):
                    b = b0 + j
                    split(b + 2, (b + 2) % 4)
                    evac(b, j, b % 4)

            act.wait_ge(oss_set, 3)
            act.wait_ge(inputs_loaded, 64)
            split(0, 0)
            split(1, 1)
            prenorm(0, 0, 0, 0, ALL, None)
            act.wait_ge(lam_prod, 2)
            nc.scalar.activation(lamd[:, 2:4], lamd[:, 0:2], ACT.Exp).then_inc(lam_exp, 1)
            step(B_QKV, 24)

            for n in range(40 + 3):
                if n < 40:
                    h, i = divmod(n, 5)
                    rows, w = queries(i)[1], span(i)
                    if i == 0:
                        if h >= 2:
                            act.wait_ge(negs_ready, 10 * (h - 1))
                        slope = 2.0 ** (-8.0 * (h + 1) / HEADS)
                        nc.scalar.activation(biasT[:, h % 2], con[:, C_DIST:C_DIST + TOK], ACT.Copy, scale=slope)\
                            .then_inc(bias_ready, 1)
                    for c in range(2):
                        act.wait_ge(negs_ready, 2 * n + c + 1)
                        if n >= 2:
                            act.wait_ge(at_ready, n - 1)
                        nc.scalar.activation(prob[0:rows, n % 2, c, 0:w], negs[0:rows, c, 0:w], ACT.Exp, scale=-1.0,
                                             bias=nmax[0:rows, c, n:n + 1], accum_out=den[0:rows, c, n:n + 1])\
                            .then_inc(prob_ready, 1)
                    if i == 0:
                        act.wait_ge(v_turned, h + 1)
                        if h >= 2:
                            act.wait_ge(o_ready, 5 * (h - 1))
                        nc.scalar.activation(vtok[:, h % 2, 1:5, :], PV[:].rearrange("p (j v) -> p j v", v=P), ACT.Copy)\
                            .then_inc(v_copied, 1)
                        nc.scalar.activation(vtok[0:META, h % 2, 0, :], PO[0:META, P:2 * P], ACT.Copy)\
                            .then_inc(v_copied, 1)
                if 1 <= n <= 40:
                    t = n - 1
                    h, i = divmod(t, 5)
                    rows = queries(i)[1]
                    act.wait_ge(at_ready, t + 1)
                    if t >= 2:
                        act.wait_ge(o_ready, t - 1)
                    if i > 0:
                        nc.scalar.activation(aT[:, t % 2, 1:1 + i, :], ST[:, 0:P * i].rearrange("p (j v) -> p j v", v=P),
                                             ACT.Copy)
                    nc.scalar.activation(aT[0:META, t % 2, 0, 0:rows], ST[0:META, BANK:BANK + rows], ACT.Copy)\
                        .then_inc(at_copied, 1)
                if 2 <= n <= 41:
                    t = n - 2
                    h, i = divmod(t, 5)
                    rows = queries(i)[1]
                    act.wait_ge(o_ready, t + 1)
                    nc.scalar.activation(o_all[0:rows, t, :], PO[0:rows, 0:P], ACT.Copy, scale=rden[0:rows, 0, t:t + 1])\
                        .then_inc(o_copied, 1)
                    act.wait_ge(o_copied, t + 1)
                    if t >= 1:
                        act.wait_ge(oss_ready, t)
                    nc.scalar.activation(o_sq[0:rows, :], o_all[0:rows, t, :], ACT.Square,
                                         accum_out=oss[0:rows, t:t + 1]).then_inc(oss_ready, 1)
            act.wait_ge(oss_ready, 40)
            nc.scalar.activation(orms[:], oss[:], ACT.Sqrt, scale=1.0 / P, bias=eps_t[:, 0:1]).then_inc(orms_ready, 1)
            pieces, pos = where(ALL)
            for h in range(HEADS):
                act.wait_ge(ot_ready, h + 1)
                nc.scalar.activation(xh[:, h, :], G[h % 2][:, pos], ACT.Copy, scale=gsub[:, 0:1]).then_inc(x_hi, 1)

            post_squares(B_AO, 1, NEED)
            stat_root(1, NEED)
            prenorm(2, 2, 0, 2, NEED, 0)
            mlp(0, NEED, 3)
            stat_root(3, NEED)
            prenorm(3, 4, 1, 0, NEED, 8)

            for j in range(KT):
                for r in range(3):
                    b = B_CI + 3 * j + r
                    split(b + 2, (b + 2) % 4)
                act.wait_ge(conv_step, 5 * j + 5)
                nc.scalar.activation(ah[:, 0, j, 0:SEQ], m[:, j, 2:2 + SEQ], ACT.Copy).then_inc(a_hi, 1)
            post_squares(B_CO, 5, OUT)
            stat_root(5, OUT)
            prenorm(4, 6, 1, 2, OUT, 16)
            mlp(1, OUT, 7)
            stat_root(7, OUT)
            prenorm(5, 8, 2, 0, OUT, 24)
            step(B_IN2, 25)

            act.wait_ge(S("shifted"), 1)
            nc.scalar.activation(tw[:], z[0:HD, 0, 1:], ACT.Tanh).then_inc(S("tanh_ready"), 1)
            for j in range(8):
                act.wait_ge(tile_out, B_IN2 + 18 + j)
                nc.scalar.activation(gate[:, j], gate[:, j], ACT.Silu).then_inc(S("gate_ready"), 1)

            def copy_out(need, n, done, dst, src):
                act.wait_ge(S(need), n)
                nc.scalar.activation(dst, src, ACT.Copy).then_inc(S(done), 1)

            for p in range(PAIRS):
                zk, zr, zv = z[:, 1 + p, 1:], z[:, 5 + p, 1:], z[:, 9 + p, 1:]
                if p >= 1:
                    act.wait_ge(S("yb_ready"), p)
                act.wait_ge(S("ww_ready"), p + 1)
                nc.scalar.activation(sg[:], bank(4), ACT.Sigmoid, bias=col(V_W0, p)).then_inc(S("sg_ready"), 1)
                act.wait_ge(S("aa_ready"), p + 1)
                nc.scalar.activation(av[:], bank(5), ACT.Sigmoid, bias=col(V_A0, p)).then_inc(S("av_ready"), 1)
                act.wait_ge(S("shifted"), 2 + p)
                nc.scalar.activation(kn[:], zk, ACT.Square, scale=col(V_KK, p)).then_inc(S("ksq_ready"), 1)
                act.wait_ge(S("knorm_sum"), p + 1)
                nc.scalar.activation(kn[:], bank(6), ACT.Sqrt).then_inc(S("kn_ready"), 1)
                act.wait_ge(S("cp_ready"), p + 1)
                nc.scalar.activation(Gt[:], cs[:], ACT.Exp, scale=-DECAY).then_inc(S("Gt_ready"), 1)
                nc.scalar.activation(Gi[:], cs[:], ACT.Exp, scale=DECAY).then_inc(S("Gi_ready"), 1)
                nc.scalar.activation(Gp[:], Gp[:], ACT.Exp, scale=-DECAY).then_inc(S("Gp_ready"), 1)
                act.wait_ge(S("rv_turned"), p + 1)
                for x in range(2):
                    nc.scalar.activation(UV[x][ROW[1 - x]], chunks(bank(6))[ROW[1 - x]], ACT.Copy).then_inc(S("vt_out"), 1)
                copy_out("at_turned", p + 1, "at_out", at_[:], chunks(bank(7)))
                for g in range(2):
                    copy_out("d2_ready", 2 * p + g + 1, "d2_out", PB2[:, g].rearrange("p k c t -> p (k c t)"), bank(g))
                for x in range(2):
                    copy_out("bk_turned", 2 * p + x + 1, "bk_out", BKt[x][:], chunks(bank(6 + x)))
                copy_out("w_ready", p + 1, "w_out", Wm[:], chunks(bank(2)))
                for g in range(2):
                    copy_out("d4_ready", 2 * p + g + 1, "d4_out", PB4[:, g].rearrange("p k c t -> p (k c t)"), bank(g))
                for g in range(2):
                    copy_out("d8_ready", 2 * p + g + 1, "d8_out", Dm[:, HALF[g]], chunks(bank(2 + g)[:, 0:4 * CH]))
                for g in range(2):
                    copy_out("td_ready", 2 * p + g + 1, "td_out", PB2[:, g, 0], chunks(bank(g)[:, 0:4 * CH]))
                for g in range(2):
                    copy_out("ht_ready", 2 * p + g + 1, "ht_out", PB2[:, g, 1], chunks(bank(2 + g)[:, 0:4 * CH]))
                copy_out("q_ready", p + 1, "q_out", Yb[:], chunks(bank(4)))
                copy_out("pt_ready", p + 1, "pt_out", PT[:], chunks(bank(5)))
                act.wait_ge(S("y_ready"), p + 1)
                nc.scalar.activation(sg[:], bank(0), ACT.Copy).then_inc(S("yt_out"), 1)
                act.wait_ge(S("yc_ready"), p + 1)
                nc.scalar.activation(kn[:], av[:], ACT.Square).then_inc(S("ysq_ready"), 1)
                act.wait_ge(S("var_ready"), p + 1)
                nc.scalar.activation(kn[:], bank(2), ACT.Sqrt, scale=1.0 / HD, bias=eps_t[:, 1:2]).then_inc(S("sd_ready"), 1)

            for k in range(KT):
                if k < 4:
                    act.wait_ge(S("ya_ready"), k + 1)
                    src = zu[:, k, PAD:]
                else:
                    act.wait_ge(S("yb_ready"), k - 3)
                    src = z[:, 1 + k, 1:]
                if k == 0:
                    act.wait_ge(S("yb_ready"), PAIRS)
                nc.scalar.activation(x2h[:, k, META:], src, ACT.Copy).then_inc(x_hi, 1)
            for j in range(KT):
                split(B_O2 + j + 2, (B_O2 + j + 2) % 4)
                act.wait_ge(tile_out, B_O2 + j + 1)
                n = 32 + j
                act.wait_ge(psq_added, n - 1)
                nc.scalar.activation(sq[:, (B_O2 + j) % 2, 0:SEQ], hres[:, j, META:], ACT.Square).then_inc(psq_ready, 1)
            stat_root(9, OUT)

        @block.vector
        def _(dve):
            def stat_recip(s, cols):
                c = slice(*cols)
                dve.wait_ge(rms_ready, s + 1)
                nc.vector.reciprocal(rstd[:, s % 2, c], rms[:, c]).then_inc(rstd_ready, 1)

            def low_x(f, layer, n, k, c):
                dve.wait_ge(x_hi, 8 * f + k + 1)
                hi, lo = (x2h, x2l) if layer == 2 else (xh, xl)
                nc.vector.scalar_tensor_tensor(lo[:, k, c], hres[:, k, c], gain(layer, n, k), hi[:, k, c].bitcast(F32),
                                               ALU.mult, ALU.subtract).then_inc(x_ready, 1)

            def postnorm(s, layer, n, cols, h0, pre):
                c = slice(*cols)
                w = cols[1] - cols[0]
                dve.wait_ge(rstd_ready, s + 1)
                for k in range(KT + 2):
                    if k < KT:
                        if k >= 2:
                            dve.wait_ge(h_ready, h0 + k - 1)
                        nc.vector.scalar_tensor_tensor(t1[:, k % 2, 0:w], m[:, k, 0:w], gain(layer, n, k),
                                                       rstd[:, s % 2, c], ALU.mult, ALU.mult).then_inc(t1_ready, 1)
                    if 1 <= k <= KT:
                        dve.wait_ge(t1_ready, h0 + k)
                        nc.vector.tensor_tensor(hres[:, k - 1, c], hres[:, k - 1, c], t1[:, (k - 1) % 2, 0:w], ALU.add)\
                            .then_inc(h_ready, 1)
                    if k >= 2 and pre:
                        low_x(*pre, k - 2, c)

            def out_tiles(b0, cols, before=None, s=None):
                _, pos = where(cols)
                w = cols[1] - cols[0]

                def body(b, j, s):
                    dve.wait_ge(block_done, b + 1)
                    mt = tile(m, j, slice(0, w))
                    if before is None:
                        nc.vector.tensor_copy(mt, G[s % 2][:, pos]).then_inc(tile_out, 1)
                    else:
                        dve.wait_ge(tile_out, j + (before + 1))
                        nc.vector.tensor_tensor(mt, G[s % 2][:, pos], mt, ALU.add).then_inc(tile_out, 1)
                if s is None:
                    blocks(dve, b0, 8, body)
                    return
                for j in range(KT + 1):
                    if j < KT:
                        body(b0 + j, j, (b0 + j) % 4)
                    if j >= 1:
                        n = 4 * (s - 1) + j - 1
                        dve.wait_ge(psq_ready, n + 1)
                        if j == 1:
                            nc.vector.tensor_copy(acc[:, 0:w], sq[:, (j - 1) % 2, 0:w]).then_inc(psq_added, 1)
                        else:
                            dve.wait_ge(psq_added, n)
                            nc.vector.tensor_tensor(acc[:, 0:w], acc[:, 0:w], sq[:, (j - 1) % 2, 0:w], ALU.add)\
                                .then_inc(psq_added, 1)

            def mlp(layer, cols, s):
                b0 = B_MLP[layer]
                _, pos = where(cols)
                w = cols[1] - cols[0]
                c0 = slice(*cols)
                for c in range(FF_CHUNKS + 1):
                    if c < FF_CHUNKS:
                        f = 5 * layer + c
                        n0 = 32 * layer + 8 * c

                        def low(j, s4):
                            dve.wait_ge(a_hi, j + (8 * f + 1))
                            dve.wait_ge(sqr_ready, j + (n0 + 1))
                            nc.vector.tensor_tensor(tile(al[:, f % 2], j, slice(0, w)), act2[:, s4 % 2, 0:w],
                                                    tile(ah[:, f % 2], j, slice(0, w)).bitcast(F32), ALU.subtract)\
                                .then_inc(a_ready, 1)

                        def up(b, j, s4):
                            dve.wait_ge(block_done, b + 1)
                            if isinstance(j, int) and n0 + j < 2:
                                pass
                            else:
                                dve.wait_ge(sqr_ready, j + (n0 - 1))
                            nc.vector.scalar_tensor_tensor(t1[:, s4 % 2, 0:w], G[s4 % 2][:, pos], 0.0, rstd[:, s % 2, c0],
                                                           ALU.max, ALU.mult).then_inc(tile_out, 1)
                            low(j, s4)
                        if f == 0:
                            for j in range(8):
                                up(b0 + UP[c] + j, j, (b0 + UP[c] + j) % 4)
                        else:
                            blocks(dve, b0 + UP[c], 8, up)
                    if c >= 1:
                        out_tiles(b0 + DOWN[c - 1], cols, None if c == 1 else b0 + DOWN[c - 2],
                                  s + 1 if c == FF_CHUNKS else None)

            nc.vector.memset(eps_t[:, 0:1], EPS).then_inc(oss_set, 1)
            nc.vector.memset(eps_t[:, 1:2], GN_EPS).then_inc(oss_set, 1)
            nc.vector.memset(oss[:], 1.0).then_inc(oss_set, 1)
            dve.wait_ge(inputs_loaded, 64)
            lam = vec[:, V_LAM:V_LAM + 256].rearrange("p (a b n) -> p a b n", a=2, b=2)
            for a in range(2):
                nc.vector.tensor_tensor_reduce(lamt[:, a, :], lam[:, a, 0, :], lam[:, a, 1, :], 1.0, 0.0, ALU.mult,
                                               ALU.add, lamd[:, a:a + 1]).then_inc(lam_prod, 1)
            nc.vector.tensor_scalar(gsub[:], vec[:, V_SUBLN:V_SUBLN + 1], 1.0 - LAM_INIT, None, ALU.mult)\
                .then_inc(lam_ready, 1)
            for k in range(KT):
                low_x(0, 0, 0, k, slice(*ALL))
            dve.wait_ge(lam_exp, 1)
            nc.vector.tensor_scalar(lamd[:, 4:5], lamd[:, 3:4], lamd[:, 2:3], -LAM_INIT, ALU.subtract, ALU.add)\
                .then_inc(lam_ready, 1)
            stat_recip(0, ALL)
            dve.wait_ge(rstd_ready, 1)
            _, pos = where(ALL)

            for b in range(24):
                h, r = divmod(b, 3)
                dve.wait_ge(block_done, b + 1)
                nc.vector.scalar_tensor_tensor((qT, kT, vT)[r][:, h, :], G[b % 2][:, pos], 0.125 if r == 0 else 1.0,
                                               rstd[:, 0, :], ALU.mult, ALU.mult).then_inc(tile_out, 1)

            for n in range(41):
                if n < 40:
                    h, i = divmod(n, 5)
                    rows, w = queries(i)[1], span(i)
                    q0 = queries(i)[0]
                    sh = META + P * 3 - q0
                    dve.wait_ge(bias_ready, h + 1)
                    for c in range(2):
                        dve.wait_ge(scores_ready, 2 * n + c + 1)
                        if n >= 1:
                            dve.wait_ge(prob_ready, 2 * n + c - 1)
                        nc.vector.tensor_tensor_reduce(negs[0:rows, c, 0:w], G[c][0:rows, S0:S0 + w],
                                                       biasT[0:rows, h % 2, sh:sh + w], -1.0, 3e38,
                                                       ALU.add, ALU.min, nmax[0:rows, c, n:n + 1]).then_inc(negs_ready, 1)
                if n >= 1:
                    t = n - 1
                    h, i = divmod(t, 5)
                    rows, w = queries(i)[1], span(i)
                    dve.wait_ge(prob_ready, 2 * t + 2)
                    nc.vector.reciprocal(rden[0:rows, :, t:t + 1], den[0:rows, :, t:t + 1]).then_inc(coef_step, 1)
                    dve.wait_ge(coef_step, 2 * t + 1)
                    dve.wait_ge(lam_ready, 2)
                    nc.vector.scalar_tensor_tensor(coef[0:rows, t:t + 1], rden[0:rows, 1, t:t + 1], lamd[0:rows, 4:5],
                                                   den[0:rows, 0, t:t + 1], ALU.mult, ALU.mult).then_inc(coef_step, 1)
                    dve.wait_ge(coef_step, 2 * t + 2)
                    nc.vector.scalar_tensor_tensor(prob[0:rows, t % 2, 1, 0:w], prob[0:rows, t % 2, 1, 0:w],
                                                   coef[0:rows, t:t + 1], prob[0:rows, t % 2, 0, 0:w],
                                                   ALU.mult, ALU.add).then_inc(a_done, 1)
            dve.wait_ge(orms_ready, 1)
            nc.vector.reciprocal(orstd[:], orms[:]).then_inc(orstd_ready, 1)
            dve.wait_ge(orstd_ready, 1)
            for h in range(HEADS + 1):
                if h < HEADS:
                    if h >= 2:
                        dve.wait_ge(ot_ready, h - 1)
                    for i in range(5):
                        rows = queries(i)[1]
                        t = 5 * h + i
                        last = nc.vector.tensor_scalar(o_sc[0:rows, h % 2, i, :], o_all[0:rows, t, :],
                                                       orstd[0:rows, t:t + 1], None, ALU.mult)
                        last.then_inc(osc_ready, 1)
                if h >= 1:
                    k = h - 1
                    dve.wait_ge(x_hi, 8 + k + 1)
                    nc.vector.scalar_tensor_tensor(xl[:, k, :], G[k % 2][:, pos], gsub[:, 0:1], xh[:, k, :].bitcast(F32),
                                                   ALU.mult, ALU.subtract).then_inc(x_ready, 1)
            out_tiles(B_AO, NEED, None, 1)
            stat_recip(1, NEED)
            postnorm(1, 0, 1, NEED, 0, (2, 0, 2))
            stat_recip(2, NEED)
            dve.wait_ge(rstd_ready, 3)
            mlp(0, NEED, 2)
            stat_recip(3, NEED)
            postnorm(3, 0, 3, NEED, 8, (3, 1, 0))
            stat_recip(4, NEED)
            dve.wait_ge(rstd_ready, 5)

            _, pos = where(NEED)
            c0 = slice(*NEED)
            w = NEED[1] - NEED[0]
            for j in range(KT):
                for r in range(3):
                    b = B_CI + 3 * j + r
                    dve.wait_ge(block_done, b + 1)
                    if j >= 1 and r == 0:
                        dve.wait_ge(conv_step, 5 * j)
                    nc.vector.scalar_tensor_tensor(cb[:, r, :], G[b % 2][:, pos], 1.0, rstd[:, 0, c0], ALU.mult, ALU.mult)\
                        .then_inc(tile_out, 1)
                dve.wait_ge(tile_out, B_CI + 3 * j + 3)
                taps = [vec[:, V_CONV + CW * j + i:V_CONV + CW * j + i + 1] for i in range(CW)]
                nc.vector.tensor_tensor(cb[:, 2, :], cb[:, 2, :], cb[:, 1, :], ALU.mult).then_inc(conv_step, 1)
                dve.wait_ge(conv_step, 5 * j + 1)
                y = m[:, j, 2:2 + SEQ]
                nc.vector.tensor_scalar(y, cb[:, 2, 0:SEQ], taps[0], None, ALU.mult).then_inc(conv_step, 1)
                dve.wait_ge(conv_step, 5 * j + 2)
                for i in (1, 2):
                    nc.vector.scalar_tensor_tensor(y, cb[:, 2, i:i + SEQ], taps[i], y, ALU.mult, ALU.add)\
                        .then_inc(conv_step, 1)
                    dve.wait_ge(conv_step, 5 * j + 2 + i)
                nc.vector.tensor_tensor(y, y, cb[:, 0, 2:2 + SEQ], ALU.mult).then_inc(conv_step, 1)
                dve.wait_ge(conv_step, 5 * j + 5)
                dve.wait_ge(a_hi, 32 + j + 1)
                nc.vector.tensor_tensor(al[:, 0, j, 0:SEQ], y, ah[:, 0, j, 0:SEQ].bitcast(F32), ALU.subtract)\
                    .then_inc(a_ready, 1)
            out_tiles(B_CO, OUT, None, 5)
            stat_recip(5, OUT)
            postnorm(5, 1, 1, OUT, 16, (4, 1, 2))
            stat_recip(6, OUT)
            dve.wait_ge(rstd_ready, 7)
            mlp(1, OUT, 6)
            stat_recip(7, OUT)
            postnorm(7, 1, 3, OUT, 24, (5, 2, 0))
            stat_recip(8, OUT)

            nc.vector.memset(z[:, :, 0:1], 0.0).then_inc(S("pads_set"), 1)
            nc.vector.memset(zu[:, :, 0:PAD], 0.0).then_inc(S("pads_set"), 1)
            nc.vector.memset(t1[:, :, 0:PAD], 0.0).then_inc(S("pads_set"), 1)
            dve.wait_ge(S("pads_set"), 3)
            dve.wait_ge(rstd_ready, 9)
            for j in range(25):
                b = B_IN2 + j
                dst = z[:, j, 1:] if j < 13 else zu[:, j - 13, PAD:] if j < 17 else gate[:, j - 17]
                dve.wait_ge(block_done, b + 1)
                nc.vector.scalar_tensor_tensor(dst, G[b % 2][:, BANK:], 1.0, rstd[:, 0, META:], ALU.mult, ALU.mult)\
                    .then_inc(tile_out, 1)
                if 1 <= j <= 13:
                    i = j - 1
                    dve.wait_ge(tile_out, b)
                    if i >= 2:
                        dve.wait_ge(S("shifted"), i - 1)
                    nc.vector.tensor_tensor(t1[:, i % 2, PAD:], z[:, i, 0:SEQ], z[:, i, 1:], ALU.subtract)\
                        .then_inc(S("shift_step"), 1)
                    dve.wait_ge(S("shift_step"), i + 1)
                    nc.vector.scalar_tensor_tensor(z[:, i, 1:], t1[:, i % 2, PAD:], col(V_MU, i), z[:, i, 1:], ALU.mult,
                                                   ALU.add).then_inc(S("shifted"), 1)

            def mask(c0):
                return con[:, c0:c0 + CH].unsqueeze(1).to_broadcast([P, 4, CH])

            for p in range(PAIRS):
                zk, zr, zv = z[:, 1 + p, 1:], z[:, 5 + p, 1:], z[:, 9 + p, 1:]

                def op(done, need, instr):
                    pass
                dve.wait_ge(S("shifted"), 13)
                dve.wait_ge(S("sg_ready"), p + 1)
                nc.vector.tensor_tensor_scan(cs[:], con[:, C_RESET:C_RESET + SEQ], sg[:], 0.0, ALU.mult, ALU.add)\
                    .then_inc(S("cs_ready"), 1)
                dve.wait_ge(S("cs_ready"), p + 1)
                nc.vector.tensor_tensor(Gp[:], cs[:], sg[:], ALU.subtract).then_inc(S("cp_ready"), 1)
                dve.wait_ge(S("av_ready"), p + 1)
                dve.wait_ge(S("cp_ready"), p + 1)
                nc.vector.tensor_scalar(sg[:], av[:], 1.0, col(V_KA, p), ALU.subtract, ALU.mult).then_inc(S("ka_ready"), 1)
                dve.wait_ge(S("ka_ready"), p + 1)
                nc.vector.scalar_tensor_tensor(k2[:], sg[:], 1.0, zk, ALU.add, ALU.mult).then_inc(S("k2_ready"), 1)
                dve.wait_ge(S("kn_ready"), p + 1)
                nc.vector.tensor_scalar(kn[:], kn[:], 1e-12, None, ALU.max).then_inc(S("km_ready"), 1)
                dve.wait_ge(S("km_ready"), p + 1)
                nc.vector.reciprocal(kn[:], kn[:]).then_inc(S("kr_ready"), 1)
                dve.wait_ge(S("kr_ready"), p + 1)
                dve.wait_ge(S("Gp_ready"), p + 1)
                nc.vector.scalar_tensor_tensor(cs[:], zk, col(V_KK, p), kn[:], ALU.mult, ALU.mult).then_inc(S("kk_ready"), 1)
                dve.wait_ge(S("kk_ready"), p + 1)
                nc.vector.scalar_tensor_tensor(AR[:, :, 0, :], chunks(cs[:]), -1.0, chunks(Gp[:]), ALU.mult, ALU.mult)\
                    .then_inc(S("al_ready"), 1)
                nc.vector.tensor_tensor(AR[:, :, 1, :], chunks(zr), chunks(Gt[:]), ALU.mult).then_inc(S("R_ready"), 1)
                nc.vector.tensor_tensor(av[:], cs[:], av[:], ALU.mult).then_inc(S("bb_ready"), 1)
                dve.wait_ge(S("bb_ready"), p + 1)
                dve.wait_ge(S("k2_ready"), p + 1)
                for x in range(2):
                    r = ROW[x]
                    nc.vector.tensor_tensor(BK[r, :, x, :], chunks(av[r]), chunks(Gi[r]), ALU.mult)\
                        .then_inc(S("BK_ready"), 1)
                    nc.vector.tensor_tensor(BK[r, :, 1 - x, :], chunks(k2[r]), chunks(Gi[r]), ALU.mult)\
                        .then_inc(S("BK_ready"), 1)
                nc.vector.scalar_tensor_tensor(kn[:], zr, col(V_RK, p), k2[:], ALU.mult, ALU.mult).then_inc(S("rk_ready"), 1)

                for x in range(2):
                    r = ROW[x]
                    for g in range(2):
                        dve.wait_ge(S("gram_ready"), 4 * p + 2 * x + g + 1)
                        gram = bank(2 * x + g).rearrange("p (c t) -> p c t", t=2 * CH)
                        nc.vector.tensor_tensor(MR[x][:, HALF[g]], gram[:, :, CH:], mask(C_MR), ALU.mult)\
                            .then_inc(S("gram_out"), 1)
                        nc.vector.tensor_tensor(DL[x][:, HALF[g]], gram[:, :, 0:CH], mask(C_MDL + CH * x), ALU.mult)\
                            .then_inc(S("gram_out"), 1)
                        nc.vector.tensor_tensor(ET[r, HALF[g]], gram[r, :, 0:CH], mask(C_ME)[r], ALU.mult)\
                            .then_inc(S("gram_out"), 1)
                for g in range(2):
                    dve.wait_ge(S("lm_ready"), 2 * p + g + 1)
                    nc.vector.tensor_tensor(Dm[:, HALF[g]], chunks(bank(4 + g)[:, 0:4 * CH]), mask(C_MD), ALU.mult)\
                        .then_inc(S("D_out"), 1)
                dve.wait_ge(S("gram_out"), 12 * (p + 1))
                for x in range(2):
                    r = ROW[x]
                    eye = con[r, C_IDENT + HD * x:C_IDENT + HD * x + HD].unsqueeze(1).to_broadcast([HD, NCH, CH])
                    nc.vector.tensor_tensor(Ya[r], DL[x][r], eye, ALU.add).then_inc(S("y1_out"), 1)
                dve.wait_ge(S("y1_out"), 2 * (p + 1))
                dve.wait_ge(S("bonus_sum"), p + 1)
                nc.vector.tensor_tensor(k2[:], bank(7), zv, ALU.mult).then_inc(S("bonus_ready"), 1)

                def add_out(need, banks, dst, base, done, view=None):
                    for g in range(2):
                        dve.wait_ge(S(need), 2 * p + g + 1)
                        nc.vector.tensor_tensor(dst(g), chunks(bank(banks + g)[:, 0:4 * CH]), base[:, HALF[g]], ALU.add)\
                            .then_inc(S(done), 1)
                    dve.wait_ge(S(done), 2 * p + 2)
                add_out("y2_ready", 4, lambda g: Yb[:, HALF[g]], Ya, "y2_out")
                add_out("y3_ready", 6, lambda g: Ya[:, HALF[g]], Yb, "y3_out")
                add_out("y4_ready", 4, lambda g: Yb[:, HALF[g]], Ya, "y4_out")
                add_out("z1_ready", 6, lambda g: Ya[:, HALF[g]], Yb, "z1_out")
                add_out("z2_ready", 4, lambda g: PB4[:, g, 0], Yb, "z2_out")
                add_out("z3_ready", 6, lambda g: Ya[:, HALF[g]], Yb, "z3_out")

                dve.wait_ge(S("q_out"), p + 1)
                for c in range(NCH):
                    if c == 0:
                        for x in range(2):
                            nc.vector.tensor_copy(UV[x][ROW[x], 0, :], Yb[ROW[x], 0, :]).then_inc(S("u_out"), 1)
                    else:
                        if c < NCH - 1:
                            nc.vector.tensor_scalar(Sg[:], Sm[:, c, :], Gt[:, CH * c + CH - 1:CH * c + CH], None, ALU.mult)\
                                .then_inc(S("sg_out"), 1)
                        dve.wait_ge(S("u_ready"), (NCH - 1) * p + c)
                        for x in range(2):
                            nc.vector.tensor_tensor(UV[x][ROW[x], c, :], bank(6)[ROW[x], 0:CH], Yb[ROW[x], c, :], ALU.add)\
                                .then_inc(S("u_out"), 1)
                    if c < NCH - 1:
                        dve.wait_ge(S("s_ready"), (NCH - 1) * p + c + 1)
                        end = Gt[:, CH * c + CH - 1:CH * c + CH]
                        if c == 0:
                            nc.vector.tensor_scalar(Sm[:, 1, :], bank(7)[:, 0:CH], end, None, ALU.mult)\
                                .then_inc(S("s_out"), 1)
                        else:
                            dve.wait_ge(S("sg_out"), (NCH - 2) * p + c)
                            nc.vector.scalar_tensor_tensor(Sm[:, c + 1, :], bank(7)[:, 0:CH], end, Sg[:], ALU.mult, ALU.add)\
                                .then_inc(S("s_out"), 1)
                        dve.wait_ge(S("s_out"), (NCH - 1) * p + c + 1)

                dve.wait_ge(S("yt_out"), p + 1)
                dve.wait_ge(S("mu_ready"), p + 1)
                nc.vector.scalar_tensor_tensor(av[:], bank(1), -1.0 / HD, sg[:], ALU.mult, ALU.add).then_inc(S("yc_ready"), 1)
                dve.wait_ge(S("sd_ready"), p + 1)
                nc.vector.reciprocal(kn[:], kn[:]).then_inc(S("rs_ready"), 1)
                dve.wait_ge(S("rs_ready"), p + 1)
                nc.vector.scalar_tensor_tensor(av[:], av[:], col(V_GG, p), kn[:], ALU.mult, ALU.mult)\
                    .then_inc(S("yn_ready"), 1)
                dve.wait_ge(S("yn_ready"), p + 1)
                nc.vector.scalar_tensor_tensor(av[:], av[:], col(V_GB, p), k2[:], ALU.add, ALU.add).then_inc(S("yw_ready"), 1)
                dve.wait_ge(S("yw_ready"), p + 1)
                dve.wait_ge(S("gate_ready"), 5 + p)
                nc.vector.tensor_tensor(zr, av[:], gate[:, 4 + p], ALU.mult).then_inc(S("yb_ready"), 1)

            for g, w in enumerate(POOL_W):
                src = zu[:, g]
                n0 = sum(range(1, g + 1))
                if g:
                    dve.wait_ge(S("pooled"), g)
                for i in range(g + 1):
                    dst = t1[:, i % 2]
                    sh = 1 << i
                    if i:
                        dve.wait_ge(S("pool_step"), n0 + i + g)
                    nc.vector.tensor_tensor(dst[:, PAD:], src[:, PAD:], src[:, PAD - sh:PAD + SEQ - sh], ALU.add)\
                        .then_inc(S("pool_step"), 1)
                    src = dst
                dve.wait_ge(S("pool_step"), n0 + g + 1 + g)
                fix = con[:, C_PFIX + 16 * g:C_PFIX + 16 * g + 16]
                nc.vector.tensor_tensor(src[:, PAD:PAD + 16], src[:, PAD:PAD + 16], fix, ALU.mult).then_inc(S("pool_step"), 1)
                dve.wait_ge(S("pool_step"), n0 + g + 2 + g)
                if g >= 2:
                    dve.wait_ge(S("mix_ready"), g - 1)
                nc.vector.scalar_tensor_tensor((Gt, Gi)[g % 2][:], src[:, PAD:], 1.0 / w, zu[:, g, PAD:], ALU.mult,
                                               ALU.subtract).then_inc(S("pooled"), 1)
            for g in range(4):
                dve.wait_ge(S("mix_ready"), g + 1)
                dve.wait_ge(S("gate_ready"), g + 1)
                nc.vector.scalar_tensor_tensor(zu[:, g, PAD:], bank(3 + g), col(V_POOL, g), gate[:, g], ALU.mult, ALU.mult)\
                    .then_inc(S("ya_ready"), 1)

            for k in range(KT):
                src = zu[:, k, PAD:] if k < 4 else z[:, 1 + k, 1:]
                dve.wait_ge(x_hi, 48 + k + 1)
                nc.vector.tensor_tensor(x2l[:, k, META:], src, x2h[:, k, META:].bitcast(F32), ALU.subtract)\
                    .then_inc(x_ready, 1)
            for j in range(KT + 1):
                if j < KT:
                    b = B_O2 + j
                    dve.wait_ge(block_done, b + 1)
                    nc.vector.tensor_tensor(hres[:, j, META:], G[b % 2][:, BANK:], hres[:, j, META:], ALU.add)\
                        .then_inc(tile_out, 1)
                if j >= 1:
                    n = 32 + j - 1
                    dve.wait_ge(psq_ready, n + 1)
                    part = sq[:, (B_O2 + j - 1) % 2, 0:SEQ]
                    if j == 1:
                        nc.vector.tensor_copy(acc[:, 0:SEQ], part).then_inc(psq_added, 1)
                    else:
                        dve.wait_ge(psq_added, n)
                        nc.vector.tensor_tensor(acc[:, 0:SEQ], acc[:, 0:SEQ], part, ALU.add).then_inc(psq_added, 1)
            stat_recip(9, OUT)
            dve.wait_ge(rstd_ready, 10)
            for k in range(KT):
                nc.vector.scalar_tensor_tensor(hres[:, k, META:], hres[:, k, META:], col(V_FG, k), rstd[:, 1, META:], ALU.mult,
                                               ALU.mult).then_inc(S("out_ready"), 1)

        @block.tensor
        def _(pe):
            def stat(s, cols, off):
                pieces, _ = where(cols)
                if s >= 1:
                    pe.wait_ge(rms_ready, s)
                if s % 2:
                    pe.wait_ge(psq_added, 4 * (s + 1))
                    for t0, t1_, p0, p1 in pieces:
                        last = nc.tensor.matmul(ST[:, p0:p1], ones, acc[:, t0 - off:t1_ - off], start=True, stop=True)
                    last.then_inc(post_sum, 1)
                    return
                for k in range(KT):
                    n = 4 * s + k
                    pe.wait_ge(sq_ready, n + 1)
                    for t0, t1_, p0, p1 in pieces:
                        last = nc.tensor.matmul(ST[:, p0:p1], ones, sq[:, n % 2, t0 - off:t1_ - off], start=k == 0,
                                                stop=k == KT - 1)
                    last.then_inc(sq_used, 1)

            def product(b0, n, ready, first, hi, lo, cols, off):
                pieces, _ = where(cols)

                def body(b, j, s):
                    pe.wait_ge(lo_ready, b + 1)
                    if not isinstance(b, int) or b >= 2:
                        pe.wait_ge(tile_out, b - 1)
                    for k in range(KT):
                        if s == b0 % 4:
                            pe.wait_ge(ready, first + k + 1)
                        ws = slice(k * P, k * P + P)
                        for q, (wt, xt) in enumerate(((whi, hi), (whi, lo), (wlo, hi))):
                            for t0, t1_, p0, p1 in pieces:
                                last = nc.tensor.matmul(G[s % 2][:, p0:p1], wt[:, s % 2, ws], xt[:, k, t0 - off:t1_ - off],
                                                        start=k == 0 and q == 0, stop=k == KT - 1 and q == 2)
                    last.then_inc(block_done, 1)
                blocks(pe, b0, n, body)

            stat(0, ALL, 0)
            product(B_QKV, 24, x_ready, 0, xh, xl, ALL, 0)

            for n in range(42):
                if n < 40:
                    h, i = divmod(n, 5)
                    q0, rows = queries(i)
                    for c in range(2):
                        if n == 0:
                            pe.wait_ge(tile_out, 24)
                        else:
                            pe.wait_ge(negs_ready, 2 * n + c - 1)
                        f = slice(64 * c, 64 * c + 64)
                        last = nc.tensor.matmul(G[c][0:rows, S0:S0 + META], qT[f, h, q0:q0 + rows], kT[f, h, 0:META],
                                                start=True, stop=True)
                        if i > 0:
                            last = nc.tensor.matmul(G[c][0:rows, BANK:BANK + P * i], qT[f, h, q0:q0 + rows],
                                                    kT[f, h, META:META + P * i], start=True, stop=True)
                        last.then_inc(scores_ready, 1)
                if 1 <= n <= 40:
                    t = n - 1
                    i = t % 5
                    rows = queries(i)[1]
                    pe.wait_ge(a_done, t + 1)
                    if t >= 1:
                        pe.wait_ge(at_copied, t)
                    else:
                        pe.wait_ge(rms_ready, 1)
                    for j in range(1, i + 1):
                        nc.tensor.transpose(ST[:, P * (j - 1):P * j], prob[:, t % 2, 1, META + P * (j - 1):META + P * j], ident)
                    nc.tensor.transpose(ST[0:META, BANK:BANK + rows], prob[0:rows, t % 2, 1, 0:META], ident[0:rows, 0:rows])\
                        .then_inc(at_ready, 1)
                if n < 40 and n % 5 == 0:
                    h = n // 5
                    if n >= 3:
                        pe.wait_ge(o_copied, n - 2)
                    if h >= 1:
                        pe.wait_ge(v_copied, 2 * h)
                    for j in range(4):
                        nc.tensor.transpose(PV[:, P * j:P * j + P], vT[:, h, META + P * j:META + P * j + P], ident)
                    nc.tensor.transpose(PO[0:META, P:2 * P], vT[:, h, 0:META], ident).then_inc(v_turned, 1)
                if n >= 2:
                    t = n - 2
                    h, i = divmod(t, 5)
                    rows = queries(i)[1]
                    pe.wait_ge(at_copied, t + 1)
                    if t >= 1:
                        pe.wait_ge(o_copied, t)
                    pe.wait_ge(v_copied, 2 * (min(n, 39) // 5 + 1))
                    for j, (_, nk) in enumerate(keys(i)):
                        last = nc.tensor.matmul(PO[0:rows, 0:P], aT[0:nk, t % 2, j, 0:rows], vtok[0:nk, h % 2, j, :],
                                                start=j == 0, stop=j == i)
                    last.then_inc(o_ready, 1)
            for h in range(HEADS):
                pe.wait_ge(osc_ready, 5 * (h + 1))
                if h >= 2:
                    pe.wait_ge(x_ready, 8 + h - 1)
                else:
                    pe.wait_ge(negs_ready, 80)
                for i in range(5):
                    q0, rows = queries(i)
                    p0 = q0 + BANK - SPLIT
                    last = nc.tensor.transpose(G[h % 2][:, p0:p0 + rows], o_sc[0:rows, h % 2, i, :], ident[0:rows, 0:rows])
                last.then_inc(ot_ready, 1)

            pe.wait_ge(x_ready, 16)
            product(B_AO, 8, x_ready, 8, xh, xl, NEED, 0)
            stat(1, NEED, NEED[0])
            stat(2, NEED, 0)

            def mlp(layer, cols, xfill, s):
                b0 = B_MLP[layer]
                for c in range(FF_CHUNKS + 1):
                    f = 5 * layer + c
                    if c < FF_CHUNKS:
                        product(b0 + UP[c], 8, x_ready, 8 * xfill, xh, xl, cols, 0)
                    if c >= 1:
                        product(b0 + DOWN[c - 1], 8, a_ready, 8 * (f - 1), ah[:, (f - 1) % 2], al[:, (f - 1) % 2], cols,
                                cols[0])
                stat(s, cols, cols[0])

            mlp(0, NEED, 2, 3)
            stat(4, NEED, 0)
            product(B_CI, 24, x_ready, 24, xh, xl, NEED, 0)
            product(B_CO, 8, a_ready, 32, ah[:, 0], al[:, 0], OUT, OUT[0])
            stat(5, OUT, OUT[0])
            stat(6, OUT, 0)
            mlp(1, OUT, 4, 7)
            stat(8, OUT, 0)
            product(B_IN2, 25, x_ready, 40, x2h, x2l, OUT, 0)

            blk = con[:, C_BLK:C_BLK + P]

            def mm(out_, lhsT, rhs, start=True, stop=True):
                return nc.tensor.matmul(out_, lhsT, rhs, start=start, stop=stop)

            def both(out_, lhsT, rhs, g):
                for x in range(2):
                    for c in range(4 * g, 4 * g + 4):
                        last = mm(out_(x, c), lhsT(x, c), rhs(x, c))
                return last

            for p in range(PAIRS):
                zv = z[:, 9 + p, 1:]
                ps = slice(P * p, P * p + P)
                if p == 0:
                    pe.wait_ge(S("tanh_ready"), 1)
                    pe.wait_ge(rms_ready, 9)
                mm(bank(4), mat[0:HD, ps], tw[:]).then_inc(S("ww_ready"), 1)
                mm(bank(5), mat[HD:P, ps], z[HD:P, 0, 1:]).then_inc(S("aa_ready"), 1)
                pe.wait_ge(S("ksq_ready"), p + 1)
                mm(bank(6), blk, kn[:]).then_inc(S("knorm_sum"), 1)
                pe.wait_ge(S("rk_ready"), p + 1)
                mm(bank(7), blk, kn[:]).then_inc(S("bonus_sum"), 1)

                alpha = lambda x, c: AR[ROW[x], c, 0, :]
                eye = lambda x, c: con[ROW[x], C_IDENT + HD * x:C_IDENT + HD * x + HD]
                at4 = lambda b: (lambda x, c: bank(b + c // 4)[ROW[x], CH * (c % 4):CH * (c % 4) + CH])
                whole_ = lambda t: (lambda x, c: t[ROW[x], c, :])
                pair = lambda t, kind: (lambda x, c: t[ROW[x], c // 4, kind, c % 4, :])
                DT = lambda x, c: DL[x][ROW[x], c, :]
                LakT = lambda x, c: DL[x][ROW[1 - x], c, :]

                pe.wait_ge(S("BK_ready"), 4 * (p + 1))
                if p == 0:
                    pe.wait_ge(tile_out, B_IN2 + 25)
                else:
                    pe.wait_ge(S("yb_ready"), p)
                for x in range(2):
                    for g in range(2):
                        for c in range(4 * g, 4 * g + 4):
                            last = mm(bank(2 * x + g)[:, 2 * CH * (c % 4):2 * CH * (c % 4 + 1)],
                                      BK[ROW[x], c].rearrange("p k t -> p (k t)"),
                                      AR[ROW[x], c].rearrange("p k t -> p (k t)"))
                        last.then_inc(S("gram_ready"), 1)
                for g in range(2):
                    both(at4(4), alpha, lambda x, c: BK[ROW[x], c, x, :], g).then_inc(S("lm_ready"), 1)
                pe.wait_ge(S("bonus_ready"), p + 1)
                for g in range(2):
                    last = both(lambda x, c: bank(6)[ROW[1 - x], CH * c:CH * c + CH],
                                lambda x, c: zv[ROW[x], CH * c:CH * c + CH], eye, g)
                last.then_inc(S("rv_turned"), 1)
                for g in range(2):
                    last = both(lambda x, c: bank(7)[ROW[x], CH * c:CH * c + CH], alpha, eye, g)
                last.then_inc(S("at_turned"), 1)
                pe.wait_ge(S("gram_out"), 12 * (p + 1))
                for g in range(2):
                    pe.wait_ge(S("D_out"), 2 * p + g + 1)
                    both(lambda x, c: bank(g)[ROW[x], CH * (c % 4):CH * (c % 4) + CH], DT, whole_(Dm), g)
                    both(lambda x, c: bank(g)[ROW[x], CH * (4 + c % 4):CH * (5 + c % 4)], whole_(Dm), DT, g)\
                        .then_inc(S("d2_ready"), 1)
                pe.wait_ge(S("vt_out"), 2 * (p + 1))
                pe.wait_ge(S("at_out"), p + 1)
                for x in range(2):
                    for c in range(NCH):
                        last = nc.tensor.transpose(bank(6 + x)[:, CH * c:CH * c + CH],
                                                   BK[ROW[x], c].rearrange("p k t -> p (k t)"), eye(x, c))
                    last.then_inc(S("bk_turned"), 1)
                for g in range(2):
                    last = both(lambda x, c: bank(2)[ROW[x], CH * c:CH * c + CH], LakT,
                                lambda x, c: UV[x][ROW[1 - x], c, :], g)
                last.then_inc(S("w_ready"), 1)
                for g in range(2):
                    pe.wait_ge(S("d2_out"), 2 * p + g + 1)
                    both(lambda x, c: bank(g)[ROW[x], CH * (c % 4):CH * (c % 4) + CH], pair(PB2, 1), pair(PB2, 0), g)
                    both(lambda x, c: bank(g)[ROW[x], CH * (4 + c % 4):CH * (5 + c % 4)], pair(PB2, 0), pair(PB2, 1), g)\
                        .then_inc(S("d4_ready"), 1)
                pe.wait_ge(S("y1_out"), 2 * (p + 1))
                for g in range(2):
                    both(at4(4), pair(PB2, 0), whole_(Ya), g).then_inc(S("y2_ready"), 1)
                pe.wait_ge(S("w_out"), p + 1)
                pe.wait_ge(S("bk_out"), 2 * (p + 1))
                for g in range(2):
                    pe.wait_ge(S("d4_out"), 2 * p + g + 1)
                    both(at4(2), pair(PB4, 1), pair(PB4, 0), g).then_inc(S("d8_ready"), 1)
                for g in range(2):
                    pe.wait_ge(S("y2_out"), 2 * p + g + 1)
                    both(at4(6), pair(PB4, 0), whole_(Yb), g).then_inc(S("y3_ready"), 1)
                for g in range(2):
                    pe.wait_ge(S("y3_out"), 2 * p + g + 1)
                    pe.wait_ge(S("d8_out"), 2 * p + g + 1)
                    both(at4(4), whole_(Dm), whole_(Ya), g).then_inc(S("y4_ready"), 1)
                for g in range(2):
                    pe.wait_ge(S("y4_out"), 2 * p + g + 1)
                    both(at4(0), whole_(Yb), eye, g).then_inc(S("td_ready"), 1)
                for g in range(2):
                    pe.wait_ge(S("td_out"), 2 * p + g + 1)
                    both(at4(2), whole_(ET), pair(PB2, 0), g).then_inc(S("ht_ready"), 1)
                for name, need, b, src in (("z1_ready", "ht_out", 6, whole_(Yb)), ("z2_ready", "z1_out", 4, whole_(Ya)),
                                           ("z3_ready", "z2_out", 6, pair(PB4, 0))):
                    for g in range(2):
                        pe.wait_ge(S(need), 2 * p + g + 1)
                        both(at4(b), pair(PB2, 1), src, g).then_inc(S(name), 1)
                pe.wait_ge(S("z3_out"), 2 * p + 2)
                for g in range(2):
                    last = both(lambda x, c: bank(4)[ROW[x], CH * c:CH * c + CH], whole_(Ya), whole_(Wm), g)
                last.then_inc(S("q_ready"), 1)
                for g in range(2):
                    last = both(lambda x, c: bank(5)[ROW[x], CH * c:CH * c + CH], whole_(at_), whole_(Ya), g)
                last.then_inc(S("pt_ready"), 1)

                pe.wait_ge(S("pt_out"), p + 1)
                for c in range(NCH):
                    n = (NCH - 1) * p + c
                    if c >= 1:
                        pe.wait_ge(S("s_out"), n)
                        for x in range(2):
                            last = mm(bank(6)[ROW[x], 0:CH], PT[ROW[x], c, :], Sm[ROW[x], c, :])
                        last.then_inc(S("u_ready"), 1)
                    if c < NCH - 1:
                        pe.wait_ge(S("u_out"), 2 * (NCH * p + c + 1))
                        for x in range(2):
                            last = mm(bank(7)[ROW[x], 0:CH], BKt[x][:, c, :], UV[x][:, c, :])
                        last.then_inc(S("s_ready"), 1)
                pe.wait_ge(S("u_out"), 2 * NCH * (p + 1))
                for x in range(2):
                    for c in range(NCH):
                        o = bank(0)[ROW[x], CH * c:CH * c + CH]
                        last = mm(o, UV[x][:, c, :], MR[x][:, c, :], stop=c == 0)
                        if c >= 1:
                            last = mm(o, Sm[ROW[x], c, :], AR[ROW[x], c, 1, :], start=False)
                last.then_inc(S("y_ready"), 1)
                pe.wait_ge(S("yt_out"), p + 1)
                mm(bank(1), blk, sg[:]).then_inc(S("mu_ready"), 1)
                pe.wait_ge(S("ysq_ready"), p + 1)
                mm(bank(2), blk, kn[:]).then_inc(S("var_ready"), 1)

            for g in range(4):
                pe.wait_ge(S("pooled"), g + 1)
                if g == 0:
                    pe.wait_ge(S("yb_ready"), PAIRS)
                mm(bank(3 + g), mat[:, SEQ + P * g:SEQ + P * g + P], (Gt, Gi)[g % 2][:]).then_inc(S("mix_ready"), 1)

            pe.wait_ge(S("ya_ready"), 4)
            product(B_O2, 8, x_ready, 48, x2h, x2l, OUT, 0)
            stat(9, OUT, OUT[0])


def layout(v):
    return v.reshape(-1, P).T


def weight_blocks(w):
    n = w.shape[1] // P
    return w.reshape(KT, P, n, P).transpose(2, 1, 0, 3).reshape(n, P, KT * P)


def kernel(**inputs):
    import concourse.bacc as bacc
    from concourse.bass_utils import run_bass_kernel_spmd as run

    a = {k: np.asarray(v) for k, v in inputs.items()}
    xT = np.ascontiguousarray(np.concatenate([a["meta_tokens"], a["x"][0]], axis=0).T)
    lam = np.broadcast_to(a["lambda_params"].reshape(1, 256), (P, 256))
    conv = a["conv_w"][0].reshape(CW, KT, P).transpose(2, 1, 0).reshape(P, KT * CW)
    mu = layout(a["shift_mu_2"])[:, [12, *range(4, 8), *range(0, 4), *range(8, 12)]]
    second = [layout(a[n]) for n in ("w0_2", "a0_2", "k_k_2", "k_a_2", "r_k_2", "gn_gain_2", "gn_bias_2", "final_gain_2")]
    vecs = np.ascontiguousarray(np.concatenate([layout(a["norm_g"]), layout(a["subln_g"]), conv, lam,
                                                layout(a["norm_gain_2"]), layout(a["pool_scale_2"]), mu, *second], axis=1))
    mats = np.concatenate([np.concatenate([a["w_up_2"][0], a["a_up_2"][0]], axis=0),
                           a["pool_w_2"][0].transpose(1, 0, 2).reshape(P, SEQ)], axis=1)

    q = np.arange(P)[:, None]
    dist = np.arange(TOK)[None, :] - META - 3 * P - q
    dist = np.where(dist > 0, MASKED, dist)
    heads = np.kron(np.eye(2), np.ones((HD, HD)))
    i, j = np.arange(CH)[:, None], np.arange(CH)[None, :]
    near = i // SUB == j // SUB
    twice = lambda m: np.concatenate([m, m], axis=0)
    diag, strict = near & (i < j), i < j
    mdl = np.concatenate([np.concatenate([diag, strict]), np.concatenate([strict, diag])], axis=1)
    reset = np.broadcast_to(np.arange(SEQ) % CH != 0, (P, SEQ))
    pos = np.arange(16)
    fix = np.concatenate([w / np.minimum(pos + 1, w) for w in POOL_W])
    consts = np.concatenate([np.eye(P), np.ones((P, P)), dist, heads, mdl, twice(i <= j), twice(strict & ~near),
                             twice(near & (j < i)), reset, np.broadcast_to(fix, (P, 64))], axis=1).astype(np.float32)

    def interleave(w, n):
        b = weight_blocks(w)
        return b.reshape(n, KT, P, D).transpose(1, 0, 2, 3).reshape(n * KT, P, D)

    def mlp_blocks(up, down):
        u = weight_blocks(up).reshape(FF_CHUNKS, KT, P, D)
        d = [weight_blocks(down[c * D:(c + 1) * D]) for c in range(FF_CHUNKS)]
        return [u[0], u[1], d[0], u[2], d[1], u[3], d[2], d[3]]

    w = [interleave(a["w_in"][0], 3), weight_blocks(a["w_out"][0])]
    w += mlp_blocks(a["w_up"][0], a["w_down"][0])
    w += [interleave(a["w_in"][1], 3), weight_blocks(a["w_out"][1])]
    w += mlp_blocks(a["w_up"][1], a["w_down"][1])
    w2 = weight_blocks(a["w_in_2"][0])
    w += [w2[[20, *range(12, 16), *range(8, 12), *range(16, 20), *range(0, 8), *range(21, 25)]]]
    w += [weight_blocks(a["w_out_2"][0])]
    weights = np.concatenate(w, axis=0)

    nc = bacc.Bacc("TRN2", target_bir_lowering=False, num_devices=1)
    arrays, args = {}, []
    for name, v in (("xT", xT), ("vecs", vecs), ("consts", consts), ("mats", mats), ("weights", weights)):
        arrays[name + "_dram"] = v
        args.append(nc.dram_tensor(name + "_dram", v.shape, F32, kind="ExternalInput").ap())
    args.append(nc.dram_tensor("out_dram", (D, SEQ), F32, kind="ExternalOutput").ap())
    program(nc, *args)
    r = run(nc, [arrays], core_ids=[0])
    return np.ascontiguousarray(r.results[0]["out_dram"].T)[None]
```

```python
from contextlib import ExitStack
import math

import numpy as np
import concourse.bass as bass
from concourse import mybir

F32 = mybir.dt.float32
F32R = mybir.dt.float32r
ACT = mybir.ActivationFunctionType
ALU = mybir.AluOpType

P = 128
D = 1024
KT = D // P
META, SEQ = 16, 512
TOK = META + SEQ
HEADS = 8
CW = 3
FF_CHUNKS = 4
EPS = 1e-6
LAM_INIT = 0.8 - 0.6 * math.exp(-0.3 * 0)
MASKED = -1e32

ALL = (0, TOK)
NEED = (META - (CW - 1), TOK)
OUT = (META, TOK)
SPLIT = META + SEQ // 2
BANK = 512

V_NORM, V_SUBLN, V_CONV, V_LAM = 0, 64, 65, 89
V_N2 = V_LAM + 256
V_POOL, V_MU = V_N2 + 8, V_N2 + 12
V_W0 = V_MU + 13
V_A0, V_KK, V_KA, V_RK, V_GG, V_GB, V_FG = (V_W0 + 4 * i for i in range(1, 8))
V_END = V_FG + 8
C_IDENT, C_ONES, C_DIST = 0, P, 2 * P
C_BLK = C_DIST + TOK
C_MDL, C_MR, C_ME, C_MD = C_BLK + P, C_BLK + 2 * P, C_BLK + 2 * P + 64, C_BLK + 3 * P
C_RESET = C_MD + 64
C_PFIX = C_RESET + SEQ
C_END = C_PFIX + 4 * 16

HD = 64
CH = 64
SUB = 16
NCH = SEQ // CH
PAIRS = 4
NORM_EPS = 1e-6
GN_EPS = 64e-5
DECAY = math.exp(-0.5)
POOL_W = (2, 4, 8, 16)
PAD = 16


def where(cols):
    a, b = cols
    if b - a <= BANK:
        return [(a, b, BANK, BANK + b - a)], slice(BANK, BANK + b - a)
    off = BANK - SPLIT
    return [(a, SPLIT, a + off, BANK), (SPLIT, b, BANK, b + off)], slice(a + off, b + off)


def program(nc, xT, vecs, consts, mats, weights, out):
    NBLK = weights.shape[0]
    with ExitStack() as whole:
        def sb(name, shape, dt=F32, ctx=whole):
            return ctx.enter_context(nc.sbuf_tensor(name, shape, dt))

        def sem(name):
            return whole.enter_context(nc.semaphore(name))

        hres = sb("hres", [P, KT, TOK])
        vec = sb("vec", [P, V_END])
        con = sb("con", [P, C_END])
        raw = sb("raw", [P, 4, D])
        whi = sb("whi", [P, 2, D], F32R)
        wlo = sb("wlo", [P, 2, D], F32R)
        sq = sb("sq", [P, 2, TOK])
        acc = sb("acc", [P, TOK])
        rms = sb("rms", [P, TOK])
        rstd = sb("rstd", [P, 2, TOK])
        t1 = sb("t1", [P, 2, TOK])
        eps_t = sb("eps_t", [P, 2])
        mat = sb("mat", [P, 2 * SEQ])
        first = ExitStack()
        xh = sb("xh", [P, KT, TOK], F32R, first)
        xl = sb("xl", [P, KT, TOK], F32R, first)
        NW = NEED[1] - NEED[0]
        ah = [sb("ah0", [P, KT, NW], F32R, first)]
        al = [sb("al0", [P, KT, NW], F32R, first)]
        with ExitStack() as attn:
            qT, kT, vT = (sb(n, [P, 2, TOK], F32, attn) for n in ("qT", "kT", "vT"))
            o_all = sb("o_all", [P, 2, 5, P], F32, attn)
            biasT = sb("biasT", [P, 2, TOK], F32, attn)
            negs = sb("negs", [P, 2, 2, TOK], F32, attn)
            prob = sb("prob", [P, 2, 2, TOK], F32, attn)
            aT = sb("aT", [P, 2, 5, P], F32, attn)
            vtok = sb("vtok", [P, 2, 5, P], F32, attn)
            o_sc = sb("o_sc", [P, 2, 5, P], F32, attn)
            o_sq = sb("o_sq", [P, P], F32, attn)
            nmax = sb("nmax", [P, 2, 40], F32, attn)
            den = sb("den", [P, 2, 40], F32, attn)
            rden = sb("rden", [P, 2, 40], F32, attn)
            coef = sb("coef", [P, 40], F32, attn)
            oss = sb("oss", [P, 40], F32, attn)
            orms = sb("orms", [P, 40], F32, attn)
            orstd = sb("orstd", [P, 40], F32, attn)
            lamt = sb("lamt", [P, 2, 64], F32, attn)
            lamd = sb("lamd", [P, 8], F32, attn)
            gsub = sb("gsub", [P, 1], F32, attn)
        with ExitStack() as mlp:
            ah.append(sb("ah1", [P, KT, NW], F32R, mlp))
            al.append(sb("al1", [P, KT, NW], F32R, mlp))
            m = sb("m", [P, KT, NW], F32, mlp)
            act2 = sb("act2", [P, 2, NW], F32, mlp)
            cb = sb("cb", [P, 3, NW], F32, mlp)
        first.close()
        with ExitStack() as tri:
            def mats_of(name, *shape):
                return sb(name, [P, *(shape or (NCH, CH))], F32, tri)

            def chain_mats(i):
                return [[mats_of(f"{n}{i}{x}") for x in range(2)] for n in ("MR", "BKt", "UV")]
            DL = [mats_of(f"DL{x}") for x in range(2)]
            ET, Dm, Ya, Yb = (mats_of(n) for n in ("ET", "Dm", "Ya", "Yb"))
            PB2, PB4 = mats_of("PB2", 2, 2, 4, CH), mats_of("PB4", 2, 2, 4, CH)
            Sg = mats_of("Sg", CH)
            first_mats = chain_mats(0)
            sb("tri_pad", [P, 2 * KT * TOK - 16 * SEQ - CH], F32, tri)
            MR, BKt, UV = zip(first_mats, chain_mats(1))
        second = ExitStack()
        x2h = sb("x2h", [P, KT, TOK], F32R, second)
        x2l = sb("x2l", [P, KT, TOK], F32R, second)
        sg, av, cs, Gp, Gt, Gi, kn, k2 = (sb(n, [P, SEQ], F32, second)
                                          for n in ("sg", "av", "cs", "Gp", "Gt", "Gi", "kn", "k2"))
        tw = sb("tw", [HD, SEQ], F32, second)
        z = sb("z", [P, 13, 1 + SEQ], F32, second)
        zu = sb("zu", [P, 4, PAD + SEQ], F32, second)
        gate = sb("gate", [P, 8, SEQ], F32, second)
        BK = sb("BK", [P, PAIRS, NCH, 2, CH], F32, second)
        bonus = sb("bonus", [P, PAIRS, SEQ], F32, second)
        g_end = sb("g_end", [P, PAIRS, NCH], F32, second)
        second.close()
        Wm, at_ = (sq[:, i, 0:SEQ].rearrange("p (c t) -> p c t", t=CH) for i in range(2))
        gn_y, gn_sd, gn_c = acc[:, 0:SEQ], rms[:, 0:SEQ], rstd[:, 0, 0:SEQ]

        G = [whole.enter_context(nc.psum_tensor(f"G{i}", [P, 2 * BANK], F32)) for i in range(2)]
        ST = whole.enter_context(nc.psum_tensor("ST", [P, 2 * BANK], F32))
        PO = whole.enter_context(nc.psum_tensor("PO", [P, BANK], F32))
        PV = whole.enter_context(nc.psum_tensor("PV", [P, BANK], F32))

        inputs_loaded = sem("inputs_loaded")
        w_loaded = [sem(f"w_loaded{i}") for i in range(4)]
        hi_ready = sem("hi_ready"); lo_ready = sem("lo_ready")
        block_done = sem("block_done"); tile_out = sem("tile_out")
        x_hi = sem("x_hi"); x_ready = sem("x_ready")
        a_hi = sem("a_hi"); a_ready = sem("a_ready")
        sq_ready = sem("sq_ready"); sq_used = sem("sq_used")
        psq_ready = sem("psq_ready"); psq_added = sem("psq_added"); post_sum = sem("post_sum")
        rms_ready = sem("rms_ready"); rstd_ready = sem("rstd_ready")
        t1_ready = sem("t1_ready"); h_ready = sem("h_ready")
        sqr_ready = sem("sqr_ready")
        lam_prod = sem("lam_prod"); lam_exp = sem("lam_exp"); lam_ready = sem("lam_ready")
        oss_set = sem("oss_set")
        bias_ready = sem("bias_ready")
        scores_ready = sem("scores_ready"); negs_ready = sem("negs_ready"); prob_ready = sem("prob_ready")
        coef_step = sem("coef_step"); a_done = sem("a_done")
        at_ready = sem("at_ready"); at_copied = sem("at_copied")
        v_turned = sem("v_turned"); v_copied = sem("v_copied")
        o_ready = sem("o_ready"); o_copied = sem("o_copied"); oss_ready = sem("oss_ready")
        orms_ready = sem("orms_ready"); orstd_ready = sem("orstd_ready")
        osc_ready = sem("osc_ready"); ot_ready = sem("ot_ready")
        conv_step = sem("conv_step")
        stored = sem("stored")
        sems = {}

        def S(name):
            if name not in sems:
                sems[name] = sem(name)
            return sems[name]

        def bank(n):
            return (G[0][:, 0:BANK], G[0][:, BANK:], G[1][:, 0:BANK], G[1][:, BANK:], ST[:, 0:BANK], ST[:, BANK:],
                    PO[:], PV[:])[n]

        def chunks(ap):
            return ap.rearrange("p (c t) -> p c t", t=CH)

        def col(v, p):
            return vec[:, v + p:v + p + 1]

        HALF = [slice(0, 4), slice(4, 8)]
        ROW = [slice(0, HD), slice(HD, P)]
        B_IN2, B_O2 = 192, 217

        ident = con[:, C_IDENT:C_IDENT + P]
        ones = con[:, C_ONES:C_ONES + P]

        def gain(layer, n, k):
            if layer == 2:
                return col(V_N2, k)
            c = V_NORM + (layer * 4 + n) * KT + k
            return vec[:, c:c + 1]

        B_QKV, B_AO = 0, 24
        B_MLP = [32, 128]
        B_CI, B_CO = 96, 120
        UP = [0, 8, 24, 40]
        DOWN = [16, 32, 48, 56]

        def blocks(eng, b0, n, body):
            lead = 4 if b0 == 0 else 0
            for j in range(lead):
                body(b0 + j, j, (b0 + j) % 4)
            if n - lead >= 8:
                with eng.Fori(0, (n - lead) // 4) as i:
                    for u in range(4):
                        body(i * 4 + (b0 + lead + u), i * 4 + (lead + u), (b0 + u) % 4)
                lead += (n - lead) // 4 * 4
            for j in range(lead, n):
                body(b0 + j, j, (b0 + j) % 4)

        def tile(buf, j, cols):
            if isinstance(j, int):
                return buf[:, j, cols]
            return buf[:, bass.ds(j, 1), cols]

        def queries(i):
            return (0, META) if i == 0 else (META + P * (i - 1), P)

        def keys(i):
            return [(0, META)] + [(META + P * j, P) for j in range(i)]

        def span(i):
            return META + P * i
        S0 = BANK - META

        TURNS = 3 * HEADS + 4

        def tiles(s):
            h, r = s // 3 - 1, s % 3
            if not 0 <= h < HEADS:
                return []
            return [5 * h + i for i in ((0, 1), (2, 3), (4,))[r]]

        def meta_bank(i):
            return (PV, P) if i == 4 else (PO, 3 * P)

        def turned_head(s):
            h = HEADS - 1 if s == TURNS - 1 else (s - 8) // 3
            return h if (s % 3 == 2 and 0 <= h < HEADS - 1) or s == TURNS - 1 else None

        Z_SLOT = [0] + [i + p for p in range(PAIRS) for i in (1, 5, 9)]

        def feature_step(j):
            p, i = divmod(j - 2, 5)
            return (p, i) if j >= 2 and p < PAIRS else (None, None)

        SYSTEM = [("gram", 0), ("gram", 1), ("lm", 0), ("lm", 1), ("gram", 2), ("gram", 3), ("rv", 0), ("D2", 0), ("at", 0),
                  ("D2", 1), ("bk", 0), ("D4", 0), ("y2", 0), ("bk", 1), ("D4", 1), ("y2", 1), ("w", 0), ("D8", 0), ("y3", 0),
                  ("D8", 1), ("y3", 1)]
        SYSTEM += [(n, g) for n in ("y4", "td", "ht", "z1", "z2", "z3") for g in range(2)] + [("q", 0), ("pt", 0)]
        CHAIN = [("u", 0)] + [(n, c + d) for c in range(NCH - 1) for n, d in (("s", 0), ("u", 1))]
        TAIL = CHAIN + [("y", 0), ("y", 1), ("mu", 0), ("sq", 0), ("var", 0), ("sd", 0), ("norm", 0)]
        LEAD = 5

        def woven(p):
            other = [(tail_, p - 1, *t) for t in TAIL] if p else [(mix_, g, "mix", 0) for g in range(4)]
            lead = LEAD if p else 20
            if p == PAIRS:
                return other
            steps = []
            for i, t in enumerate(SYSTEM):
                steps.append((system_, p, *t))
                if i >= lead and other:
                    steps.append(other.pop(0))
            return steps + other
        system_, tail_, mix_ = range(3)

        def alpha(p, x, c):
            return z[ROW[x], 1 + p, 1 + CH * c:1 + CH * c + CH]

        def rcv(p, x, c):
            return z[ROW[x], 5 + p, 1 + CH * c:1 + CH * c + CH]

        def state(p, c):
            return z[:, 9 + p, 1 + CH * c:1 + CH * c + CH]

        block = whole.enter_context(nc.Block())

        @block.sync
        def _(sp):
            sp.dma_start(vec[:], vecs).then_inc(inputs_loaded, 16)
            sp.dma_start(con[:], consts).then_inc(inputs_loaded, 16)
            sp.dma_start(mat[:], mats).then_inc(inputs_loaded, 16)
            sp.dma_start(hres[:], xT.rearrange("(k p) t -> p k t", p=P)).then_inc(inputs_loaded, 16)

            def load(b, j, s):
                if not isinstance(b, int):
                    sp.wait_ge(lo_ready, b - 3)
                elif b >= 4:
                    sp.wait_ge(lo_ready, b - 3)
                src = weights[b] if isinstance(b, int) else weights[bass.ds(b, 1)].rearrange("b p n -> p (b n)")
                sp.dma_start(raw[:, s], src).then_inc(w_loaded[s], 16)
            blocks(sp, 0, NBLK, load)
            for k in range(KT):
                sp.wait_ge(S("out_ready"), k + 1)
                sp.dma_start(out[k * P:(k + 1) * P, :], hres[:, k, META:]).then_inc(stored, 16)
            sp.wait_ge(stored, 16 * KT)

        @block.gpsimd
        def _(pool):
            def low(b, j, s):
                pool.wait_ge(hi_ready, b + 1)
                if not isinstance(b, int) or b >= 2:
                    pool.wait_ge(block_done, b - 1)
                nc.gpsimd.tensor_tensor(wlo[:, s % 2], raw[:, s], whi[:, s % 2].bitcast(F32), ALU.subtract)\
                    .then_inc(lo_ready, 1)
            blocks(pool, 0, B_O2 + 2, low)

            pool.wait_ge(tile_out, B_IN2 + 17)
            pool.wait_ge(S("BK_ready"), 4 * PAIRS)
            pool.wait_ge(S("pads_set"), 3)
            n = 0
            for g, w in enumerate(POOL_W):
                src = zu[:, g]
                for i in range(g + 1):
                    dst = t1[:, i % 2]
                    sh = 1 << i
                    if n:
                        pool.wait_ge(S("pool_step"), n)
                    nc.gpsimd.tensor_tensor(dst[:, PAD:], src[:, PAD:], src[:, PAD - sh:PAD + SEQ - sh], ALU.add)\
                        .then_inc(S("pool_step"), 1)
                    src = dst
                    n += 1
                mean = (Gt, Gi, cs, Gp)[g]
                fix = con[:, C_PFIX + 16 * g:C_PFIX + 16 * g + 16]
                pool.wait_ge(S("pool_step"), n)
                nc.gpsimd.tensor_tensor(src[:, PAD:PAD + 16], src[:, PAD:PAD + 16], fix, ALU.mult)\
                    .then_inc(S("pool_step"), 1)
                pool.wait_ge(S("pool_step"), n + 1)
                nc.gpsimd.tensor_scalar(mean[:], src[:, PAD:], 1.0 / w, None, ALU.mult).then_inc(S("pool_step"), 1)
                pool.wait_ge(S("pool_step"), n + 2)
                nc.gpsimd.tensor_tensor(mean[:], mean[:], zu[:, g, PAD:], ALU.subtract).then_inc(S("pooled"), 1)
                n += 2
            blocks(pool, B_O2 + 2, KT - 2, low)

        @block.scalar
        def _(act):
            def split(b, s):
                if isinstance(b, int):
                    if b >= NBLK:
                        return
                    act.wait_ge(w_loaded[s], 16 * (b // 4 + 1))
                    if b >= 2:
                        act.wait_ge(block_done, b - 1)
                nc.scalar.activation(whi[:, s % 2], raw[:, s], ACT.Copy).then_inc(hi_ready, 1)

            def step(b0, n, evac=None):
                def body(b, j, s):
                    if isinstance(b, int):
                        split(b + 2, (s + 2) % 4)
                    else:
                        i4 = b - s
                        s2 = (s + 2) % 4
                        act.wait_ge(w_loaded[s2], (i4 + 4 * ((s + 2) // 4)) * 4 + 16)
                        act.wait_ge(block_done, b + 1)
                        nc.scalar.activation(whi[:, s2 % 2], raw[:, s2], ACT.Copy).then_inc(hi_ready, 1)
                    if evac:
                        evac(b, j, s)
                blocks(act, b0, n, body)

            def stat_root(s, cols):
                if s % 2 == 0:
                    act.wait_ge(sq_used, 8 * (s // 2 + 1))
                else:
                    act.wait_ge(post_sum, s // 2 + 1)
                if s >= 1:
                    act.wait_ge(rstd_ready, s)
                _, pos = where(cols)
                nc.scalar.activation(rms[:, cols[0]:cols[1]], ST[:, pos], ACT.Sqrt, scale=1.0 / D, bias=eps_t[:, 0:1])\
                    .then_inc(rms_ready, 1)

            def prenorm(f, s, layer, n, cols, h0):
                c = slice(*cols)
                for k in range(KT):
                    if h0 is None:
                        act.wait_ge(inputs_loaded, 64)
                    else:
                        act.wait_ge(h_ready, h0 + k + 1)
                    nc.scalar.activation((x2h if layer == 2 else xh)[:, k, c], hres[:, k, c], ACT.Copy,
                                         scale=gain(layer, n, k)).then_inc(x_hi, 1)
                    if 4 * s + k >= 2:
                        act.wait_ge(sq_used, 4 * s + k - 1)
                    nc.scalar.activation(sq[:, k % 2, c], hres[:, k, c], ACT.Square).then_inc(sq_ready, 1)
                stat_root(s, cols)

            def post_squares(b0, s, cols):
                w = cols[1] - cols[0]

                def evac(b, j, s4):
                    act.wait_ge(tile_out, b + 1)
                    n = 4 * (s - 1) + j
                    if n >= 2:
                        act.wait_ge(psq_added, n - 1)
                    nc.scalar.activation(sq[:, s4 % 2, 0:w], m[:, j, 0:w], ACT.Square).then_inc(psq_ready, 1)
                straight(b0, evac)

            def mlp(layer, cols, s):
                b0 = B_MLP[layer]
                w = cols[1] - cols[0]
                for c in range(FF_CHUNKS + 1):
                    if c < FF_CHUNKS:
                        f = 5 * layer + c + 1
                        n0 = 32 * layer + 8 * c

                        def up(b, j, s4):
                            act.wait_ge(tile_out, b + 1)
                            nc.scalar.activation(tile(ah[f % 2], j, slice(0, w)), t1[:, s4 % 2, 0:w], ACT.Square)\
                                .then_inc(a_hi, 1)
                            act.wait_ge(a_ready, j + (8 * f - 1))
                            nc.scalar.activation(act2[:, s4 % 2, 0:w], t1[:, s4 % 2, 0:w], ACT.Square)\
                                .then_inc(sqr_ready, 1)
                        step(b0 + UP[c], 8, up)
                    if c >= 1 and c < FF_CHUNKS:
                        step(b0 + DOWN[c - 1], 8)
                    elif c == FF_CHUNKS:
                        post_squares(b0 + DOWN[c - 1], s, cols)

            def straight(b0, evac):
                for j in range(8):
                    b = b0 + j
                    split(b + 2, (b + 2) % 4)
                    evac(b, j, b % 4)

            act.wait_ge(oss_set, 3)
            act.wait_ge(inputs_loaded, 64)
            split(0, 0)
            split(1, 1)
            prenorm(0, 0, 0, 0, ALL, None)
            act.wait_ge(lam_prod, 2)
            nc.scalar.activation(lamd[:, 2:4], lamd[:, 0:2], ACT.Exp).then_inc(lam_exp, 1)

            for s in range(TURNS):
                prev, cur = tiles(s - 1), tiles(s)
                if s < 24:
                    split(s + 2, (s + 2) % 4)
                if s % 3 == 2 and s < 24:
                    h = s // 3
                    if h >= 2:
                        act.wait_ge(negs_ready, 10 * (h - 1))
                    slope = 2.0 ** (-8.0 * (h + 1) / HEADS)
                    nc.scalar.activation(biasT[:, h % 2], con[:, C_DIST:C_DIST + TOK], ACT.Copy, scale=slope)\
                        .then_inc(bias_ready, 1)
                if cur and s % 3 == 0:
                    h = s // 3 - 1
                    act.wait_ge(v_turned, h + 1)
                    if h >= 2:
                        act.wait_ge(o_ready, 5 * (h - 1))
                    nc.scalar.activation(vtok[:, h % 2, 1:5, :], G[1][:, BANK:].rearrange("p (j v) -> p j v", v=P), ACT.Copy)\
                        .then_inc(v_copied, 1)
                    nc.scalar.activation(vtok[0:META, h % 2, 0, :], G[1][0:META, 0:P], ACT.Copy).then_inc(v_copied, 1)

                def head_high():
                    h = turned_head(s)
                    act.wait_ge(ot_ready, h + 1)
                    nc.scalar.activation(ah[0][:, h, :], ST[:, where(NEED)[1]], ACT.Copy, scale=gsub[:, 0:1])\
                        .then_inc(a_hi, 1)
                if turned_head(s) is not None and s < TURNS - 1:
                    head_high()
                for t in prev:
                    i = t % 5
                    rows = queries(i)[1]
                    act.wait_ge(at_ready, t + 1)
                    if t >= 2:
                        act.wait_ge(o_ready, t - 1)
                    if i > 0:
                        nc.scalar.activation(aT[:, t % 2, 1:1 + i, :], PO[:, 0:P * i].rearrange("p (j v) -> p j v", v=P),
                                             ACT.Copy)
                    mb, m0 = meta_bank(i)
                    nc.scalar.activation(aT[0:META, t % 2, 0, 0:rows], mb[0:META, m0:m0 + rows], ACT.Copy)\
                        .then_inc(at_copied, 1)
                for t in prev:
                    h, i = divmod(t, 5)
                    rows = queries(i)[1]
                    act.wait_ge(o_ready, t + 1)
                    if h >= 2:
                        act.wait_ge(osc_ready, 5 * (h - 1))
                    nc.scalar.activation(o_all[0:rows, h % 2, i, :], PV[0:rows, 0:P], ACT.Copy,
                                         scale=rden[0:rows, 0, t:t + 1]).then_inc(o_copied, 1)
                    act.wait_ge(o_copied, t + 1)
                    if t >= 1:
                        act.wait_ge(oss_ready, t)
                    nc.scalar.activation(o_sq[0:rows, :], o_all[0:rows, h % 2, i, :], ACT.Square,
                                         accum_out=oss[0:rows, t:t + 1]).then_inc(oss_ready, 1)
                for n in cur:
                    i = n % 5
                    rows, w = queries(i)[1], span(i)
                    for c in range(2):
                        act.wait_ge(negs_ready, 2 * n + c + 1)
                        if n >= 2:
                            act.wait_ge(at_ready, n - 1)
                        nc.scalar.activation(prob[0:rows, n % 2, c, 0:w], negs[0:rows, n % 2, c, 0:w], ACT.Exp, scale=-1.0,
                                             bias=nmax[0:rows, c, n:n + 1], accum_out=den[0:rows, c, n:n + 1])\
                            .then_inc(prob_ready, 1)
                if prev and prev[-1] % 5 == 4:
                    h = prev[-1] // 5
                    act.wait_ge(oss_ready, 5 * (h + 1))
                    hs = slice(5 * h, 5 * h + 5)
                    nc.scalar.activation(orms[:, hs], oss[:, hs], ACT.Sqrt, scale=1.0 / P, bias=eps_t[:, 0:1])\
                        .then_inc(orms_ready, 1)
                if s == TURNS - 1:
                    head_high()

            post_squares(B_AO, 1, NEED)
            stat_root(1, NEED)
            prenorm(1, 2, 0, 2, NEED, 0)
            mlp(0, NEED, 3)
            stat_root(3, NEED)
            prenorm(2, 4, 1, 0, NEED, 8)

            for j in range(KT):
                for r in range(3):
                    b = B_CI + 3 * j + r
                    split(b + 2, (b + 2) % 4)
                act.wait_ge(conv_step, 5 * j + 5)
                nc.scalar.activation(ah[1][:, j, 0:SEQ], m[:, j, 2:2 + SEQ], ACT.Copy).then_inc(a_hi, 1)
            post_squares(B_CO, 5, OUT)
            stat_root(5, OUT)
            prenorm(3, 6, 1, 2, OUT, 16)
            mlp(1, OUT, 7)
            stat_root(7, OUT)
            prenorm(4, 8, 2, 0, OUT, 24)
            for j in range(25):
                split(B_IN2 + j + 2, (B_IN2 + j + 2) % 4)
                p, i = feature_step(j)
                if j == 1:
                    act.wait_ge(S("shifted"), 1)
                    nc.scalar.activation(tw[:], z[0:HD, 0, 1:], ACT.Tanh).then_inc(S("tanh_ready"), 1)
                if i == 0:
                    act.wait_ge(S("ww_ready"), p + 1)
                    if p:
                        act.wait_ge(S("BK_ready"), 4 * p)
                    nc.scalar.activation(sg[:], bank(4), ACT.Sigmoid, bias=col(V_W0, p)).then_inc(S("sg_ready"), 1)
                    act.wait_ge(S("aa_ready"), p + 1)
                    nc.scalar.activation(av[:], bank(5), ACT.Sigmoid, bias=col(V_A0, p)).then_inc(S("av_ready"), 1)
                    act.wait_ge(S("shifted"), 3 * p + 2)
                    nc.scalar.activation(kn[:], z[:, 1 + p, 1:], ACT.Square, scale=col(V_KK, p)).then_inc(S("ksq_ready"), 1)
                if i == 1:
                    act.wait_ge(S("knorm_sum"), p + 1)
                    nc.scalar.activation(kn[:], bank(6), ACT.Sqrt).then_inc(S("kn_ready"), 1)
                    act.wait_ge(S("cp_ready"), p + 1)
                    nc.scalar.activation(Gt[:], cs[:], ACT.Exp, scale=-DECAY).then_inc(S("Gt_ready"), 1)
                    nc.scalar.activation(Gi[:], cs[:], ACT.Exp, scale=DECAY).then_inc(S("Gi_ready"), 1)
                    nc.scalar.activation(Gp[:], Gp[:], ACT.Exp, scale=-DECAY).then_inc(S("Gp_ready"), 1)
                for n in {20: range(4), 21: (4,), 22: (5,), 23: (6,), 24: (7,)}.get(j, ()):
                    act.wait_ge(tile_out, B_IN2 + 18 + n)
                    nc.scalar.activation(gate[:, n], gate[:, n], ACT.Silu).then_inc(S("gate_ready"), 1)

            def copy_out(need, n, done, dst, src):
                act.wait_ge(S(need), n)
                nc.scalar.activation(dst, src, ACT.Copy).then_inc(S(done), 1)

            def system(p, name, g):
                n2 = 2 * p + g + 1
                if name == "rv":
                    act.wait_ge(S("rv_turned"), p + 1)
                    for x in range(2):
                        nc.scalar.activation(UV[p % 2][x][ROW[1 - x]], chunks(bank(0))[ROW[1 - x]], ACT.Copy)\
                            .then_inc(S("vt_out"), 1)
                elif name == "at":
                    copy_out("at_turned", p + 1, "at_out", at_, chunks(bank(1)))
                elif name == "D2":
                    copy_out("d2_ready", n2, "d2_out", PB2[:, g].rearrange("p k c t -> p (k c t)"), bank(2 + g))
                elif name == "bk":
                    copy_out("bk_turned", n2, "bk_out", BKt[p % 2][g][:], chunks(bank(g)))
                elif name == "w":
                    copy_out("w_ready", p + 1, "w_out", Wm, chunks(bank(0)))
                elif name == "D4":
                    copy_out("d4_ready", n2, "d4_out", PB4[:, g].rearrange("p k c t -> p (k c t)"), bank(2 + g))
                elif name == "D8":
                    copy_out("d8_ready", n2, "d8_out", Dm[:, HALF[g]], chunks(bank(2 + g)[:, 0:4 * CH]))
                elif name == "td":
                    copy_out("td_ready", n2, "td_out", PB2[:, g, 0], chunks(bank(4 + g)[:, 0:4 * CH]))
                elif name == "ht":
                    copy_out("ht_ready", n2, "ht_out", PB2[:, g, 1], chunks(bank(4 + g)[:, 0:4 * CH]))
                elif name == "q":
                    copy_out("q_ready", p + 1, "q_out", BK[:, p, :, 0, :], chunks(bank(0)))
                elif name == "pt":
                    copy_out("pt_ready", p + 1, "pt_out", BK[:, p, :, 1, :], chunks(bank(1)))

            def tail(p, name, c):
                if name == "y" and c == 1:
                    copy_out("y_ready", p + 1, "yt_out", gn_y, bank(7))
                elif name == "sq":
                    act.wait_ge(S("yc_ready"), p + 1)
                    nc.scalar.activation(gn_sd, gn_c, ACT.Square).then_inc(S("ysq_ready"), 1)
                elif name == "sd":
                    act.wait_ge(S("var_ready"), p + 1)
                    nc.scalar.activation(gn_sd, bank(7), ACT.Sqrt, scale=1.0 / HD, bias=eps_t[:, 1:2])\
                        .then_inc(S("sd_ready"), 1)

            for p in range(PAIRS + 1):
                for kind, n, name, g in woven(p):
                    if kind == system_:
                        system(n, name, g)
                    elif kind == tail_:
                        tail(n, name, g)

            for k in range(KT):
                if k < 4:
                    act.wait_ge(S("ya_ready"), k + 1)
                    src = zu[:, k, PAD:]
                else:
                    act.wait_ge(S("yb_ready"), k - 3)
                    src = z[:, 1 + k, 1:]
                nc.scalar.activation(x2h[:, k, META:], src, ACT.Copy).then_inc(x_hi, 1)
            for j in range(KT):
                split(B_O2 + j + 2, (B_O2 + j + 2) % 4)
                act.wait_ge(tile_out, B_O2 + j + 1)
                n = 32 + j
                act.wait_ge(psq_added, n - 1)
                nc.scalar.activation(sq[:, (B_O2 + j) % 2, 0:SEQ], hres[:, j, META:], ACT.Square).then_inc(psq_ready, 1)
            stat_root(9, OUT)

        @block.vector
        def _(dve):
            def stat_recip(s, cols):
                c = slice(*cols)
                dve.wait_ge(rms_ready, s + 1)
                nc.vector.reciprocal(rstd[:, s % 2, c], rms[:, c]).then_inc(rstd_ready, 1)

            def low_x(f, layer, n, k, c):
                dve.wait_ge(x_hi, 8 * f + k + 1)
                hi, lo = (x2h, x2l) if layer == 2 else (xh, xl)
                nc.vector.scalar_tensor_tensor(lo[:, k, c], hres[:, k, c], gain(layer, n, k), hi[:, k, c].bitcast(F32),
                                               ALU.mult, ALU.subtract).then_inc(x_ready, 1)

            def postnorm(s, layer, n, cols, h0, pre):
                c = slice(*cols)
                w = cols[1] - cols[0]
                dve.wait_ge(rstd_ready, s + 1)
                for k in range(KT + 2):
                    if k < KT:
                        if k >= 2:
                            dve.wait_ge(h_ready, h0 + k - 1)
                        nc.vector.scalar_tensor_tensor(t1[:, k % 2, 0:w], m[:, k, 0:w], gain(layer, n, k),
                                                       rstd[:, s % 2, c], ALU.mult, ALU.mult).then_inc(t1_ready, 1)
                    if 1 <= k <= KT:
                        dve.wait_ge(t1_ready, h0 + k)
                        nc.vector.tensor_tensor(hres[:, k - 1, c], hres[:, k - 1, c], t1[:, (k - 1) % 2, 0:w], ALU.add)\
                            .then_inc(h_ready, 1)
                    if k >= 2 and pre:
                        low_x(*pre, k - 2, c)

            def out_tiles(b0, cols, before=None, s=None):
                _, pos = where(cols)
                w = cols[1] - cols[0]

                def body(b, j, s):
                    dve.wait_ge(block_done, b + 1)
                    mt = tile(m, j, slice(0, w))
                    if before is None:
                        nc.vector.tensor_copy(mt, G[s % 2][:, pos]).then_inc(tile_out, 1)
                    else:
                        dve.wait_ge(tile_out, j + (before + 1))
                        nc.vector.tensor_tensor(mt, G[s % 2][:, pos], mt, ALU.add).then_inc(tile_out, 1)
                if s is None:
                    blocks(dve, b0, 8, body)
                    return
                for j in range(KT + 1):
                    if j < KT:
                        body(b0 + j, j, (b0 + j) % 4)
                    if j >= 1:
                        n = 4 * (s - 1) + j - 1
                        dve.wait_ge(psq_ready, n + 1)
                        if j == 1:
                            nc.vector.tensor_copy(acc[:, 0:w], sq[:, (j - 1) % 2, 0:w]).then_inc(psq_added, 1)
                        else:
                            dve.wait_ge(psq_added, n)
                            nc.vector.tensor_tensor(acc[:, 0:w], acc[:, 0:w], sq[:, (j - 1) % 2, 0:w], ALU.add)\
                                .then_inc(psq_added, 1)

            def mlp(layer, cols, s):
                b0 = B_MLP[layer]
                _, pos = where(cols)
                w = cols[1] - cols[0]
                c0 = slice(*cols)
                for c in range(FF_CHUNKS + 1):
                    if c < FF_CHUNKS:
                        f = 5 * layer + c + 1
                        n0 = 32 * layer + 8 * c

                        def low(j, s4):
                            dve.wait_ge(a_hi, j + (8 * f + 1))
                            dve.wait_ge(sqr_ready, j + (n0 + 1))
                            nc.vector.tensor_tensor(tile(al[f % 2], j, slice(0, w)), act2[:, s4 % 2, 0:w],
                                                    tile(ah[f % 2], j, slice(0, w)).bitcast(F32), ALU.subtract)\
                                .then_inc(a_ready, 1)

                        def up(b, j, s4):
                            dve.wait_ge(block_done, b + 1)
                            if n0 or c or not isinstance(j, int) or j >= 2:
                                dve.wait_ge(sqr_ready, j + (n0 - 1))
                            nc.vector.scalar_tensor_tensor(t1[:, s4 % 2, 0:w], G[s4 % 2][:, pos], 0.0, rstd[:, s % 2, c0],
                                                           ALU.max, ALU.mult).then_inc(tile_out, 1)
                            low(j, s4)
                        if f == 1:
                            for j in range(8):
                                up(b0 + UP[c] + j, j, (b0 + UP[c] + j) % 4)
                        else:
                            blocks(dve, b0 + UP[c], 8, up)
                    if c >= 1:
                        out_tiles(b0 + DOWN[c - 1], cols, None if c == 1 else b0 + DOWN[c - 2],
                                  s + 1 if c == FF_CHUNKS else None)

            nc.vector.memset(eps_t[:, 0:1], EPS).then_inc(oss_set, 1)
            nc.vector.memset(eps_t[:, 1:2], GN_EPS).then_inc(oss_set, 1)
            nc.vector.memset(oss[:], 1.0).then_inc(oss_set, 1)
            dve.wait_ge(inputs_loaded, 64)
            lam = vec[:, V_LAM:V_LAM + 256].rearrange("p (a b n) -> p a b n", a=2, b=2)
            for a in range(2):
                nc.vector.tensor_tensor_reduce(lamt[:, a, :], lam[:, a, 0, :], lam[:, a, 1, :], 1.0, 0.0, ALU.mult,
                                               ALU.add, lamd[:, a:a + 1]).then_inc(lam_prod, 1)
            nc.vector.tensor_scalar(gsub[:], vec[:, V_SUBLN:V_SUBLN + 1], 1.0 - LAM_INIT, None, ALU.mult)\
                .then_inc(lam_ready, 1)
            for k in range(KT):
                low_x(0, 0, 0, k, slice(*ALL))
            dve.wait_ge(lam_exp, 1)
            nc.vector.tensor_scalar(lamd[:, 4:5], lamd[:, 3:4], lamd[:, 2:3], -LAM_INIT, ALU.subtract, ALU.add)\
                .then_inc(lam_ready, 1)
            stat_recip(0, ALL)
            dve.wait_ge(rstd_ready, 1)
            dve.wait_ge(lam_ready, 2)
            _, pos = where(ALL)

            def scale_heads(h):
                hs = slice(5 * h, 5 * h + 5)
                dve.wait_ge(orms_ready, h + 1)
                nc.vector.reciprocal(orstd[:, hs], orms[:, hs]).then_inc(orstd_ready, 1)
                dve.wait_ge(orstd_ready, h + 1)
                if h >= 2:
                    dve.wait_ge(ot_ready, h - 1)
                for i in range(5):
                    rows = queries(i)[1]
                    t = 5 * h + i
                    nc.vector.tensor_scalar(o_sc[0:rows, h % 2, i, :], o_all[0:rows, h % 2, i, :], orstd[0:rows, t:t + 1],
                                            None, ALU.mult).then_inc(osc_ready, 1)

            for s in range(TURNS):
                if s < 24:
                    h, r = divmod(s, 3)
                    dve.wait_ge(block_done, s + 1)
                    nc.vector.scalar_tensor_tensor((qT, kT, vT)[r][:, h % 2, :], G[0][:, pos], 0.125 if r == 0 else 1.0,
                                                   rstd[:, 0, :], ALU.mult, ALU.mult).then_inc(tile_out, 1)
                if s == TURNS - 1:
                    scale_heads(HEADS - 1)
                if turned_head(s) is not None:
                    h = turned_head(s)
                    dve.wait_ge(a_hi, h + 1)
                    nc.vector.scalar_tensor_tensor(al[0][:, h, :], ST[:, where(NEED)[1]], gsub[:, 0:1],
                                                   ah[0][:, h, :].bitcast(F32), ALU.mult, ALU.subtract).then_inc(a_ready, 1)
                for n in tiles(s):
                    h, i = divmod(n, 5)
                    q0, rows = queries(i)
                    w = span(i)
                    sh = META + P * 3 - q0
                    dve.wait_ge(bias_ready, h + 1)
                    for c in range(2):
                        dve.wait_ge(scores_ready, 2 * n + c + 1)
                        if n >= 2:
                            dve.wait_ge(prob_ready, 2 * n + c - 3)
                        nc.vector.tensor_tensor_reduce(negs[0:rows, n % 2, c, 0:w], (G[1], ST)[c][0:rows, S0:S0 + w],
                                                       biasT[0:rows, h % 2, sh:sh + w], -1.0, 3e38, ALU.add, ALU.min,
                                                       nmax[0:rows, c, n:n + 1]).then_inc(negs_ready, 1)
                for t in tiles(s):
                    i = t % 5
                    rows, w = queries(i)[1], span(i)
                    dve.wait_ge(prob_ready, 2 * t + 2)
                    nc.vector.reciprocal(rden[0:rows, :, t:t + 1], den[0:rows, :, t:t + 1]).then_inc(coef_step, 1)
                    dve.wait_ge(coef_step, 2 * t + 1)
                    nc.vector.scalar_tensor_tensor(coef[0:rows, t:t + 1], rden[0:rows, 1, t:t + 1], lamd[0:rows, 4:5],
                                                   den[0:rows, 0, t:t + 1], ALU.mult, ALU.mult).then_inc(coef_step, 1)
                    dve.wait_ge(coef_step, 2 * t + 2)
                    nc.vector.scalar_tensor_tensor(prob[0:rows, t % 2, 1, 0:w], prob[0:rows, t % 2, 1, 0:w],
                                                   coef[0:rows, t:t + 1], prob[0:rows, t % 2, 0, 0:w],
                                                   ALU.mult, ALU.add).then_inc(a_done, 1)
                if s % 3 == 1 and 0 <= (s - 7) // 3 < HEADS - 1:
                    scale_heads((s - 7) // 3)
            out_tiles(B_AO, NEED, None, 1)
            stat_recip(1, NEED)
            postnorm(1, 0, 1, NEED, 0, (1, 0, 2))
            stat_recip(2, NEED)
            dve.wait_ge(rstd_ready, 3)
            mlp(0, NEED, 2)
            stat_recip(3, NEED)
            postnorm(3, 0, 3, NEED, 8, (2, 1, 0))
            stat_recip(4, NEED)
            dve.wait_ge(rstd_ready, 5)

            _, pos = where(NEED)
            c0 = slice(*NEED)
            w = NEED[1] - NEED[0]
            for j in range(KT):
                for r in range(3):
                    b = B_CI + 3 * j + r
                    dve.wait_ge(block_done, b + 1)
                    if j >= 1 and r == 0:
                        dve.wait_ge(conv_step, 5 * j)
                    nc.vector.scalar_tensor_tensor(cb[:, r, :], G[b % 2][:, pos], 1.0, rstd[:, 0, c0], ALU.mult, ALU.mult)\
                        .then_inc(tile_out, 1)
                dve.wait_ge(tile_out, B_CI + 3 * j + 3)
                taps = [vec[:, V_CONV + CW * j + i:V_CONV + CW * j + i + 1] for i in range(CW)]
                nc.vector.tensor_tensor(cb[:, 2, :], cb[:, 2, :], cb[:, 1, :], ALU.mult).then_inc(conv_step, 1)
                dve.wait_ge(conv_step, 5 * j + 1)
                y = m[:, j, 2:2 + SEQ]
                nc.vector.tensor_scalar(y, cb[:, 2, 0:SEQ], taps[0], None, ALU.mult).then_inc(conv_step, 1)
                dve.wait_ge(conv_step, 5 * j + 2)
                for i in (1, 2):
                    nc.vector.scalar_tensor_tensor(y, cb[:, 2, i:i + SEQ], taps[i], y, ALU.mult, ALU.add)\
                        .then_inc(conv_step, 1)
                    dve.wait_ge(conv_step, 5 * j + 2 + i)
                nc.vector.tensor_tensor(y, y, cb[:, 0, 2:2 + SEQ], ALU.mult).then_inc(conv_step, 1)
                dve.wait_ge(conv_step, 5 * j + 5)
                dve.wait_ge(a_hi, 40 + j + 1)
                nc.vector.tensor_tensor(al[1][:, j, 0:SEQ], y, ah[1][:, j, 0:SEQ].bitcast(F32), ALU.subtract)\
                    .then_inc(a_ready, 1)
            out_tiles(B_CO, OUT, None, 5)
            stat_recip(5, OUT)
            postnorm(5, 1, 1, OUT, 16, (3, 1, 2))
            stat_recip(6, OUT)
            dve.wait_ge(rstd_ready, 7)
            mlp(1, OUT, 6)
            stat_recip(7, OUT)
            postnorm(7, 1, 3, OUT, 24, (4, 2, 0))
            stat_recip(8, OUT)

            nc.vector.memset(z[:, :, 0:1], 0.0).then_inc(S("pads_set"), 1)
            nc.vector.memset(zu[:, :, 0:PAD], 0.0).then_inc(S("pads_set"), 1)
            nc.vector.memset(t1[:, :, 0:PAD], 0.0).then_inc(S("pads_set"), 1)
            dve.wait_ge(S("pads_set"), 3)
            dve.wait_ge(rstd_ready, 9)
            for j in range(25):
                b = B_IN2 + j
                dst = z[:, Z_SLOT[j], 1:] if j < 13 else zu[:, j - 13, PAD:] if j < 17 else gate[:, j - 17]
                dve.wait_ge(block_done, b + 1)
                nc.vector.scalar_tensor_tensor(dst, G[b % 2][:, BANK:], 1.0, rstd[:, 0, META:], ALU.mult, ALU.mult)\
                    .then_inc(tile_out, 1)
                if 1 <= j <= 13:
                    i = j - 1
                    zi = z[:, Z_SLOT[i]]
                    dve.wait_ge(tile_out, b)
                    if i >= 2:
                        dve.wait_ge(S("shifted"), i - 1)
                    nc.vector.tensor_tensor(t1[:, i % 2, PAD:], zi[:, 0:SEQ], zi[:, 1:], ALU.subtract)\
                        .then_inc(S("shift_step"), 1)
                    dve.wait_ge(S("shift_step"), i + 1)
                    nc.vector.scalar_tensor_tensor(zi[:, 1:], t1[:, i % 2, PAD:], col(V_MU, Z_SLOT[i]), zi[:, 1:], ALU.mult,
                                                   ALU.add).then_inc(S("shifted"), 1)
                p, i = feature_step(j)
                if i == 0 and p or j == 2 + 5 * PAIRS:
                    q = (j - 2) // 5 - 1
                    dve.wait_ge(S("bonus_sum"), q + 1)
                    nc.vector.tensor_tensor(bonus[:, q], bank(7), z[:, 9 + q, 1:], ALU.mult).then_inc(S("bonus_ready"), 1)
                if i is None:
                    continue
                zk, zr = z[:, 1 + p, 1:], z[:, 5 + p, 1:]
                if i == 1:
                    dve.wait_ge(S("sg_ready"), p + 1)
                    nc.vector.tensor_tensor_scan(cs[:], con[:, C_RESET:C_RESET + SEQ], sg[:], 0.0, ALU.mult, ALU.add)\
                        .then_inc(S("cs_ready"), 1)
                    dve.wait_ge(S("cs_ready"), p + 1)
                    nc.vector.tensor_tensor(Gp[:], cs[:], sg[:], ALU.subtract).then_inc(S("cp_ready"), 1)
                    dve.wait_ge(S("av_ready"), p + 1)
                    dve.wait_ge(S("cp_ready"), p + 1)
                    nc.vector.tensor_scalar(sg[:], av[:], 1.0, col(V_KA, p), ALU.subtract, ALU.mult)\
                        .then_inc(S("ka_ready"), 1)
                    dve.wait_ge(S("ka_ready"), p + 1)
                    dve.wait_ge(S("shifted"), 3 * p + 2)
                    nc.vector.scalar_tensor_tensor(k2[:], sg[:], 1.0, zk, ALU.add, ALU.mult).then_inc(S("k2_ready"), 1)
                elif i == 2:
                    dve.wait_ge(S("kn_ready"), p + 1)
                    nc.vector.tensor_scalar(kn[:], kn[:], 1e-12, None, ALU.max).then_inc(S("km_ready"), 1)
                    dve.wait_ge(S("km_ready"), p + 1)
                    nc.vector.reciprocal(kn[:], kn[:]).then_inc(S("kr_ready"), 1)
                elif i == 3:
                    dve.wait_ge(S("Gp_ready"), p + 1)
                    dve.wait_ge(S("k2_ready"), p + 1)
                    dve.wait_ge(S("shifted"), 3 * p + 3)
                    nc.vector.scalar_tensor_tensor(sg[:], zr, col(V_RK, p), k2[:], ALU.mult, ALU.mult)\
                        .then_inc(S("rk_ready"), 1)
                    dve.wait_ge(S("kr_ready"), p + 1)
                    nc.vector.scalar_tensor_tensor(cs[:], zk, col(V_KK, p), kn[:], ALU.mult, ALU.mult)\
                        .then_inc(S("kk_ready"), 1)
                    nc.vector.tensor_tensor(zr, zr, Gt[:], ALU.mult).then_inc(S("R_ready"), 1)
                    dve.wait_ge(S("kk_ready"), p + 1)
                    nc.vector.scalar_tensor_tensor(zk, cs[:], -1.0, Gp[:], ALU.mult, ALU.mult).then_inc(S("al_ready"), 1)
                    nc.vector.tensor_tensor(av[:], cs[:], av[:], ALU.mult).then_inc(S("bb_ready"), 1)
                elif i == 4:
                    nc.vector.tensor_copy(g_end[:, p], chunks(Gt[:])[:, :, CH - 1]).then_inc(S("end_ready"), 1)
                    dve.wait_ge(S("bb_ready"), p + 1)
                    dve.wait_ge(S("R_ready"), p + 1)
                    dve.wait_ge(S("al_ready"), p + 1)
                    for x in range(2):
                        r = ROW[x]
                        nc.vector.tensor_tensor(BK[r, p, :, x, :], chunks(av[r]), chunks(Gi[r]), ALU.mult)\
                            .then_inc(S("BK_ready"), 1)
                        nc.vector.tensor_tensor(BK[r, p, :, 1 - x, :], chunks(k2[r]), chunks(Gi[r]), ALU.mult)\
                            .then_inc(S("BK_ready"), 1)

            def mask(c0):
                return con[:, c0:c0 + CH].unsqueeze(1).to_broadcast([P, 4, CH])

            def system(p, name, k):
                n2 = 2 * p + k + 1

                def add_out(need, dst, base, based, done):
                    dve.wait_ge(S(need), n2)
                    dve.wait_ge(S(based), n2)
                    nc.vector.tensor_tensor(dst, chunks(bank(4 + k)[:, 0:4 * CH]), base[:, HALF[k]], ALU.add)\
                        .then_inc(S(done), 1)

                if name == "gram":
                    x, g = divmod(k, 2)
                    r = ROW[x]
                    dve.wait_ge(S("gram_ready"), 4 * p + k + 1)
                    gram = bank(2 * (1 - x) + g).rearrange("p (c t) -> p c t", t=2 * CH)
                    nc.vector.tensor_tensor(MR[p % 2][x][:, HALF[g]], gram[:, :, CH:], mask(C_MR), ALU.mult)\
                        .then_inc(S("gram_out"), 1)
                    nc.vector.tensor_tensor(DL[x][:, HALF[g]], gram[:, :, 0:CH], mask(C_MDL + CH * x), ALU.mult)\
                        .then_inc(S("gram_out"), 1)
                    nc.vector.tensor_tensor(ET[r, HALF[g]], gram[r, :, 0:CH], mask(C_ME)[r], ALU.mult)\
                        .then_inc(S("gram_out"), 1)
                elif name == "lm":
                    dve.wait_ge(S("lm_ready"), n2)
                    nc.vector.tensor_tensor(Dm[:, HALF[k]], chunks(bank(4 + k)[:, 0:4 * CH]), mask(C_MD), ALU.mult)\
                        .then_inc(S("D_out"), 1)
                elif name == "rv":
                    dve.wait_ge(S("gram_out"), 12 * (p + 1))
                    for x in range(2):
                        r = ROW[x]
                        eye = con[r, C_IDENT + HD * x:C_IDENT + HD * x + HD].unsqueeze(1).to_broadcast([HD, NCH, CH])
                        nc.vector.tensor_tensor(Ya[r], DL[x][r], eye, ALU.add).then_inc(S("y1_out"), 1)
                elif name == "y2":
                    dve.wait_ge(S("y1_out"), 2 * (p + 1))
                    add_out("y2_ready", Yb[:, HALF[k]], Ya, "D_out", "y2_out")
                elif name == "y3":
                    add_out("y3_ready", Ya[:, HALF[k]], Yb, "y2_out", "y3_out")
                elif name == "y4":
                    add_out("y4_ready", Yb[:, HALF[k]], Ya, "y3_out", "y4_out")
                elif name == "z1":
                    add_out("z1_ready", Ya[:, HALF[k]], Yb, "y4_out", "z1_out")
                elif name == "z2":
                    add_out("z2_ready", PB4[:, k, 0], Yb, "y4_out", "z2_out")
                elif name == "z3":
                    add_out("z3_ready", Ya[:, HALF[k]], Yb, "y4_out", "z3_out")

            def tail(p, name, c):
                U = UV[p % 2]
                if name == "u":
                    if c == 0:
                        dve.wait_ge(S("q_out"), p + 1)
                        for x in range(2):
                            nc.vector.tensor_copy(U[x][ROW[x], 0, :], BK[ROW[x], p, 0, 0, :]).then_inc(S("u_out"), 1)
                        return
                    if c < NCH - 1:
                        dve.wait_ge(S("s_out"), (NCH - 1) * p + c)
                        nc.vector.tensor_scalar(Sg[:], state(p, c), g_end[:, p, c:c + 1], None, ALU.mult)\
                            .then_inc(S("sg_out"), 1)
                    dve.wait_ge(S("u_ready"), (NCH - 1) * p + c)
                    for x in range(2):
                        nc.vector.tensor_tensor(U[x][ROW[x], c, :], bank(6)[ROW[x], 0:CH], BK[ROW[x], p, c, 0, :], ALU.add)\
                            .then_inc(S("u_out"), 1)
                elif name == "s":
                    end = g_end[:, p, c:c + 1]
                    dve.wait_ge(S("s_ready"), (NCH - 1) * p + c + 1)
                    if c == 0:
                        nc.vector.tensor_scalar(state(p, 1), bank(6)[:, CH:2 * CH], end, None, ALU.mult)\
                            .then_inc(S("s_out"), 1)
                    else:
                        dve.wait_ge(S("sg_out"), (NCH - 2) * p + c)
                        nc.vector.scalar_tensor_tensor(state(p, c + 1), bank(6)[:, CH:2 * CH], end, Sg[:], ALU.mult, ALU.add)\
                            .then_inc(S("s_out"), 1)
                elif name == "mu":
                    dve.wait_ge(S("yt_out"), p + 1)
                    dve.wait_ge(S("mu_ready"), p + 1)
                    nc.vector.scalar_tensor_tensor(gn_c, bank(7), -1.0 / HD, gn_y, ALU.mult, ALU.add)\
                        .then_inc(S("yc_ready"), 1)
                elif name == "norm":
                    dve.wait_ge(S("sd_ready"), p + 1)
                    nc.vector.reciprocal(gn_y, gn_sd).then_inc(S("rs_ready"), 1)
                    dve.wait_ge(S("rs_ready"), p + 1)
                    nc.vector.scalar_tensor_tensor(gn_c, gn_c, col(V_GG, p), gn_y, ALU.mult, ALU.mult)\
                        .then_inc(S("yn_ready"), 1)
                    dve.wait_ge(S("yn_ready"), p + 1)
                    nc.vector.scalar_tensor_tensor(gn_c, gn_c, col(V_GB, p), bonus[:, p], ALU.add, ALU.add)\
                        .then_inc(S("yw_ready"), 1)
                    dve.wait_ge(S("yw_ready"), p + 1)
                    dve.wait_ge(S("gate_ready"), 5 + p)
                    nc.vector.tensor_tensor(z[:, 5 + p, 1:], gn_c, gate[:, 4 + p], ALU.mult).then_inc(S("yb_ready"), 1)

            for p in range(PAIRS + 1):
                for kind, n, name, g in woven(p):
                    if kind == system_:
                        system(n, name, g)
                    elif kind == tail_:
                        tail(n, name, g)
                    else:
                        dve.wait_ge(S("mix_ready"), n + 1)
                        dve.wait_ge(S("gate_ready"), n + 1)
                        nc.vector.scalar_tensor_tensor(zu[:, n, PAD:], bank(6 + n % 2), col(V_POOL, n), gate[:, n], ALU.mult,
                                                       ALU.mult).then_inc(S("ya_ready"), 1)

            for k in range(KT):
                src = zu[:, k, PAD:] if k < 4 else z[:, 1 + k, 1:]
                dve.wait_ge(x_hi, 40 + k + 1)
                nc.vector.tensor_tensor(x2l[:, k, META:], src, x2h[:, k, META:].bitcast(F32), ALU.subtract)\
                    .then_inc(x_ready, 1)
            for j in range(KT + 1):
                if j < KT:
                    b = B_O2 + j
                    dve.wait_ge(block_done, b + 1)
                    nc.vector.tensor_tensor(hres[:, j, META:], G[b % 2][:, BANK:], hres[:, j, META:], ALU.add)\
                        .then_inc(tile_out, 1)
                if j >= 1:
                    n = 32 + j - 1
                    dve.wait_ge(psq_ready, n + 1)
                    part = sq[:, (B_O2 + j - 1) % 2, 0:SEQ]
                    if j == 1:
                        nc.vector.tensor_copy(acc[:, 0:SEQ], part).then_inc(psq_added, 1)
                    else:
                        dve.wait_ge(psq_added, n)
                        nc.vector.tensor_tensor(acc[:, 0:SEQ], acc[:, 0:SEQ], part, ALU.add).then_inc(psq_added, 1)
            stat_recip(9, OUT)
            dve.wait_ge(rstd_ready, 10)
            for k in range(KT):
                nc.vector.scalar_tensor_tensor(hres[:, k, META:], hres[:, k, META:], col(V_FG, k), rstd[:, 1, META:], ALU.mult,
                                               ALU.mult).then_inc(S("out_ready"), 1)

        @block.tensor
        def _(pe):
            def stat_tile(s, k, cols):
                pieces, _ = where(cols)
                if k == 0 and s >= 1:
                    pe.wait_ge(rms_ready, s)
                n = 4 * s + k
                pe.wait_ge(sq_ready, n + 1)
                for t0, t1_, p0, p1 in pieces:
                    last = nc.tensor.matmul(ST[:, p0:p1], ones, sq[:, n % 2, t0:t1_], start=k == 0, stop=k == KT - 1,
                                            skip_group_check=True)
                last.then_inc(sq_used, 1)

            def post_stat(s, cols):
                pieces, _ = where(cols)
                off = cols[0]
                pe.wait_ge(rms_ready, s)
                pe.wait_ge(psq_added, 4 * (s + 1))
                for t0, t1_, p0, p1 in pieces:
                    last = nc.tensor.matmul(ST[:, p0:p1], ones, acc[:, t0 - off:t1_ - off], start=True, stop=True)
                last.then_inc(post_sum, 1)

            def product(b0, n, ready, first, hi, lo, cols, off, stat=None, acc_of=None, lead=False):
                pieces, _ = where(cols)

                def body(b, j, s, lead=False):
                    pe.wait_ge(lo_ready, b + 1)
                    if not isinstance(b, int) or b >= 2:
                        pe.wait_ge(tile_out, b - 1)
                    to = acc_of(b) if acc_of else G[s % 2]
                    for k in range(KT):
                        if lead:
                            pe.wait_ge(ready, first + k + 1)
                            if stat is not None:
                                stat_tile(stat, k, cols)
                        ws = slice(k * P, k * P + P)
                        for q, (wt, xt) in enumerate(((whi, hi), (whi, lo), (wlo, hi))):
                            for t0, t1_, p0, p1 in pieces:
                                last = nc.tensor.matmul(to[:, p0:p1], wt[:, s % 2, ws], xt[:, k, t0 - off:t1_ - off],
                                                        start=k == 0 and q == 0, stop=k == KT - 1 and q == 2)
                    last.then_inc(block_done, 1)
                if n == 1:
                    body(b0, 0, b0 % 4, lead)
                    return
                for j in range(4):
                    body(b0 + j, j, (b0 + j) % 4, j == 0)
                if n - 4 >= 8:
                    with pe.Fori(0, (n - 4) // 4) as i:
                        for u in range(4):
                            body(i * 4 + (b0 + 4 + u), i * 4 + (4 + u), (b0 + u) % 4)
                    done = 4 + (n - 4) // 4 * 4
                else:
                    done = 4
                for j in range(done, n):
                    body(b0 + j, j, (b0 + j) % 4)
            def scores(n):
                h, i = divmod(n, 5)
                q0, rows = queries(i)
                pe.wait_ge(tile_out, 3 * h + 2)
                for c in range(2):
                    if n >= 1:
                        pe.wait_ge(negs_ready, 2 * n + c - 1)
                    if c == 0:
                        pe.wait_ge(v_copied, 2 * (h + 1))
                    elif n == 0:
                        pe.wait_ge(rms_ready, 1)
                    elif i == 4 and h >= 1:
                        pe.wait_ge(a_ready, h)
                    f = slice(64 * c, 64 * c + 64)
                    ps = (G[1], ST)[c]
                    qs = qT[f, h % 2, q0:q0 + rows]
                    last = nc.tensor.matmul(ps[0:rows, S0:S0 + META], qs, kT[f, h % 2, 0:META], start=True, stop=True)
                    if i > 0:
                        last = nc.tensor.matmul(ps[0:rows, BANK:BANK + P * i], qs, kT[f, h % 2, META:META + P * i],
                                                start=True, stop=True)
                    last.then_inc(scores_ready, 1)

            def turn_weights(t):
                i = t % 5
                rows = queries(i)[1]
                pe.wait_ge(a_done, t + 1)
                if t >= 1:
                    pe.wait_ge(at_copied, t)
                    if i == 4:
                        pe.wait_ge(o_copied, t)
                pr = prob[:, t % 2, 1]
                for j in range(1, i + 1):
                    nc.tensor.transpose(PO[:, P * (j - 1):P * j], pr[:, META + P * (j - 1):META + P * j], ident)
                mb, m0 = meta_bank(i)
                nc.tensor.transpose(mb[0:META, m0:m0 + rows], pr[0:rows, 0:META], ident[0:rows, 0:rows]).then_inc(at_ready, 1)

            def values(t):
                h, i = divmod(t, 5)
                rows = queries(i)[1]
                pe.wait_ge(at_copied, t + 1)
                if t >= 1:
                    pe.wait_ge(o_copied, t)
                for j, (_, nk) in enumerate(keys(i)):
                    last = nc.tensor.matmul(PV[0:rows, 0:P], aT[0:nk, t % 2, j, 0:rows], vtok[0:nk, h % 2, j, :],
                                            start=j == 0, stop=j == i)
                last.then_inc(o_ready, 1)

            def turn_values(h):
                pe.wait_ge(tile_out, 3 * h + 3)
                if h >= 1:
                    pe.wait_ge(negs_ready, 10 * h)
                for j in range(4):
                    nc.tensor.transpose(G[1][:, BANK + P * j:BANK + P * j + P], vT[:, h % 2, META + P * j:META + P * j + P],
                                        ident)
                nc.tensor.transpose(G[1][0:META, 0:P], vT[:, h % 2, 0:META], ident).then_inc(v_turned, 1)

            def turn_head(h, s):
                pe.wait_ge(osc_ready, 5 * (h + 1))
                pe.wait_ge(negs_ready, 10 * HEADS if s == TURNS - 1 else 2 * tiles(s)[0])
                for i in range(5):
                    q0, rows = queries(i)
                    p0 = q0 + BANK - SPLIT
                    last = nc.tensor.transpose(ST[:, p0:p0 + rows], o_sc[0:rows, h % 2, i, :], ident[0:rows, 0:rows])
                last.then_inc(ot_ready, 1)

            for s in range(TURNS):
                prev, cur = tiles(s - 1), tiles(s)
                if s == 0:
                    product(B_QKV, 1, x_ready, 0, xh, xl, ALL, 0, 0, acc_of=lambda b: G[0], lead=True)
                elif s < 24:
                    pe.wait_ge(tile_out, s)
                    product(B_QKV + s, 1, x_ready, 0, xh, xl, ALL, 0, acc_of=lambda b: G[0])
                if cur and s % 3 == 0:
                    turn_values(s // 3 - 1)
                if turned_head(s) is not None and s < TURNS - 1:
                    turn_head(turned_head(s), s)
                late = s % 3 != 1
                for k in range(2):
                    if k < len(prev):
                        turn_weights(prev[k])
                    if k < len(cur) and not late:
                        scores(cur[k])
                    if k < len(prev):
                        values(prev[k])
                if late:
                    for n in cur:
                        scores(n)
                if s == TURNS - 1:
                    turn_head(HEADS - 1, s)

            product(B_AO, 8, a_ready, 0, ah[0], al[0], NEED, NEED[0])
            post_stat(1, NEED)

            def mlp(layer, cols, xfill, s):
                b0 = B_MLP[layer]
                for c in range(FF_CHUNKS + 1):
                    f = 5 * layer + c + 1
                    if c < FF_CHUNKS:
                        product(b0 + UP[c], 8, x_ready, 8 * xfill, xh, xl, cols, 0, s - 1 if c == 0 else None)
                    if c >= 1:
                        product(b0 + DOWN[c - 1], 8, a_ready, 8 * (f - 1), ah[(f - 1) % 2], al[(f - 1) % 2], cols,
                                cols[0])
                post_stat(s, cols)

            mlp(0, NEED, 1, 3)
            product(B_CI, 24, x_ready, 16, xh, xl, NEED, 0, 4)
            product(B_CO, 8, a_ready, 40, ah[1], al[1], OUT, OUT[0])
            post_stat(5, OUT)
            mlp(1, OUT, 3, 7)

            blk = con[:, C_BLK:C_BLK + P]

            def mm(out_, lhsT, rhs, start=True, stop=True):
                return nc.tensor.matmul(out_, lhsT, rhs, start=start, stop=stop)

            for j in range(25):
                product(B_IN2 + j, 1, x_ready, 32, x2h, x2l, OUT, 0, 8, lead=j == 0)
                p, i = feature_step(j)
                if i == 0 and p or j == 2 + 5 * PAIRS:
                    q = (j - 2) // 5 - 1
                    pe.wait_ge(S("rk_ready"), q + 1)
                    if q:
                        pe.wait_ge(S("bonus_ready"), q)
                    mm(bank(7), blk, sg[:]).then_inc(S("bonus_sum"), 1)
                if i == 0:
                    ps = slice(P * p, P * p + P)
                    if p == 0:
                        pe.wait_ge(S("tanh_ready"), 1)
                        pe.wait_ge(rms_ready, 9)
                    else:
                        pe.wait_ge(S("av_ready"), p)
                    mm(bank(4), mat[0:HD, ps], tw[:]).then_inc(S("ww_ready"), 1)
                    mm(bank(5), mat[HD:P, ps], z[HD:P, 0, 1:]).then_inc(S("aa_ready"), 1)
                elif i == 1:
                    pe.wait_ge(S("ksq_ready"), p + 1)
                    if p:
                        pe.wait_ge(S("kn_ready"), p)
                    mm(bank(6), blk, kn[:]).then_inc(S("knorm_sum"), 1)

            def both(out_, lhsT, rhs, g):
                for x in range(2):
                    for c in range(4 * g, 4 * g + 4):
                        last = mm(out_(x, c), lhsT(x, c), rhs(x, c))
                return last

            def eye(x, c):
                return con[ROW[x], C_IDENT + HD * x:C_IDENT + HD * x + HD]

            def at4(b):
                return lambda x, c: bank(b + c // 4)[ROW[x], CH * (c % 4):CH * (c % 4) + CH]

            def at8(b, swap=False):
                return lambda x, c: bank(b)[ROW[1 - x if swap else x], CH * c:CH * c + CH]

            def of(t):
                return lambda x, c: t[ROW[x], c, :]

            def kind_of(t, kind):
                return lambda x, c: t[ROW[x], c // 4, kind, c % 4, :]

            def system(p, name, g):
                n2 = 2 * p + g + 1
                DT = lambda x, c: DL[x][ROW[x], c, :]
                LakT = lambda x, c: DL[x][ROW[1 - x], c, :]
                al = lambda x, c: alpha(p, x, c)
                halves = range(2)
                if name == "gram":
                    x, h = divmod(g, 2)
                    if p == 0 and g == 0:
                        pe.wait_ge(S("BK_ready"), 4 * PAIRS)
                        pe.wait_ge(tile_out, B_IN2 + 25)
                    elif p and x == 1:
                        pe.wait_ge(S(("q_out", "pt_out")[h]), p)
                    for c in range(4 * h, 4 * h + 4):
                        last = mm(bank(2 * (1 - x) + h)[:, 2 * CH * (c % 4):2 * CH * (c % 4 + 1)]
                                  .rearrange("p (k t) -> p k t", t=CH), BK[ROW[x], p, c].rearrange("p k t -> p (k t)"),
                                  z[ROW[x], 1 + p:6 + p:4, 1 + CH * c:1 + CH * c + CH])
                    last.then_inc(S("gram_ready"), 1)
                elif name == "lm":
                    both(at4(4), al, lambda x, c: BK[ROW[x], p, c, x, :], g).then_inc(S("lm_ready"), 1)
                elif name == "rv":
                    pe.wait_ge(S("gram_out"), 12 * p + 9)
                    pe.wait_ge(S("bonus_ready"), PAIRS)
                    for h in halves:
                        last = both(at8(0, True), lambda x, c: z[ROW[x], 9 + p, 1 + CH * c:1 + CH * c + CH], eye, h)
                    last.then_inc(S("rv_turned"), 1)
                elif name == "at":
                    pe.wait_ge(S("gram_out"), 12 * p + 12)
                    for h in halves:
                        last = both(at8(1), al, eye, h)
                    last.then_inc(S("at_turned"), 1)
                elif name == "D2":
                    pe.wait_ge(S("gram_out"), 12 * p + 9 + 3 * g)
                    pe.wait_ge(S("D_out"), n2)
                    both(lambda x, c: bank(2 + g)[ROW[x], CH * (c % 4):CH * (c % 4) + CH], DT, of(Dm), g)
                    both(lambda x, c: bank(2 + g)[ROW[x], CH * (4 + c % 4):CH * (5 + c % 4)], of(Dm), DT, g)\
                        .then_inc(S("d2_ready"), 1)
                elif name == "bk":
                    if g == 0:
                        pe.wait_ge(S("vt_out"), 2 * (p + 1))
                    else:
                        pe.wait_ge(S("at_out"), p + 1)
                    for c in range(NCH):
                        last = nc.tensor.transpose(bank(g)[:, CH * c:CH * c + CH],
                                                   BK[ROW[g], p, c].rearrange("p k t -> p (k t)"), eye(g, c))
                    last.then_inc(S("bk_turned"), 1)
                elif name == "w":
                    pe.wait_ge(S("bk_out"), 2 * p + 1)
                    for h in halves:
                        last = both(at8(0), LakT, lambda x, c: UV[p % 2][x][ROW[1 - x], c, :], h)
                    last.then_inc(S("w_ready"), 1)
                elif name == "D4":
                    pe.wait_ge(S("d2_out"), n2)
                    both(lambda x, c: bank(2 + g)[ROW[x], CH * (c % 4):CH * (c % 4) + CH], kind_of(PB2, 1), kind_of(PB2, 0), g)
                    both(lambda x, c: bank(2 + g)[ROW[x], CH * (4 + c % 4):CH * (5 + c % 4)], kind_of(PB2, 0),
                         kind_of(PB2, 1), g).then_inc(S("d4_ready"), 1)
                elif name == "y2":
                    pe.wait_ge(S("y1_out"), 2 * (p + 1))
                    both(at4(4), kind_of(PB2, 0), of(Ya), g).then_inc(S("y2_ready"), 1)
                elif name == "D8":
                    pe.wait_ge(S("d4_out"), n2)
                    both(at4(2), kind_of(PB4, 1), kind_of(PB4, 0), g).then_inc(S("d8_ready"), 1)
                elif name == "y3":
                    pe.wait_ge(S("y2_out"), n2)
                    both(at4(4), kind_of(PB4, 0), of(Yb), g).then_inc(S("y3_ready"), 1)
                elif name == "y4":
                    pe.wait_ge(S("y3_out"), n2)
                    pe.wait_ge(S("d8_out"), n2)
                    both(at4(4), of(Dm), of(Ya), g).then_inc(S("y4_ready"), 1)
                elif name == "td":
                    pe.wait_ge(S("y4_out"), n2)
                    both(at4(4), of(Yb), eye, g).then_inc(S("td_ready"), 1)
                elif name == "ht":
                    pe.wait_ge(S("td_out"), n2)
                    both(at4(4), of(ET), kind_of(PB2, 0), g).then_inc(S("ht_ready"), 1)
                elif name in ("z1", "z2", "z3"):
                    need, src = {"z1": ("ht_out", of(Yb)), "z2": ("z1_out", of(Ya)), "z3": ("z2_out", kind_of(PB4, 0))}[name]
                    pe.wait_ge(S(need), n2)
                    both(at4(4), kind_of(PB2, 1), src, g).then_inc(S(name + "_ready"), 1)
                elif name == "q":
                    pe.wait_ge(S("z3_out"), 2 * p + 2)
                    pe.wait_ge(S("w_out"), p + 1)
                    for h in halves:
                        last = both(at8(0), of(Ya), of(Wm), h)
                    last.then_inc(S("q_ready"), 1)
                elif name == "pt":
                    pe.wait_ge(S("bk_out"), 2 * p + 2)
                    for h in halves:
                        last = both(at8(1), of(at_), of(Ya), h)
                    last.then_inc(S("pt_ready"), 1)

            def tail(p, name, c):
                U = UV[p % 2]
                if name == "u" and c:
                    if c == 1:
                        pe.wait_ge(S("pt_out"), p + 1)
                    pe.wait_ge(S("s_out"), (NCH - 1) * p + c)
                    for x in range(2):
                        last = mm(bank(6)[ROW[x], 0:CH], BK[ROW[x], p, c, 1, :], state(p, c)[ROW[x]])
                    last.then_inc(S("u_ready"), 1)
                elif name == "s":
                    if p == 0 and c == 0:
                        pe.wait_ge(S("ya_ready"), 3)
                    pe.wait_ge(S("u_out"), 2 * (NCH * p + c + 1))
                    for x in range(2):
                        last = mm(bank(6)[ROW[x], CH:2 * CH], BKt[p % 2][x][:, c, :], U[x][:, c, :])
                    last.then_inc(S("s_ready"), 1)
                elif name == "y":
                    x = c
                    if x == 0:
                        pe.wait_ge(S("u_out"), 2 * NCH * (p + 1))
                        if p == 0:
                            pe.wait_ge(S("ya_ready"), 4)
                        else:
                            pe.wait_ge(S("sd_ready"), p)
                    for c in range(NCH):
                        o = at8(7)(x, c)
                        last = mm(o, U[x][:, c, :], MR[p % 2][x][:, c, :], stop=c == 0)
                        if c >= 1:
                            last = mm(o, state(p, c)[ROW[x]], rcv(p, x, c), start=False)
                    if x == 1:
                        last.then_inc(S("y_ready"), 1)
                elif name == "mu":
                    pe.wait_ge(S("yt_out"), p + 1)
                    mm(bank(7), blk, gn_y).then_inc(S("mu_ready"), 1)
                elif name == "var":
                    pe.wait_ge(S("ysq_ready"), p + 1)
                    mm(bank(7), blk, gn_sd).then_inc(S("var_ready"), 1)

            for p in range(PAIRS + 1):
                for kind, n, name, g in woven(p):
                    if kind == system_:
                        system(n, name, g)
                    elif kind == tail_:
                        tail(n, name, g)
                    else:
                        pe.wait_ge(S("pooled"), n + 1)
                        if n >= 2:
                            pe.wait_ge(S("ya_ready"), n - 1)
                        mm(bank(6 + n % 2), mat[:, SEQ + P * n:SEQ + P * n + P], (Gt, Gi, cs, Gp)[n][:])\
                            .then_inc(S("mix_ready"), 1)

            pe.wait_ge(S("ya_ready"), 4)
            product(B_O2, 8, x_ready, 40, x2h, x2l, OUT, 0)
            post_stat(9, OUT)


def layout(v):
    return v.reshape(-1, P).T


def weight_blocks(w):
    n = w.shape[1] // P
    return w.reshape(KT, P, n, P).transpose(2, 1, 0, 3).reshape(n, P, KT * P)


def kernel(**inputs):
    import concourse.bacc as bacc
    from concourse.bass_utils import run_bass_kernel_spmd as run

    a = {k: np.asarray(v) for k, v in inputs.items()}
    xT = np.ascontiguousarray(np.concatenate([a["meta_tokens"], a["x"][0]], axis=0).T)
    lam = np.broadcast_to(a["lambda_params"].reshape(1, 256), (P, 256))
    conv = a["conv_w"][0].reshape(CW, KT, P).transpose(2, 1, 0).reshape(P, KT * CW)
    mu = layout(a["shift_mu_2"])[:, [12, *range(4, 8), *range(0, 4), *range(8, 12)]]
    second = [layout(a[n]) for n in ("w0_2", "a0_2", "k_k_2", "k_a_2", "r_k_2", "gn_gain_2", "gn_bias_2", "final_gain_2")]
    vecs = np.ascontiguousarray(np.concatenate([layout(a["norm_g"]), layout(a["subln_g"]), conv, lam,
                                                layout(a["norm_gain_2"]), layout(a["pool_scale_2"]), mu, *second], axis=1))
    mats = np.concatenate([np.concatenate([a["w_up_2"][0], a["a_up_2"][0]], axis=0),
                           a["pool_w_2"][0].transpose(1, 0, 2).reshape(P, SEQ)], axis=1)

    q = np.arange(P)[:, None]
    dist = np.arange(TOK)[None, :] - META - 3 * P - q
    dist = np.where(dist > 0, MASKED, dist)
    heads = np.kron(np.eye(2), np.ones((HD, HD)))
    i, j = np.arange(CH)[:, None], np.arange(CH)[None, :]
    near = i // SUB == j // SUB
    twice = lambda m: np.concatenate([m, m], axis=0)
    diag, strict = near & (i < j), i < j
    mdl = np.concatenate([np.concatenate([diag, strict]), np.concatenate([strict, diag])], axis=1)
    reset = np.broadcast_to(np.arange(SEQ) % CH != 0, (P, SEQ))
    pos = np.arange(16)
    fix = np.concatenate([w / np.minimum(pos + 1, w) for w in POOL_W])
    consts = np.concatenate([np.eye(P), np.ones((P, P)), dist, heads, mdl, twice(i <= j), twice(strict & ~near),
                             twice(near & (j < i)), reset, np.broadcast_to(fix, (P, 64))], axis=1).astype(np.float32)

    def interleave(w, n):
        b = weight_blocks(w)
        return b.reshape(n, KT, P, D).transpose(1, 0, 2, 3).reshape(n * KT, P, D)

    def mlp_blocks(up, down):
        u = weight_blocks(up).reshape(FF_CHUNKS, KT, P, D)
        d = [weight_blocks(down[c * D:(c + 1) * D]) for c in range(FF_CHUNKS)]
        return [u[0], u[1], d[0], u[2], d[1], u[3], d[2], d[3]]

    w = [interleave(a["w_in"][0], 3), weight_blocks(a["w_out"][0])]
    w += mlp_blocks(a["w_up"][0], a["w_down"][0])
    w += [interleave(a["w_in"][1], 3), weight_blocks(a["w_out"][1])]
    w += mlp_blocks(a["w_up"][1], a["w_down"][1])
    w2 = weight_blocks(a["w_in_2"][0])
    w += [w2[[20, *(i + p for p in range(PAIRS) for i in (12, 8, 16)), *range(0, 8), *range(21, 25)]]]
    w += [weight_blocks(a["w_out_2"][0])]
    weights = np.concatenate(w, axis=0)

    nc = bacc.Bacc("TRN2", target_bir_lowering=False, num_devices=1)
    arrays, args = {}, []
    for name, v in (("xT", xT), ("vecs", vecs), ("consts", consts), ("mats", mats), ("weights", weights)):
        arrays[name + "_dram"] = v
        args.append(nc.dram_tensor(name + "_dram", v.shape, F32, kind="ExternalInput").ap())
    args.append(nc.dram_tensor("out_dram", (D, SEQ), F32, kind="ExternalOutput").ap())
    program(nc, *args)
    r = run(nc, [arrays], core_ids=[0])
    return np.ascontiguousarray(r.results[0]["out_dram"].T)[None]
```

```python
from contextlib import ExitStack
import math

import numpy as np
import concourse.bass as bass
from concourse import mybir

F32 = mybir.dt.float32
F32R = mybir.dt.float32r
ACT = mybir.ActivationFunctionType
ALU = mybir.AluOpType

P = 128
D = 1024
KT = D // P
META, SEQ = 16, 512
TOK = META + SEQ
HEADS = 8
CW = 3
FF_CHUNKS = 4
EPS = 1e-6
LAM_INIT = 0.8 - 0.6 * math.exp(-0.3 * 0)
MASKED = -1e32

ALL = (0, TOK)
NEED = (META - (CW - 1), TOK)
OUT = (META, TOK)
SPLIT = META + SEQ // 2
BANK = 512

V_NORM, V_SUBLN, V_CONV, V_LAM = 0, 64, 65, 89
V_N2 = V_LAM + 256
V_POOL, V_MU = V_N2 + 8, V_N2 + 12
V_W0 = V_MU + 13
V_A0, V_KK, V_KA, V_RK, V_GG, V_GB, V_FG = (V_W0 + 4 * i for i in range(1, 8))
V_END = V_FG + 8
C_IDENT, C_ONES, C_DIST = 0, P, 2 * P
C_BLK = C_DIST + TOK
C_MDL, C_MR, C_ME, C_MD = C_BLK + P, C_BLK + 2 * P, C_BLK + 2 * P + 64, C_BLK + 3 * P
C_RESET = C_MD + 64
C_PFIX = C_RESET + SEQ
C_END = C_PFIX + 4 * 16

HD = 64
CH = 64
SUB = 16
NCH = SEQ // CH
PAIRS = 4
GN_EPS = 64e-5
DECAY = math.exp(-0.5)
POOL_W = (2, 4, 8, 16)
PAD = 16

OPEN = 6
O2_TILES = [(o, k) for o in range(OPEN) for k in range(KT - 1)] + [(o, KT - 1) for o in range(OPEN)]
O2_TILES += [(o, k) for o in range(OPEN, KT) for k in range(KT)]
O2_EARLY = OPEN * (KT - 1)


def where(cols):
    a, b = cols
    off = BANK - SPLIT
    return [(a, SPLIT, a + off, BANK), (SPLIT, b, BANK, b + off)], slice(a + off, b + off)


def part(cols, half=None):
    return where(cols)[0] if half is None else [where(cols)[0][half]]


def block_part(cols, half=None):
    if cols[1] - cols[0] > BANK:
        return part(cols, half)
    mid = BANK + SPLIT - cols[0]
    return [[(*cols, BANK, 2 * BANK)], [(cols[0], SPLIT, BANK, mid)], [(SPLIT, cols[1], mid, 2 * BANK)]][
        0 if half is None else half + 1]


def block_slice(cols):
    p = block_part(cols)
    return slice(p[0][2], p[-1][3])


def tokens(cols, half=None, off=0):
    p = part(cols, half)
    return slice(p[0][0] - off, p[-1][1] - off)


def x_base(fill):
    return 0 if fill == 0 else KT + 2 * KT * (fill - 1)


def sq_base(s):
    return x_base(s // 2)


def stat_count(s, half=None):
    return 1 if s == 0 else 2 * s + (half or 0)


POST_SQ, POST_ADD = KT + 2, KT


def program(nc, xT, vecs, consts, mats, weights, out):
    NBLK = weights.shape[0]
    with ExitStack() as whole:
        def sb(name, shape, dt=F32, ctx=whole):
            return ctx.enter_context(nc.sbuf_tensor(name, shape, dt))

        def sem(name):
            return whole.enter_context(nc.semaphore(name))

        hres = sb("hres", [P, KT, TOK])
        vec = sb("vec", [P, V_END])
        con = sb("con", [P, C_END])
        raw = sb("raw", [P, 4, D])
        whi = sb("whi", [P, 2, D], F32R)
        wlo = sb("wlo", [P, 2, D], F32R)
        sq = sb("sq", [P, 2, TOK])
        acc = sb("acc", [P, TOK])
        rms = sb("rms", [P, TOK])
        rstd = sb("rstd", [P, 2, TOK])
        t1 = sb("t1", [P, 2, TOK])
        eps_t = sb("eps_t", [P, 2])
        warm = sb("warm", [P, 1])
        mat = sb("mat", [P, 2 * SEQ])
        first = ExitStack()
        xh = sb("xh", [P, KT, TOK], F32R, first)
        xl = sb("xl", [P, KT, TOK], F32R, first)
        NW = NEED[1] - NEED[0]
        ah = [sb("ah0", [P, KT, NW], F32R, first)]
        al = [sb("al0", [P, KT, NW], F32R, first)]
        with ExitStack() as attn:
            qT, kT, vT = (sb(n, [P, 2, TOK], F32, attn) for n in ("qT", "kT", "vT"))
            o_all = sb("o_all", [P, 2, 5, P], F32, attn)
            biasT = sb("biasT", [P, 2, TOK], F32, attn)
            negs = sb("negs", [P, 2, 2, TOK], F32, attn)
            prob = sb("prob", [P, 2, 2, TOK], F32, attn)
            aT = sb("aT", [P, 2, 5, P], F32, attn)
            vtok = sb("vtok", [P, 2, 5, P], F32, attn)
            o_sc = sb("o_sc", [P, 2, 5, P], F32, attn)
            o_sq = sb("o_sq", [P, P], F32, attn)
            nmax = sb("nmax", [P, 2, 40], F32, attn)
            den = sb("den", [P, 2, 40], F32, attn)
            rden = sb("rden", [P, 2, 40], F32, attn)
            coef = sb("coef", [P, 40], F32, attn)
            oss = sb("oss", [P, 40], F32, attn)
            orms = sb("orms", [P, 40], F32, attn)
            orstd = sb("orstd", [P, 40], F32, attn)
            lamt = sb("lamt", [P, 2, 64], F32, attn)
            lamd = sb("lamd", [P, 8], F32, attn)
            gsub = sb("gsub", [P, 1], F32, attn)
        with ExitStack() as mlp:
            ah.append(sb("ah1", [P, KT, NW], F32R, mlp))
            al.append(sb("al1", [P, KT, NW], F32R, mlp))
            m = sb("m", [P, KT, NW], F32, mlp)
            act2 = sb("act2", [P, 2, NW], F32, mlp)
            cb = sb("cb", [P, 3, NW], F32, mlp)
        first.close()
        with ExitStack() as tri:
            def mats_of(name, *shape):
                return sb(name, [P, *(shape or (NCH, CH))], F32, tri)

            def chain_mats(i):
                return [[mats_of(f"{n}{i}{x}") for x in range(2)] for n in ("MR", "BKt", "UV")]
            DL = [mats_of(f"DL{x}") for x in range(2)]
            ET = mats_of("ET", NCH, 2 * CH)
            Dm, Ya, Yb, D4m = (mats_of(n) for n in ("Dm", "Ya", "Yb", "D4m"))
            PB2 = mats_of("PB2", 2, 2, 4, CH)
            first_mats = chain_mats(0)
            sb("tri_pad", [P, 2 * KT * TOK - 16 * SEQ], F32, tri)
            MR, BKt, UV = zip(first_mats, chain_mats(1))
        second = ExitStack()
        x2h = sb("x2h", [P, KT, TOK], F32R, second)
        x2l = sb("x2l", [P, KT, TOK], F32R, second)
        sg, av, cs, Gp, Gt, Gi, kn, k2 = (sb(n, [P, SEQ], F32, second)
                                          for n in ("sg", "av", "cs", "Gp", "Gt", "Gi", "kn", "k2"))
        tw = sb("tw", [HD, SEQ], F32, second)
        z = sb("z", [P, 13, 1 + SEQ], F32, second)
        zu = sb("zu", [P, 4, PAD + SEQ], F32, second)
        gate = sb("gate", [P, 8, SEQ], F32, second)
        BK = sb("BK", [P, PAIRS, NCH, 2, CH], F32, second)
        bonus = sb("bonus", [P, PAIRS, SEQ], F32, second)
        g_end = sb("g_end", [P, PAIRS, NCH], F32, second)
        Sg = sb("Sg", [P, CH], F32, second)
        BD = sb("BD", [P, NCH, 2 * CH], F32, second)
        second.close()
        at_ = sq.rearrange("p a t -> p (a t)")[:, 0:2 * SEQ].rearrange("p (c t) -> p c t", t=2 * CH)
        Wm = rstd[:, 1, 0:SEQ].rearrange("p (c t) -> p c t", t=CH)
        gn_y, gn_sd, gn_c = acc[:, 0:SEQ], rms[:, 0:SEQ], rstd[:, 0, 0:SEQ]

        G = [whole.enter_context(nc.psum_tensor(f"G{i}", [P, 2 * BANK], F32)) for i in range(2)]
        ST = whole.enter_context(nc.psum_tensor("ST", [P, 2 * BANK], F32))
        PO = whole.enter_context(nc.psum_tensor("PO", [P, BANK], F32))
        PV = whole.enter_context(nc.psum_tensor("PV", [P, BANK], F32))

        vec_loaded = sem("vec_loaded"); con_loaded = sem("con_loaded")
        con2_loaded = sem("con2_loaded"); mat_loaded = sem("mat_loaded")
        h_loaded = [sem(f"h_loaded{k}") for k in range(KT)]
        w_loaded = [sem(f"w_loaded{i}") for i in range(4)]
        hi_ready = sem("hi_ready"); lo_ready = sem("lo_ready")
        block_done = sem("block_done"); tile_out = sem("tile_out")
        x_hi = sem("x_hi"); x_ready = sem("x_ready")
        a_hi = sem("a_hi"); a_ready = sem("a_ready")
        sq_ready = sem("sq_ready"); sq_used = sem("sq_used")
        psq_ready = sem("psq_ready"); psq_added = sem("psq_added"); post_sum = sem("post_sum")
        rms_ready = sem("rms_ready"); rstd_ready = sem("rstd_ready")
        t1_ready = sem("t1_ready"); h_ready = sem("h_ready")
        half_done = sem("half_done"); half_out = sem("half_out")
        sqr_ready = sem("sqr_ready")
        lam_prod = sem("lam_prod"); lam_exp = sem("lam_exp"); lam_ready = sem("lam_ready")
        oss_set = sem("oss_set")
        bias_ready = sem("bias_ready")
        scores_ready = sem("scores_ready"); negs_ready = sem("negs_ready"); prob_ready = sem("prob_ready")
        coef_step = sem("coef_step"); a_done = sem("a_done")
        at_ready = sem("at_ready"); at_copied = sem("at_copied")
        v_turned = sem("v_turned"); v_copied = sem("v_copied")
        o_ready = sem("o_ready"); o_copied = sem("o_copied"); oss_ready = sem("oss_ready")
        orms_ready = sem("orms_ready"); orstd_ready = sem("orstd_ready")
        osc_ready = sem("osc_ready"); ot_ready = sem("ot_ready")
        conv_step = sem("conv_step")
        stored = sem("stored")
        sems = {}

        def S(name):
            if name not in sems:
                sems[name] = sem(name)
            return sems[name]

        def bank(n):
            return (G[0][:, 0:BANK], G[0][:, BANK:], G[1][:, 0:BANK], G[1][:, BANK:], ST[:, 0:BANK], ST[:, BANK:],
                    PO[:], PV[:])[n]

        def chunks(ap):
            return ap.rearrange("p (c t) -> p c t", t=CH)

        def own(x):
            return slice(CH * x, CH * x + CH)

        def col(v, p):
            return vec[:, v + p:v + p + 1]

        HALF = [slice(0, 4), slice(4, 8)]
        ROW = [slice(0, HD), slice(HD, P)]
        B_IN2, B_O2 = 192, 217

        ident = con[:, C_IDENT:C_IDENT + P]
        ones = con[:, C_ONES:C_ONES + P]

        def gain(layer, n, k):
            if layer == 2:
                return col(V_N2, k)
            c = V_NORM + (layer * 4 + n) * KT + k
            return vec[:, c:c + 1]

        B_QKV, B_AO = 0, 24
        B_MLP = [32, 128]
        B_CI, B_CO = 96, 120
        UP = [0, 8, 24, 40]
        DOWN = [16, 32, 48, 56]

        def blocks(eng, b0, n, body):
            lead = 4 if b0 == 0 else 0
            for j in range(lead):
                body(b0 + j, j, (b0 + j) % 4)
            if n - lead >= 8:
                with eng.Fori(0, (n - lead) // 4) as i:
                    for u in range(4):
                        body(i * 4 + (b0 + lead + u), i * 4 + (lead + u), (b0 + u) % 4)
                lead += (n - lead) // 4 * 4
            for j in range(lead, n):
                body(b0 + j, j, (b0 + j) % 4)

        def tile(buf, j, cols):
            if isinstance(j, int):
                return buf[:, j, cols]
            return buf[:, bass.ds(j, 1), cols]

        def queries(i):
            return (0, META) if i == 0 else (META + P * (i - 1), P)

        def keys(i):
            return [(0, META)] + [(META + P * j, P) for j in range(i)]

        def span(i):
            return META + P * i
        S0 = BANK - META

        TURNS = 3 * HEADS + 4

        def tiles(s):
            h, r = s // 3 - 1, s % 3
            if not 0 <= h < HEADS:
                return []
            return [5 * h + i for i in ((0, 1), (2, 3), (4,))[r]]

        def qkv_acc(s):
            return G[s % 2 if s < 3 else 0]

        def meta_bank(i):
            return (PV, P) if i == 4 else (PO, 3 * P)

        def turned_head(s):
            h = HEADS - 1 if s == TURNS - 1 else (s - 8) // 3
            return h if (s % 3 == 2 and 0 <= h < HEADS - 1) or s == TURNS - 1 else None

        Z_SLOT = [0] + [i + p for p in range(PAIRS) for i in (1, 5, 9)]

        def feature_step(j):
            p, i = divmod(j - 2, 5)
            return (p, i) if j >= 2 and p < PAIRS else (None, None)

        START = [("gram", 0), ("gram", 1), ("lm", 0), ("lm", 1)]
        SYSTEM = [("gram", 2), ("gram", 3), ("rv", 0), ("D2", 0), ("D2", 1), ("bk", 0), ("D4", 0), ("y2", 0), ("D4", 1),
                  ("y2", 1), ("at", 0), ("D8", 0), ("y3", 0), ("D8", 1), ("y3", 1), ("y4", 0), ("y4", 1), ("w", 0),
                  ("td", 0), ("td", 1), ("bk", 1)]
        SYSTEM += [(n, g) for n in ("ht", "z1", "z2", "z3") for g in range(2)] + [("q", 0), ("pt", 0)]
        UNDER = {("z2", 1): START[:1], ("z3", 1): START[1:2], ("q", 0): START[2:]}
        CHAIN = [("u", 0)] + [(n, c + d) for c in range(NCH - 1) for n, d in (("s", 0), ("u", 1))]
        TAIL = CHAIN + [("y", 0), ("y", 1), ("mu", 0), ("sq", 0), ("var", 0), ("sd", 0)] + [("norm", i) for i in range(7)]
        JOIN = {"u": 5, "s": 5, "mix": 20, "y": 19}

        def woven():
            steps = [(system_, 0, *t) for t in START]
            other = [(mix_, g, "mix", 0) for g in range(4)]
            for p in range(PAIRS):
                for i, t in enumerate(SYSTEM):
                    steps.append((system_, p, *t))
                    if p + 1 < PAIRS:
                        steps += [(system_, p + 1, *n) for n in UNDER.get(t, ())]
                    if other and (other[0][1] < p - 1 or i >= JOIN.get(other[0][2], 0)):
                        steps.append(other.pop(0))
                other += [(tail_, p, *t) for t in TAIL]
            ends, n = [], 0
            for i, t in enumerate(other):
                ends.append(t)
                more = min(n + (1 if i < KT - 1 else 2), O2_EARLY)
                ends += [(out_, j, "out", 0) for j in range(n, more)]
                n = more
            return steps, ends + [(out_, j, "out", 0) for j in range(n, O2_EARLY)]

        system_, tail_, mix_, out_ = range(4)
        STEPS, ENDS = woven()

        def alpha(p, x, c):
            return z[ROW[x], 1 + p, 1 + CH * c:1 + CH * c + CH]

        def rcv(p, x, c):
            return z[ROW[x], 5 + p, 1 + CH * c:1 + CH * c + CH]

        def state(p, c):
            return z[:, 9 + p, 1 + CH * c:1 + CH * c + CH]

        block = whole.enter_context(nc.Block())

        @block.sync
        def _(sp):
            def load_rows(k):
                sp.dma_start(hres[:, k], xT[k * P:(k + 1) * P, :]).then_inc(h_loaded[k], 16)

            def load_first(b):
                sp.dma_start(raw[:, b], weights[b]).then_inc(w_loaded[b], 16)

            sp.dma_start(vec[:], vecs).then_inc(vec_loaded, 16)
            load_first(0)
            load_rows(0)
            load_rows(1)
            sp.dma_start(con[:, 0:C_BLK], consts[:, 0:C_BLK]).then_inc(con_loaded, 16)
            for k in range(2, 5):
                load_rows(k)
            load_first(1)
            for k in range(5, KT):
                load_rows(k)
            load_first(2)
            load_first(3)
            sp.dma_start(con[:, C_BLK:], consts[:, C_BLK:]).then_inc(con2_loaded, 16)
            sp.dma_start(mat[:], mats).then_inc(mat_loaded, 16)

            def load(b, j, s):
                if isinstance(b, int) and b < 4:
                    return
                sp.wait_ge(lo_ready, b - 3)
                src = weights[b] if isinstance(b, int) else weights[bass.ds(b, 1)].rearrange("b p n -> p (b n)")
                sp.dma_start(raw[:, s], src).then_inc(w_loaded[s], 16)
            blocks(sp, 0, NBLK, load)
            for k in range(KT):
                sp.wait_ge(S("out_ready"), k + 1)
                sp.dma_start(out[k * P:(k + 1) * P, :], hres[:, k, META:]).then_inc(stored, 16)
            sp.wait_ge(stored, 16 * KT)

        @block.gpsimd
        def _(pool):
            def low(b, j, s):
                pool.wait_ge(hi_ready, b + 1)
                if not isinstance(b, int) or b >= 2:
                    pool.wait_ge(block_done, b - 1)
                nc.gpsimd.tensor_tensor(wlo[:, s % 2], raw[:, s], whi[:, s % 2].bitcast(F32), ALU.subtract)\
                    .then_inc(lo_ready, 1)
            def residual(i, half, cols):
                for k in range(KT):
                    n = 2 * KT * i + KT * half + k + 1
                    pool.wait_ge(t1_ready, n)
                    c = tokens(cols, half)
                    nc.gpsimd.tensor_tensor(hres[:, k, c], hres[:, k, c], t1[:, k % 2, tokens(cols, half, cols[0])], ALU.add)\
                        .then_inc(h_ready, 1)

            done = 0
            for i, (b, cols) in enumerate(((B_MLP[0], NEED), (B_CI, NEED), (B_MLP[1], OUT), (B_IN2, OUT))):
                blocks(pool, done, b + 1 - done, low)
                residual(i, 0, cols)
                low(b + 1, 1, (b + 1) % 4)
                residual(i, 1, cols)
                done = b + 2
            blocks(pool, done, B_O2 + 2 - done, low)

            pool.wait_ge(tile_out, B_IN2 + 17)
            pool.wait_ge(S("BK_ready"), 4 * PAIRS)
            pool.wait_ge(S("pads_set"), 3)
            pool.wait_ge(con2_loaded, 16)
            n = 0
            for g, w in enumerate(POOL_W):
                src = zu[:, g]
                for i in range(g + 1):
                    dst = t1[:, i % 2]
                    sh = 1 << i
                    if n:
                        pool.wait_ge(S("pool_step"), n)
                    nc.gpsimd.tensor_tensor(dst[:, PAD:], src[:, PAD:], src[:, PAD - sh:PAD + SEQ - sh], ALU.add)\
                        .then_inc(S("pool_step"), 1)
                    src = dst
                    n += 1
                mean = (Gt, Gi, cs, Gp)[g]
                fix = con[:, C_PFIX + 16 * g:C_PFIX + 16 * g + 16]
                pool.wait_ge(S("pool_step"), n)
                nc.gpsimd.tensor_tensor(src[:, PAD:PAD + 16], src[:, PAD:PAD + 16], fix, ALU.mult)\
                    .then_inc(S("pool_step"), 1)
                pool.wait_ge(S("pool_step"), n + 1)
                nc.gpsimd.tensor_scalar(mean[:], src[:, PAD:], 1.0 / w, None, ALU.mult).then_inc(S("pool_step"), 1)
                pool.wait_ge(S("pool_step"), n + 2)
                nc.gpsimd.tensor_tensor(mean[:], mean[:], zu[:, g, PAD:], ALU.subtract).then_inc(S("pooled"), 1)
                n += 2
            blocks(pool, B_O2 + 2, KT - 2, low)

        @block.scalar
        def _(act):
            def split(b, s):
                if isinstance(b, int):
                    if b >= NBLK:
                        return
                    act.wait_ge(w_loaded[s], 16 * (b // 4 + 1))
                    if b >= 2:
                        act.wait_ge(block_done, b - 1)
                nc.scalar.activation(whi[:, s % 2], raw[:, s], ACT.Copy).then_inc(hi_ready, 1)

            def step(b0, n, evac=None):
                def body(b, j, s):
                    if isinstance(b, int):
                        split(b + 2, (s + 2) % 4)
                    else:
                        i4 = b - s
                        s2 = (s + 2) % 4
                        act.wait_ge(w_loaded[s2], (i4 + 4 * ((s + 2) // 4)) * 4 + 16)
                        act.wait_ge(block_done, b + 1)
                        nc.scalar.activation(whi[:, s2 % 2], raw[:, s2], ACT.Copy).then_inc(hi_ready, 1)
                    if evac:
                        evac(b, j, s)
                blocks(act, b0, n, body)

            def stat_root(s, cols, half=None):
                if s % 2 == 0:
                    act.wait_ge(sq_used, sq_base(s) + KT * ((half or 0) + 1))
                else:
                    act.wait_ge(post_sum, s + (half or 0))
                if s >= 1:
                    act.wait_ge(rstd_ready, stat_count(s - 1, 1 if s == 9 else half))
                pieces = part(cols, half)
                nc.scalar.activation(rms[:, tokens(cols, half)], ST[:, pieces[0][2]:pieces[-1][3]], ACT.Sqrt, scale=1.0 / D,
                                     bias=eps_t[:, 0:1]).then_inc(rms_ready, 1)

            def prenorm(i, layer, n, cols):
                s = 2 * i + 2
                for half in range(2):
                    c = tokens(cols, half)
                    for k in range(KT):
                        act.wait_ge(h_ready, 2 * KT * i + KT * half + k + 1)
                        nc.scalar.activation((x2h if layer == 2 else xh)[:, k, c], hres[:, k, c], ACT.Copy,
                                             scale=gain(layer, n, k)).then_inc(x_hi, 1)
                        if k >= 2:
                            act.wait_ge(sq_used, sq_base(s) + KT * half + k - 1)
                        nc.scalar.activation(sq[:, k % 2, tokens(cols, half, cols[0])], hres[:, k, c], ACT.Square)\
                            .then_inc(sq_ready, 1)
                        if half == 0 and k == 1:
                            stat_root(s - 1, cols, 1)
                    stat_root(s, cols, half)

            def post_squares(b0, i, cols):
                w = cols[1] - cols[0]
                for j in range(KT - 2):
                    split(b0 + j + 2, (b0 + j + 2) % 4)
                    act.wait_ge(tile_out, b0 + j + 1)
                    if j >= 2:
                        act.wait_ge(psq_added, POST_ADD * i + j - 1)
                    nc.scalar.activation(sq[:, j % 2, 0:w], m[:, j, 0:w], ACT.Square).then_inc(psq_ready, 1)
                for half in range(2):
                    c = tokens(cols, half, cols[0])
                    for j in (KT - 2, KT - 1):
                        if half:
                            split(b0 + j + 2, (b0 + j + 2) % 4)
                            act.wait_ge(tile_out, b0 + j + 1)
                        else:
                            act.wait_ge(half_out, 2 * i + j - (KT - 2) + 1)
                            act.wait_ge(psq_added, POST_ADD * i + j - 1)
                        nc.scalar.activation(sq[:, j % 2, c], m[:, j, c], ACT.Square).then_inc(psq_ready, 1)
                    if half == 0:
                        stat_root(2 * i + 1, cols, 0)

            def mlp(layer, cols, i):
                b0 = B_MLP[layer]
                w = cols[1] - cols[0]
                for c in range(FF_CHUNKS + 1):
                    if c < FF_CHUNKS:
                        f = 5 * layer + c + 1

                        def up(b, j, s4):
                            act.wait_ge(tile_out, b + 1)
                            nc.scalar.activation(tile(ah[f % 2], j, slice(0, w)), t1[:, s4 % 2, 0:w], ACT.Square)\
                                .then_inc(a_hi, 1)
                            act.wait_ge(a_ready, j + (8 * f - 1))
                            nc.scalar.activation(act2[:, s4 % 2, 0:w], t1[:, s4 % 2, 0:w], ACT.Square)\
                                .then_inc(sqr_ready, 1)
                        step(b0 + UP[c], 8, up)
                    if c >= 1 and c < FF_CHUNKS:
                        step(b0 + DOWN[c - 1], 8)
                    elif c == FF_CHUNKS:
                        post_squares(b0 + DOWN[c - 1], i, cols)

            act.wait_ge(oss_set, 3)
            nc.scalar.activation(warm[:], eps_t[:, 0:1], ACT.Square)
            act.wait_ge(vec_loaded, 16)
            split(0, 0)
            for k in range(KT):
                act.wait_ge(h_loaded[k], 16)
                if k == 4:
                    split(1, 1)
                nc.scalar.activation(xh[:, k], hres[:, k], ACT.Copy, scale=gain(0, 0, k)).then_inc(x_hi, 1)
                if k >= 2:
                    act.wait_ge(sq_used, k - 1)
                nc.scalar.activation(sq[:, k % 2], hres[:, k], ACT.Square).then_inc(sq_ready, 1)
            stat_root(0, ALL)
            act.wait_ge(con_loaded, 16)
            act.wait_ge(lam_prod, 2)
            nc.scalar.activation(lamd[:, 2:4], lamd[:, 0:2], ACT.Exp).then_inc(lam_exp, 1)

            def turned_weights(t):
                i = t % 5
                rows = queries(i)[1]
                act.wait_ge(at_ready, t + 1)
                if t >= 2:
                    act.wait_ge(o_ready, t - 1)
                if i > 0:
                    nc.scalar.activation(aT[:, t % 2, 1:1 + i, :], PO[:, 0:P * i].rearrange("p (j v) -> p j v", v=P), ACT.Copy)
                mb, m0 = meta_bank(i)
                nc.scalar.activation(aT[0:META, t % 2, 0, 0:rows], mb[0:META, m0:m0 + rows], ACT.Copy).then_inc(at_copied, 1)

            def attended(t):
                h, i = divmod(t, 5)
                rows = queries(i)[1]
                act.wait_ge(o_ready, t + 1)
                if h >= 2:
                    act.wait_ge(osc_ready, 5 * (h - 1))
                nc.scalar.activation(o_all[0:rows, h % 2, i, :], PV[0:rows, 0:P], ACT.Copy, scale=rden[0:rows, 0, t:t + 1])\
                    .then_inc(o_copied, 1)
                act.wait_ge(o_copied, t + 1)
                if t >= 1:
                    act.wait_ge(oss_ready, t)
                nc.scalar.activation(o_sq[0:rows, :], o_all[0:rows, h % 2, i, :], ACT.Square, accum_out=oss[0:rows, t:t + 1])\
                    .then_inc(oss_ready, 1)

            def exponentials(n):
                rows, w = queries(n % 5)[1], span(n % 5)
                for c in range(2):
                    act.wait_ge(negs_ready, 2 * n + c + 1)
                    if n >= 2:
                        act.wait_ge(at_ready, n - 1)
                    nc.scalar.activation(prob[0:rows, n % 2, c, 0:w], negs[0:rows, n % 2, c, 0:w], ACT.Exp, scale=-1.0,
                                         bias=nmax[0:rows, c, n:n + 1], accum_out=den[0:rows, c, n:n + 1])\
                        .then_inc(prob_ready, 1)

            def head_high(h):
                act.wait_ge(ot_ready, h + 1)
                nc.scalar.activation(ah[0][:, h, :], ST[:, where(NEED)[1]], ACT.Copy, scale=gsub[:, 0:1]).then_inc(a_hi, 1)

            for s in range(TURNS):
                prev, cur = tiles(s - 1), tiles(s)
                if cur and s % 3 == 0:
                    h = s // 3 - 1
                    act.wait_ge(v_turned, h + 1)
                    if h >= 2:
                        act.wait_ge(o_ready, 5 * (h - 1))
                    nc.scalar.activation(vtok[:, h % 2, 1:5, :], G[1][:, BANK:].rearrange("p (j v) -> p j v", v=P), ACT.Copy)\
                        .then_inc(v_copied, 1)
                    nc.scalar.activation(vtok[0:META, h % 2, 0, :], G[1][0:META, 0:P], ACT.Copy).then_inc(v_copied, 1)
                if s % 3 == 2 and turned_head(s) is not None:
                    head_high(turned_head(s))
                if s % 3 == 0:
                    for n in cur[:1]:
                        exponentials(n)
                    for t in prev:
                        turned_weights(t)
                    for n in cur[1:]:
                        exponentials(n)
                else:
                    for k, t in enumerate(prev):
                        turned_weights(t)
                        if k < len(cur):
                            exponentials(cur[k])
                        if s % 3 == 1 or k == 0:
                            attended(t)
                if s % 3 == 1 and not prev:
                    for n in cur:
                        exponentials(n)
                if s < 24:
                    split(s + 2, (s + 2) % 4)
                if s % 3 == 0:
                    for t in prev:
                        attended(t)
                elif s % 3 == 2 and prev:
                    attended(prev[1])
                if s % 3 == 2 and s < 24:
                    h = s // 3
                    if h >= 2:
                        act.wait_ge(negs_ready, 10 * (h - 1))
                    slope = 2.0 ** (-8.0 * (h + 1) / HEADS)
                    nc.scalar.activation(biasT[:, h % 2], con[:, C_DIST:C_DIST + TOK], ACT.Copy, scale=slope)\
                        .then_inc(bias_ready, 1)
                if prev and prev[-1] % 5 == 4:
                    h = prev[-1] // 5
                    act.wait_ge(oss_ready, 5 * (h + 1))
                    hs = slice(5 * h, 5 * h + 5)
                    nc.scalar.activation(orms[:, hs], oss[:, hs], ACT.Sqrt, scale=1.0 / P, bias=eps_t[:, 0:1])\
                        .then_inc(orms_ready, 1)
            head_high(HEADS - 1)

            post_squares(B_AO, 0, NEED)
            prenorm(0, 0, 2, NEED)
            mlp(0, NEED, 1)
            prenorm(1, 1, 0, NEED)

            for j in range(KT):
                for r in range(3):
                    b = B_CI + 3 * j + r
                    split(b + 2, (b + 2) % 4)
                act.wait_ge(conv_step, 5 * j + 5)
                nc.scalar.activation(ah[1][:, j, 0:SEQ], m[:, j, 2:2 + SEQ], ACT.Copy).then_inc(a_hi, 1)
            post_squares(B_CO, 2, OUT)
            prenorm(2, 1, 2, OUT)
            mlp(1, OUT, 3)
            prenorm(3, 2, 0, OUT)

            for j in range(25):
                split(B_IN2 + j + 2, (B_IN2 + j + 2) % 4)
                p, i = feature_step(j)
                if j == 1:
                    act.wait_ge(S("shifted"), 1)
                    nc.scalar.activation(tw[:], z[0:HD, 0, 1:], ACT.Tanh).then_inc(S("tanh_ready"), 1)
                if i == 0:
                    act.wait_ge(S("ww_ready"), p + 1)
                    if p:
                        act.wait_ge(S("BK_ready"), 4 * p)
                    nc.scalar.activation(sg[:], bank(4), ACT.Sigmoid, bias=col(V_W0, p)).then_inc(S("sg_ready"), 1)
                    act.wait_ge(S("aa_ready"), p + 1)
                    nc.scalar.activation(av[:], bank(5), ACT.Sigmoid, bias=col(V_A0, p)).then_inc(S("av_ready"), 1)
                    act.wait_ge(S("shifted"), 3 * p + 2)
                    nc.scalar.activation(kn[:], z[:, 1 + p, 1:], ACT.Square, scale=col(V_KK, p)).then_inc(S("ksq_ready"), 1)
                if i == 1:
                    act.wait_ge(S("knorm_sum"), p + 1)
                    nc.scalar.activation(kn[:], bank(6), ACT.Sqrt).then_inc(S("kn_ready"), 1)
                    act.wait_ge(S("cp_ready"), p + 1)
                    nc.scalar.activation(Gt[:], cs[:], ACT.Exp, scale=-DECAY).then_inc(S("Gt_ready"), 1)
                    nc.scalar.activation(Gi[:], cs[:], ACT.Exp, scale=DECAY).then_inc(S("Gi_ready"), 1)
                    nc.scalar.activation(Gp[:], Gp[:], ACT.Exp, scale=-DECAY).then_inc(S("Gp_ready"), 1)
                for n in {20: range(4), 21: (4,), 22: (5,), 23: (6,), 24: (7,)}.get(j, ()):
                    act.wait_ge(tile_out, B_IN2 + 18 + n)
                    nc.scalar.activation(gate[:, n], gate[:, n], ACT.Silu).then_inc(S("gate_ready"), 1)

            def copy_out(need, n, done, dst, src):
                act.wait_ge(S(need), n)
                nc.scalar.activation(dst, src, ACT.Copy).then_inc(S(done), 1)

            def to_diagonal(need, n, done, dst, half, src):
                act.wait_ge(S(need), n)
                if need == "at_turned" and n == 1:
                    act.wait_ge(S("zeroed"), 3)
                nc.scalar.activation(dst[ROW[0], half, own(0)], src[ROW[0]], ACT.Copy)
                nc.scalar.activation(dst[ROW[1], half, own(1)], src[ROW[1]], ACT.Copy).then_inc(S(done), 1)

            def system(p, name, g):
                n2 = 2 * p + g + 1
                if name == "rv":
                    act.wait_ge(S("rv_turned"), p + 1)
                    for x in range(2):
                        nc.scalar.activation(UV[p % 2][x][ROW[1 - x]], chunks(bank(0))[ROW[1 - x]], ACT.Copy)\
                            .then_inc(S("vt_out"), 1)
                elif name == "at":
                    to_diagonal("at_turned", p + 1, "at_out", at_, slice(0, NCH), chunks(bank(1)))
                elif name == "D2":
                    copy_out("d2_ready", n2, "d2_out", PB2[:, g].rearrange("p k c t -> p (k c t)"), bank(2 + g))
                elif name == "bk":
                    copy_out("bk_turned", n2, "bk_out", BKt[p % 2][g][:], chunks(bank(g)))
                elif name == "w":
                    copy_out("w_ready", p + 1, "w_out", Wm, chunks(bank(0)))
                elif name == "D4":
                    act.wait_ge(S("d4_ready"), n2)
                    nc.scalar.activation(D4m[:, HALF[g]], chunks(bank(2 + g)[:, 0:4 * CH]), ACT.Copy)
                    to_diagonal("d4_ready", n2, "d4_out", BD, HALF[g], chunks(bank(2 + g)[:, 4 * CH:]))
                elif name == "D8":
                    to_diagonal("d8_ready", n2, "d8_out", BD, HALF[g], chunks(bank(2 + g)[:, 0:4 * CH]))
                elif name == "td":
                    copy_out("td_ready", n2, "td_out", PB2[:, g, 0], chunks(bank(4 + g)[:, 0:4 * CH]))
                elif name == "ht":
                    to_diagonal("ht_ready", n2, "ht_out", BD, HALF[g], chunks(bank(4 + g)[:, 0:4 * CH]))
                elif name == "q":
                    copy_out("q_ready", p + 1, "q_out", BK[:, p, :, 0, :], chunks(bank(0)))
                elif name == "pt":
                    copy_out("pt_ready", p + 1, "pt_out", BK[:, p, :, 1, :], chunks(bank(1)))

            def tail(p, name, c):
                if name == "y" and c == 1:
                    copy_out("y_ready", p + 1, "yt_out", gn_y, bank(7))
                elif name == "sq":
                    act.wait_ge(S("yc_ready"), p + 1)
                    nc.scalar.activation(gn_sd, gn_c, ACT.Square).then_inc(S("ysq_ready"), 1)
                elif name == "sd":
                    act.wait_ge(S("var_ready"), p + 1)
                    nc.scalar.activation(gn_sd, bank(7), ACT.Sqrt, scale=1.0 / HD, bias=eps_t[:, 1:2])\
                        .then_inc(S("sd_ready"), 1)

            def last_high(k):
                if k < 4:
                    act.wait_ge(S("ya_ready"), k + 1)
                else:
                    act.wait_ge(S("yb_ready"), k - 3)
                src = zu[:, k, PAD:] if k < 4 else z[:, 1 + k, 1:]
                nc.scalar.activation(x2h[:, k, META:], src, ACT.Copy).then_inc(x_hi, 1)

            for steps in (STEPS, ENDS):
                if steps is ENDS:
                    for k in range(KT - 1):
                        last_high(k)
                for kind, n, name, g in steps:
                    if kind == system_:
                        system(n, name, g)
                    elif kind == tail_:
                        tail(n, name, g)
                    elif kind == out_ and n % KT == KT - 1:
                        b = B_O2 + n // KT + 2
                        split(b, b % 4)
            last_high(KT - 1)
            for j in range(KT):
                if j == 3:
                    split(NBLK - 1, (NBLK - 1) % 4)
                act.wait_ge(tile_out, B_O2 + j + 1)
                if j >= 2:
                    act.wait_ge(psq_added, POST_ADD * 4 + j - 1)
                nc.scalar.activation(sq[:, j % 2, 0:SEQ], hres[:, j, META:], ACT.Square).then_inc(psq_ready, 1)
            stat_root(9, OUT)

        @block.vector
        def _(dve):
            def stat_recip(s, cols, half=None):
                c = tokens(cols, half)
                dve.wait_ge(rms_ready, stat_count(s, half))
                nc.vector.reciprocal(rstd[:, s % 2, c], rms[:, c]).then_inc(rstd_ready, 1)

            def low_x(f, layer, n, k, cols, half=None):
                c = tokens(cols, half)
                dve.wait_ge(x_hi, x_base(f) + KT * (half or 0) + k + 1)
                hi, lo = (x2h, x2l) if layer == 2 else (xh, xl)
                nc.vector.scalar_tensor_tensor(lo[:, k, c], hres[:, k, c], gain(layer, n, k), hi[:, k, c].bitcast(F32),
                                               ALU.mult, ALU.subtract).then_inc(x_ready, 1)

            def add_square(i, j, cols, half=None):
                c = tokens(cols, half, cols[0])
                dve.wait_ge(psq_ready, POST_SQ * i + j + 1 + 2 * (half or 0))
                if j == 0:
                    nc.vector.tensor_copy(acc[:, c], sq[:, 0, c]).then_inc(psq_added, 1)
                else:
                    dve.wait_ge(psq_added, POST_ADD * i + j + (half or 0))
                    nc.vector.tensor_tensor(acc[:, c], acc[:, c], sq[:, j % 2, c], ALU.add).then_inc(psq_added, 1)

            def tile_to_m(j, acc_of, c, pos, before, count):
                mt = tile(m, j, c)
                if before is None:
                    nc.vector.tensor_copy(mt, acc_of[:, pos]).then_inc(count, 1)
                else:
                    dve.wait_ge(tile_out, j + (before + 1))
                    nc.vector.tensor_tensor(mt, acc_of[:, pos], mt, ALU.add).then_inc(count, 1)

            def out_tiles(b0, cols, before):
                def body(b, j, s):
                    dve.wait_ge(block_done, b + 1)
                    tile_to_m(j, G[s % 2], slice(0, cols[1] - cols[0]), block_slice(cols), before, tile_out)
                blocks(dve, b0, 8, body)

            def last_tiles(i, b0, cols, before, norm, pre):
                s = 2 * i + 1

                def half_tile(j, half):
                    _, _, p0, p1 = part(cols, half)[0]
                    if half:
                        dve.wait_ge(block_done, b0 + j + 1)
                    else:
                        dve.wait_ge(half_done, 2 * i + j - (KT - 2) + 1)
                    tile_to_m(j, G[j % 2], tokens(cols, half, cols[0]), slice(p0, p1), before, tile_out if half else half_out)

                for j in range(KT - 2):
                    dve.wait_ge(block_done, b0 + j + 1)
                    tile_to_m(j, G[j % 2], slice(0, cols[1] - cols[0]), block_slice(cols), before, tile_out)
                    if j >= 1:
                        add_square(i, j - 1, cols)
                half_tile(KT - 2, 0)
                add_square(i, KT - 3, cols)
                half_tile(KT - 1, 0)
                add_square(i, KT - 2, cols, 0)
                for half in range(2):
                    stat_recip(s, cols, half)
                    dve.wait_ge(rstd_ready, stat_count(s, half))
                    o = tokens(cols, half, cols[0])
                    for k in range(KT + 2):
                        if k < KT:
                            if k >= 2:
                                dve.wait_ge(h_ready, 2 * KT * i + KT * half + k - 1)
                            nc.vector.scalar_tensor_tensor(t1[:, k % 2, o], m[:, k, o], gain(*norm, k),
                                                           rstd[:, s % 2, tokens(cols, half)], ALU.mult, ALU.mult)\
                                .then_inc(t1_ready, 1)
                        if k == 5 and half == 1:
                            stat_recip(s + 1, cols, 0)
                        if k >= 2:
                            low_x(i + 1, *pre, k - 2, cols, half)
                        elif k == 0 and half == 0:
                            half_tile(KT - 2, 1)
                        elif k == 1 and half == 0:
                            add_square(i, KT - 2, cols, 1)
                            half_tile(KT - 1, 1)
                stat_recip(s + 1, cols, 1)
                dve.wait_ge(rstd_ready, stat_count(s + 1, 1))

            def mlp(layer, cols, s):
                b0 = B_MLP[layer]
                pos = block_slice(cols)
                w = cols[1] - cols[0]
                c0 = slice(*cols)
                for c in range(FF_CHUNKS):
                    if c < FF_CHUNKS:
                        f = 5 * layer + c + 1
                        n0 = 32 * layer + 8 * c

                        def low(j, s4):
                            dve.wait_ge(a_hi, j + (8 * f + 1))
                            dve.wait_ge(sqr_ready, j + (n0 + 1))
                            nc.vector.tensor_tensor(tile(al[f % 2], j, slice(0, w)), act2[:, s4 % 2, 0:w],
                                                    tile(ah[f % 2], j, slice(0, w)).bitcast(F32), ALU.subtract)\
                                .then_inc(a_ready, 1)

                        def up(b, j, s4):
                            dve.wait_ge(block_done, b + 1)
                            if n0 or c or not isinstance(j, int) or j >= 2:
                                dve.wait_ge(sqr_ready, j + (n0 - 1))
                            nc.vector.scalar_tensor_tensor(t1[:, s4 % 2, 0:w], G[s4 % 2][:, pos], 0.0, rstd[:, s % 2, c0],
                                                           ALU.max, ALU.mult).then_inc(tile_out, 1)
                            low(j, s4)
                        if f == 1:
                            for j in range(8):
                                up(b0 + UP[c] + j, j, (b0 + UP[c] + j) % 4)
                        else:
                            blocks(dve, b0 + UP[c], 8, up)
                    if 1 <= c < FF_CHUNKS:
                        out_tiles(b0 + DOWN[c - 1], cols, None if c == 1 else b0 + DOWN[c - 2])

            nc.vector.memset(eps_t[:, 0:1], EPS).then_inc(oss_set, 1)
            nc.vector.memset(eps_t[:, 1:2], GN_EPS).then_inc(oss_set, 1)
            nc.vector.memset(oss[:], 1.0).then_inc(oss_set, 1)
            dve.wait_ge(vec_loaded, 16)
            lam = vec[:, V_LAM:V_LAM + 256].rearrange("p (a b n) -> p a b n", a=2, b=2)
            for a in range(2):
                nc.vector.tensor_tensor_reduce(lamt[:, a, :], lam[:, a, 0, :], lam[:, a, 1, :], 1.0, 0.0, ALU.mult,
                                               ALU.add, lamd[:, a:a + 1]).then_inc(lam_prod, 1)
            nc.vector.tensor_scalar(gsub[:], vec[:, V_SUBLN:V_SUBLN + 1], 1.0 - LAM_INIT, None, ALU.mult)\
                .then_inc(lam_ready, 1)
            for k in range(KT):
                low_x(0, 0, 0, k, ALL)
            stat_recip(0, ALL)
            dve.wait_ge(lam_exp, 1)
            nc.vector.tensor_scalar(lamd[:, 4:5], lamd[:, 3:4], lamd[:, 2:3], -LAM_INIT, ALU.subtract, ALU.add)\
                .then_inc(lam_ready, 1)
            dve.wait_ge(rstd_ready, 1)
            dve.wait_ge(lam_ready, 2)
            _, pos = where(ALL)

            def scale_heads(h):
                hs = slice(5 * h, 5 * h + 5)
                dve.wait_ge(orms_ready, h + 1)
                nc.vector.reciprocal(orstd[:, hs], orms[:, hs]).then_inc(orstd_ready, 1)
                dve.wait_ge(orstd_ready, h + 1)
                if h >= 2:
                    dve.wait_ge(ot_ready, h - 1)
                for i in range(5):
                    rows = queries(i)[1]
                    t = 5 * h + i
                    nc.vector.tensor_scalar(o_sc[0:rows, h % 2, i, :], o_all[0:rows, h % 2, i, :], orstd[0:rows, t:t + 1],
                                            None, ALU.mult).then_inc(osc_ready, 1)

            def differences(t):
                i = t % 5
                rows, w = queries(i)[1], span(i)
                dve.wait_ge(prob_ready, 2 * t + 2)
                nc.vector.reciprocal(rden[0:rows, :, t:t + 1], den[0:rows, :, t:t + 1]).then_inc(coef_step, 1)
                dve.wait_ge(coef_step, 2 * t + 1)
                nc.vector.scalar_tensor_tensor(coef[0:rows, t:t + 1], rden[0:rows, 1, t:t + 1], lamd[0:rows, 4:5],
                                               den[0:rows, 0, t:t + 1], ALU.mult, ALU.mult).then_inc(coef_step, 1)
                dve.wait_ge(coef_step, 2 * t + 2)
                nc.vector.scalar_tensor_tensor(prob[0:rows, t % 2, 1, 0:w], prob[0:rows, t % 2, 1, 0:w],
                                               coef[0:rows, t:t + 1], prob[0:rows, t % 2, 0, 0:w],
                                               ALU.mult, ALU.add).then_inc(a_done, 1)

            def head_low(h):
                dve.wait_ge(a_hi, h + 1)
                nc.vector.scalar_tensor_tensor(al[0][:, h, :], ST[:, where(NEED)[1]], gsub[:, 0:1],
                                               ah[0][:, h, :].bitcast(F32), ALU.mult, ALU.subtract).then_inc(a_ready, 1)

            for s in range(TURNS):
                cur = tiles(s)
                if s % 3 == 2 and turned_head(s) is not None:
                    head_low(turned_head(s))
                for n in cur:
                    h, i = divmod(n, 5)
                    q0, rows = queries(i)
                    w = span(i)
                    sh = META + P * 3 - q0
                    dve.wait_ge(bias_ready, h + 1)
                    for c in range(2):
                        dve.wait_ge(scores_ready, 2 * n + c + 1)
                        if n >= 2:
                            dve.wait_ge(prob_ready, 2 * n + c - 3)
                        nc.vector.tensor_tensor_reduce(negs[0:rows, n % 2, c, 0:w], (G[1], ST)[c][0:rows, S0:S0 + w],
                                                       biasT[0:rows, h % 2, sh:sh + w], -1.0, 3e38, ALU.add, ALU.min,
                                                       nmax[0:rows, c, n:n + 1]).then_inc(negs_ready, 1)
                if s % 3 == 1 and 0 <= (s - 7) // 3 < HEADS - 1:
                    scale_heads((s - 7) // 3)
                for t in cur[:1]:
                    differences(t)
                if s < 24:
                    h, r = divmod(s, 3)
                    dve.wait_ge(block_done, s + 1)
                    nc.vector.scalar_tensor_tensor((qT, kT, vT)[r][:, h % 2, :], qkv_acc(s)[:, pos], 0.125 if r == 0 else 1.0,
                                                   rstd[:, 0, :], ALU.mult, ALU.mult).then_inc(tile_out, 1)
                for t in cur[1:]:
                    differences(t)
            scale_heads(HEADS - 1)
            head_low(HEADS - 1)
            last_tiles(0, B_AO, NEED, None, (0, 1), (0, 2))
            mlp(0, NEED, 2)
            last_tiles(1, B_MLP[0] + DOWN[3], NEED, B_MLP[0] + DOWN[2], (0, 3), (1, 0))

            _, pos = where(NEED)
            c0 = slice(*NEED)
            w = NEED[1] - NEED[0]
            for j in range(KT):
                for r in range(3):
                    b = B_CI + 3 * j + r
                    dve.wait_ge(block_done, b + 1)
                    if j >= 1 and r == 0:
                        dve.wait_ge(conv_step, 5 * j)
                    nc.vector.scalar_tensor_tensor(cb[:, r, :], G[b % 2][:, pos], 1.0, rstd[:, 0, c0], ALU.mult, ALU.mult)\
                        .then_inc(tile_out, 1)
                dve.wait_ge(tile_out, B_CI + 3 * j + 3)
                taps = [vec[:, V_CONV + CW * j + i:V_CONV + CW * j + i + 1] for i in range(CW)]
                nc.vector.tensor_tensor(cb[:, 2, :], cb[:, 2, :], cb[:, 1, :], ALU.mult).then_inc(conv_step, 1)
                dve.wait_ge(conv_step, 5 * j + 1)
                y = m[:, j, 2:2 + SEQ]
                nc.vector.tensor_scalar(y, cb[:, 2, 0:SEQ], taps[0], None, ALU.mult).then_inc(conv_step, 1)
                dve.wait_ge(conv_step, 5 * j + 2)
                for i in (1, 2):
                    nc.vector.scalar_tensor_tensor(y, cb[:, 2, i:i + SEQ], taps[i], y, ALU.mult, ALU.add)\
                        .then_inc(conv_step, 1)
                    dve.wait_ge(conv_step, 5 * j + 2 + i)
                nc.vector.tensor_tensor(y, y, cb[:, 0, 2:2 + SEQ], ALU.mult).then_inc(conv_step, 1)
                dve.wait_ge(conv_step, 5 * j + 5)
                dve.wait_ge(a_hi, 40 + j + 1)
                nc.vector.tensor_tensor(al[1][:, j, 0:SEQ], y, ah[1][:, j, 0:SEQ].bitcast(F32), ALU.subtract)\
                    .then_inc(a_ready, 1)
            last_tiles(2, B_CO, OUT, None, (1, 1), (1, 2))
            mlp(1, OUT, 6)
            last_tiles(3, B_MLP[1] + DOWN[3], OUT, B_MLP[1] + DOWN[2], (1, 3), (2, 0))

            dve.wait_ge(con2_loaded, 16)
            nc.vector.memset(z[:, :, 0:1], 0.0).then_inc(S("pads_set"), 1)
            nc.vector.memset(zu[:, :, 0:PAD], 0.0).then_inc(S("pads_set"), 1)
            nc.vector.memset(t1[:, :, 0:PAD], 0.0).then_inc(S("pads_set"), 1)
            dve.wait_ge(S("pads_set"), 3)
            for j in range(25):
                b = B_IN2 + j
                dst = z[:, Z_SLOT[j], 1:] if j < 13 else zu[:, j - 13, PAD:] if j < 17 else gate[:, j - 17]
                dve.wait_ge(block_done, b + 1)
                nc.vector.scalar_tensor_tensor(dst, G[b % 2][:, block_slice(OUT)], 1.0, rstd[:, 0, META:], ALU.mult, ALU.mult)\
                    .then_inc(tile_out, 1)
                if 1 <= j <= 13:
                    i = j - 1
                    zi = z[:, Z_SLOT[i]]
                    dve.wait_ge(tile_out, b)
                    if i >= 2:
                        dve.wait_ge(S("shifted"), i - 1)
                    nc.vector.tensor_tensor(t1[:, i % 2, PAD:], zi[:, 0:SEQ], zi[:, 1:], ALU.subtract)\
                        .then_inc(S("shift_step"), 1)
                    dve.wait_ge(S("shift_step"), i + 1)
                    nc.vector.scalar_tensor_tensor(zi[:, 1:], t1[:, i % 2, PAD:], col(V_MU, Z_SLOT[i]), zi[:, 1:], ALU.mult,
                                                   ALU.add).then_inc(S("shifted"), 1)
                p, i = feature_step(j)
                if i == 0 and p or j == 2 + 5 * PAIRS:
                    q = (j - 2) // 5 - 1
                    dve.wait_ge(S("bonus_sum"), q + 1)
                    nc.vector.tensor_tensor(bonus[:, q], bank(7), z[:, 9 + q, 1:], ALU.mult).then_inc(S("bonus_ready"), 1)
                if i is None:
                    continue
                zk, zr = z[:, 1 + p, 1:], z[:, 5 + p, 1:]
                if i == 1:
                    dve.wait_ge(S("sg_ready"), p + 1)
                    nc.vector.tensor_tensor_scan(cs[:], con[:, C_RESET:C_RESET + SEQ], sg[:], 0.0, ALU.mult, ALU.add)\
                        .then_inc(S("cs_ready"), 1)
                    dve.wait_ge(S("cs_ready"), p + 1)
                    nc.vector.tensor_tensor(Gp[:], cs[:], sg[:], ALU.subtract).then_inc(S("cp_ready"), 1)
                    dve.wait_ge(S("av_ready"), p + 1)
                    dve.wait_ge(S("cp_ready"), p + 1)
                    nc.vector.tensor_scalar(sg[:], av[:], 1.0, col(V_KA, p), ALU.subtract, ALU.mult)\
                        .then_inc(S("ka_ready"), 1)
                    dve.wait_ge(S("ka_ready"), p + 1)
                    dve.wait_ge(S("shifted"), 3 * p + 2)
                    nc.vector.scalar_tensor_tensor(k2[:], sg[:], 1.0, zk, ALU.add, ALU.mult).then_inc(S("k2_ready"), 1)
                elif i == 2:
                    dve.wait_ge(S("kn_ready"), p + 1)
                    nc.vector.tensor_scalar(kn[:], kn[:], 1e-12, None, ALU.max).then_inc(S("km_ready"), 1)
                    dve.wait_ge(S("km_ready"), p + 1)
                    nc.vector.reciprocal(kn[:], kn[:]).then_inc(S("kr_ready"), 1)
                elif i == 3:
                    dve.wait_ge(S("Gp_ready"), p + 1)
                    dve.wait_ge(S("k2_ready"), p + 1)
                    dve.wait_ge(S("shifted"), 3 * p + 3)
                    nc.vector.scalar_tensor_tensor(sg[:], zr, col(V_RK, p), k2[:], ALU.mult, ALU.mult)\
                        .then_inc(S("rk_ready"), 1)
                    dve.wait_ge(S("kr_ready"), p + 1)
                    nc.vector.scalar_tensor_tensor(cs[:], zk, col(V_KK, p), kn[:], ALU.mult, ALU.mult)\
                        .then_inc(S("kk_ready"), 1)
                    nc.vector.tensor_tensor(zr, zr, Gt[:], ALU.mult).then_inc(S("R_ready"), 1)
                    dve.wait_ge(S("kk_ready"), p + 1)
                    nc.vector.scalar_tensor_tensor(zk, cs[:], -1.0, Gp[:], ALU.mult, ALU.mult).then_inc(S("al_ready"), 1)
                    nc.vector.tensor_tensor(av[:], cs[:], av[:], ALU.mult).then_inc(S("bb_ready"), 1)
                elif i == 4:
                    nc.vector.tensor_copy(g_end[:, p], chunks(Gt[:])[:, :, CH - 1]).then_inc(S("end_ready"), 1)
                    dve.wait_ge(S("bb_ready"), p + 1)
                    dve.wait_ge(S("R_ready"), p + 1)
                    dve.wait_ge(S("al_ready"), p + 1)
                    for x in range(2):
                        r = ROW[x]
                        nc.vector.tensor_tensor(BK[r, p, :, x, :], chunks(av[r]), chunks(Gi[r]), ALU.mult)\
                            .then_inc(S("BK_ready"), 1)
                        nc.vector.tensor_tensor(BK[r, p, :, 1 - x, :], chunks(k2[r]), chunks(Gi[r]), ALU.mult)\
                            .then_inc(S("BK_ready"), 1)

            for t in (ET[:], BD[:], at_):
                nc.vector.memset(t, 0.0).then_inc(S("zeroed"), 1)
            dve.wait_ge(S("zeroed"), 3)

            def mask(c0):
                return con[:, c0:c0 + CH].unsqueeze(1).to_broadcast([P, 4, CH])

            def system(p, name, k):
                n2 = 2 * p + k + 1

                def add_out(need, dst, base, based, done):
                    dve.wait_ge(S(need), n2)
                    dve.wait_ge(S(based), n2)
                    nc.vector.tensor_tensor(dst, chunks(bank(4 + k)[:, 0:4 * CH]), base[:, HALF[k]], ALU.add)\
                        .then_inc(S(done), 1)

                if name == "gram":
                    x, g = divmod(k, 2)
                    r = ROW[x]
                    dve.wait_ge(S("gram_ready"), 4 * p + k + 1)
                    gram = bank(2 * (1 - x) + g).rearrange("p (c t) -> p c t", t=2 * CH)
                    nc.vector.tensor_tensor(MR[p % 2][x][:, HALF[g]], gram[:, :, CH:], mask(C_MR), ALU.mult)\
                        .then_inc(S("gram_out"), 1)
                    nc.vector.tensor_tensor(DL[x][:, HALF[g]], gram[:, :, 0:CH], mask(C_MDL + CH * x), ALU.mult)\
                        .then_inc(S("gram_out"), 1)
                    nc.vector.tensor_tensor(ET[r, HALF[g], own(x)], gram[r, :, 0:CH], mask(C_ME)[r], ALU.mult)\
                        .then_inc(S("gram_out"), 1)
                elif name == "lm":
                    dve.wait_ge(S("lm_ready"), n2)
                    nc.vector.tensor_tensor(Dm[:, HALF[k]], chunks(bank(4 + k)[:, 0:4 * CH]), mask(C_MD), ALU.mult)\
                        .then_inc(S("D_out"), 1)
                elif name == "rv":
                    dve.wait_ge(S("gram_out"), 12 * (p + 1))
                    for x in range(2):
                        r = ROW[x]
                        eye = con[r, C_IDENT + HD * x:C_IDENT + HD * x + HD].unsqueeze(1).to_broadcast([HD, NCH, CH])
                        nc.vector.tensor_tensor(Ya[r], DL[x][r], eye, ALU.add).then_inc(S("y1_out"), 1)
                elif name == "y2":
                    dve.wait_ge(S("y1_out"), 2 * (p + 1))
                    add_out("y2_ready", Yb[:, HALF[k]], Ya, "D_out", "y2_out")
                elif name == "y3":
                    add_out("y3_ready", Ya[:, HALF[k]], Yb, "y2_out", "y3_out")
                elif name == "y4":
                    add_out("y4_ready", Yb[:, HALF[k]], Ya, "y3_out", "y4_out")
                elif name == "z1":
                    add_out("z1_ready", Ya[:, HALF[k]], Yb, "y4_out", "z1_out")
                elif name == "z2":
                    add_out("z2_ready", D4m[:, HALF[k]], Yb, "y4_out", "z2_out")
                elif name == "z3":
                    add_out("z3_ready", Ya[:, HALF[k]], Yb, "y4_out", "z3_out")

            def tail(p, name, c):
                U = UV[p % 2]
                if name == "u":
                    if c == 0:
                        dve.wait_ge(S("q_out"), p + 1)
                        for x in range(2):
                            nc.vector.tensor_copy(U[x][ROW[x], 0, :], BK[ROW[x], p, 0, 0, :]).then_inc(S("u_out"), 1)
                        return
                    if c < NCH - 1:
                        dve.wait_ge(S("s_out"), (NCH - 1) * p + c)
                        nc.vector.tensor_scalar(Sg[:], state(p, c), g_end[:, p, c:c + 1], None, ALU.mult)\
                            .then_inc(S("sg_out"), 1)
                    dve.wait_ge(S("u_ready"), (NCH - 1) * p + c)
                    for x in range(2):
                        nc.vector.tensor_tensor(U[x][ROW[x], c, :], bank(6)[ROW[x], 0:CH], BK[ROW[x], p, c, 0, :], ALU.add)\
                            .then_inc(S("u_out"), 1)
                elif name == "s":
                    end = g_end[:, p, c:c + 1]
                    dve.wait_ge(S("s_ready"), (NCH - 1) * p + c + 1)
                    if c == 0:
                        nc.vector.tensor_scalar(state(p, 1), bank(6)[:, CH:2 * CH], end, None, ALU.mult)\
                            .then_inc(S("s_out"), 1)
                    else:
                        dve.wait_ge(S("sg_out"), (NCH - 2) * p + c)
                        nc.vector.scalar_tensor_tensor(state(p, c + 1), bank(6)[:, CH:2 * CH], end, Sg[:], ALU.mult, ALU.add)\
                            .then_inc(S("s_out"), 1)
                elif name == "mu":
                    dve.wait_ge(S("yt_out"), p + 1)
                    dve.wait_ge(S("mu_ready"), p + 1)
                    nc.vector.scalar_tensor_tensor(gn_c, bank(7), -1.0 / HD, gn_y, ALU.mult, ALU.add)\
                        .then_inc(S("yc_ready"), 1)
                elif name == "norm":
                    if c < 4:
                        if c == 0:
                            dve.wait_ge(S("sd_ready"), p + 1)
                        q = slice(P * c, P * c + P)
                        nc.vector.reciprocal(gn_y[:, q], gn_sd[:, q]).then_inc(S("rs_ready"), 1)
                    elif c == 4:
                        dve.wait_ge(S("rs_ready"), 4 * (p + 1))
                        nc.vector.scalar_tensor_tensor(gn_c, gn_c, col(V_GG, p), gn_y, ALU.mult, ALU.mult)\
                            .then_inc(S("yn_ready"), 1)
                    elif c == 5:
                        dve.wait_ge(S("yn_ready"), p + 1)
                        nc.vector.scalar_tensor_tensor(gn_c, gn_c, col(V_GB, p), bonus[:, p], ALU.add, ALU.add)\
                            .then_inc(S("yw_ready"), 1)
                    else:
                        dve.wait_ge(S("yw_ready"), p + 1)
                        dve.wait_ge(S("gate_ready"), 5 + p)
                        nc.vector.tensor_tensor(z[:, 5 + p, 1:], gn_c, gate[:, 4 + p], ALU.mult).then_inc(S("yb_ready"), 1)

            def last_low(k):
                src = zu[:, k, PAD:] if k < 4 else z[:, 1 + k, 1:]
                dve.wait_ge(x_hi, x_base(5) + k + 1)
                nc.vector.tensor_tensor(x2l[:, k, META:], src, x2h[:, k, META:].bitcast(F32), ALU.subtract)\
                    .then_inc(x_ready, 1)

            for steps in (STEPS, ENDS):
                if steps is ENDS:
                    last_low(0)
                    last_low(1)
                for kind, n, name, g in steps:
                    if kind == system_:
                        system(n, name, g)
                    elif kind == tail_:
                        tail(n, name, g)
                    elif kind == out_:
                        if n + 2 < KT - 1:
                            last_low(n + 2)
                    else:
                        dve.wait_ge(S("mix_ready"), n + 1)
                        dve.wait_ge(S("gate_ready"), n + 1)
                        nc.vector.scalar_tensor_tensor(zu[:, n, PAD:], bank(6 + n % 2), col(V_POOL, n), gate[:, n], ALU.mult,
                                                       ALU.mult).then_inc(S("ya_ready"), 1)

            last_low(KT - 1)
            for j in range(KT):
                if j < OPEN - 1:
                    dve.wait_ge(S("sum_ready"), j + 1)
                else:
                    dve.wait_ge(block_done, B_O2 + j + 1)
                nc.vector.tensor_tensor(hres[:, j, META:], bank(j), hres[:, j, META:], ALU.add).then_inc(tile_out, 1)
                if j >= 1:
                    add_square(4, j - 1, OUT)
            stat_recip(9, OUT)
            dve.wait_ge(rstd_ready, stat_count(9))
            for k in range(KT):
                nc.vector.scalar_tensor_tensor(hres[:, k, META:], hres[:, k, META:], col(V_FG, k), rstd[:, 1, META:], ALU.mult,
                                               ALU.mult).then_inc(S("out_ready"), 1)

        @block.tensor
        def _(pe):
            def stat_tile(s, k, cols, half=None):
                if k == 0 and s >= 1:
                    pe.wait_ge(rms_ready, stat_count(s - 1, half))
                pe.wait_ge(sq_ready, sq_base(s) + KT * (half or 0) + k + 1)
                for t0, t1_, p0, p1 in part(cols, half):
                    last = nc.tensor.matmul(ST[:, p0:p1], ones, sq[:, k % 2, t0 - cols[0]:t1_ - cols[0]], start=k == 0,
                                            stop=k == KT - 1, skip_group_check=True)
                last.then_inc(sq_used, 1)

            def post_stat(s, cols, half=None):
                off = cols[0]
                i = (s - 1) // 2
                pe.wait_ge(rms_ready, stat_count(s - 1, 1 if half is None else half))
                pe.wait_ge(psq_added, POST_ADD * i + KT - 1 + (half or 0))
                for t0, t1_, p0, p1 in part(cols, half):
                    nc.tensor.matmul(ST[:, p0:p1], ones, acc[:, t0 - off:t1_ - off], start=True, stop=False,
                                     skip_group_check=True)
                pe.wait_ge(psq_ready, POST_SQ * i + KT + 2 * (half or 0))
                for t0, t1_, p0, p1 in part(cols, half):
                    last = nc.tensor.matmul(ST[:, p0:p1], ones, sq[:, 1, t0 - off:t1_ - off], start=False, stop=True,
                                            skip_group_check=True)
                last.then_inc(post_sum, 1)

            last_of = [None]

            def some(to, w, ks, hi, lo, off, pieces):
                for k in ks:
                    ws = slice(k * P, k * P + P)
                    for q, (wt, xt) in enumerate(((whi, hi), (whi, lo), (wlo, hi))):
                        for t0, t1_, p0, p1 in pieces:
                            last_of[0] = nc.tensor.matmul(to[:, p0:p1], wt[:, w, ws], xt[:, k, t0 - off:t1_ - off],
                                                          start=k == 0 and q == 0, stop=k == KT - 1 and q == 2)

            def begin(b):
                pe.wait_ge(lo_ready, b + 1)
                if not isinstance(b, int) or b >= 2:
                    pe.wait_ge(tile_out, b - 1)

            def first_blocks(i, b0, hi, lo, cols):
                s = 2 * i + 2
                post_stat(s - 1, cols, 1)
                for half in range(2):
                    for j in range(2):
                        if half == 0:
                            begin(b0 + j)
                        for k in range(KT):
                            if j == 0:
                                pe.wait_ge(x_ready, x_base(i + 1) + KT * half + k + 1)
                                stat_tile(s, k, cols, half)
                            some(G[(b0 + j) % 2], (b0 + j) % 2, [k], hi, lo, 0, block_part(cols, half))
                        if half:
                            last_of[0].then_inc(block_done, 1)

            def last_blocks(i, b0, hi, lo, cols):
                operands = hi, lo, cols[0]
                for j in (KT - 2, KT - 1):
                    begin(b0 + j)
                    some(G[j % 2], j % 2, range(KT), *operands, part(cols, 0))
                    last_of[0].then_inc(half_done, 1)
                some(G[0], 0, range(KT // 2), *operands, part(cols, 1))
                post_stat(2 * i + 1, cols, 0)
                some(G[0], 0, range(KT // 2, KT), *operands, part(cols, 1))
                last_of[0].then_inc(block_done, 1)
                some(G[1], 1, range(KT), *operands, part(cols, 1))
                last_of[0].then_inc(block_done, 1)

            def product(b0, n, ready, first, hi, lo, cols, off, stat=None, lead=False, start=None, end=None, skip=0):
                def body(b, j, s, lead=False):
                    begin(b)
                    for k in range(KT):
                        if lead:
                            pe.wait_ge(ready, first + k + 1)
                            if stat is not None:
                                stat_tile(stat, k, cols)
                        some(G[s % 2], s % 2, [k], hi, lo, off, block_part(cols))
                    last_of[0].then_inc(block_done, 1)
                if n == 1:
                    body(b0, 0, b0 % 4, lead)
                    return
                if start is not None:
                    first_blocks(start, b0, hi, lo, cols)
                    skip = 2
                for j in range(skip, 4):
                    body(b0 + j, j, (b0 + j) % 4, j == 0)
                done = 4
                if n - 4 >= 8:
                    with pe.Fori(0, (n - 4) // 4) as i:
                        for u in range(4):
                            body(i * 4 + (b0 + 4 + u), i * 4 + (4 + u), (b0 + u) % 4)
                    done = 4 + (n - 4) // 4 * 4
                for j in range(done, n if end is None else n - 2):
                    body(b0 + j, j, (b0 + j) % 4)
                if end is not None:
                    last_blocks(end, b0, hi, lo, cols)

            def scores(n):
                h, i = divmod(n, 5)
                q0, rows = queries(i)
                pe.wait_ge(tile_out, 3 * h + 2)
                for c in range(2):
                    if n >= 1:
                        pe.wait_ge(negs_ready, 2 * n + c - 1)
                    if c == 0:
                        pe.wait_ge(v_copied, 2 * (h + 1))
                    elif n == 0:
                        pe.wait_ge(rms_ready, 1)
                    elif i == 4 and h >= 1:
                        pe.wait_ge(a_ready, h)
                    f = slice(64 * c, 64 * c + 64)
                    ps = (G[1], ST)[c]
                    qs = qT[f, h % 2, q0:q0 + rows]
                    last = nc.tensor.matmul(ps[0:rows, S0:S0 + META], qs, kT[f, h % 2, 0:META], start=True, stop=True)
                    if i > 0:
                        last = nc.tensor.matmul(ps[0:rows, BANK:BANK + P * i], qs, kT[f, h % 2, META:META + P * i],
                                                start=True, stop=True)
                    last.then_inc(scores_ready, 1)

            def turn_weights(t):
                i = t % 5
                rows = queries(i)[1]
                pe.wait_ge(a_done, t + 1)
                if t >= 1:
                    pe.wait_ge(at_copied, t)
                    if i == 4:
                        pe.wait_ge(o_copied, t)
                pr = prob[:, t % 2, 1]
                for j in range(1, i + 1):
                    nc.tensor.transpose(PO[:, P * (j - 1):P * j], pr[:, META + P * (j - 1):META + P * j], ident)
                mb, m0 = meta_bank(i)
                nc.tensor.transpose(mb[0:META, m0:m0 + rows], pr[0:rows, 0:META], ident[0:rows, 0:rows]).then_inc(at_ready, 1)

            def values(t):
                h, i = divmod(t, 5)
                rows = queries(i)[1]
                pe.wait_ge(at_copied, t + 1)
                if t >= 1:
                    pe.wait_ge(o_copied, t)
                for j, (_, nk) in enumerate(keys(i)):
                    last = nc.tensor.matmul(PV[0:rows, 0:P], aT[0:nk, t % 2, j, 0:rows], vtok[0:nk, h % 2, j, :],
                                            start=j == 0, stop=j == i)
                last.then_inc(o_ready, 1)

            def turn_values(h):
                pe.wait_ge(tile_out, 3 * h + 3)
                if h >= 1:
                    pe.wait_ge(negs_ready, 10 * h)
                for j in range(4):
                    nc.tensor.transpose(G[1][:, BANK + P * j:BANK + P * j + P], vT[:, h % 2, META + P * j:META + P * j + P],
                                        ident)
                nc.tensor.transpose(G[1][0:META, 0:P], vT[:, h % 2, 0:META], ident).then_inc(v_turned, 1)

            def turn_head(h, s):
                pe.wait_ge(osc_ready, 5 * (h + 1))
                pe.wait_ge(negs_ready, 10 * HEADS if s == TURNS - 1 else 2 * tiles(s)[0])
                for i in range(5):
                    q0, rows = queries(i)
                    p0 = q0 + BANK - SPLIT
                    last = nc.tensor.transpose(ST[:, p0:p0 + rows], o_sc[0:rows, h % 2, i, :], ident[0:rows, 0:rows])
                last.then_inc(ot_ready, 1)

            def quarter(s, i):
                ks = range(2 * i, 2 * i + 2)
                if s < 24:
                    if i == 0:
                        pe.wait_ge(lo_ready, s + 1)
                        if s >= 2:
                            pe.wait_ge(tile_out, s - 1 if s < 3 else s)
                    some(qkv_acc(s), s % 2, ks, xh, xl, 0, part(ALL))
                    if i == 3:
                        last_of[0].then_inc(block_done, 1)
                elif s - 24 == i:
                    if i == 0:
                        pe.wait_ge(lo_ready, B_AO + 1)
                        pe.wait_ge(tile_out, B_AO)
                    heads_out(0, ks)

            def heads_out(j, ks):
                pe.wait_ge(a_ready, ks[-1] + 1)
                some(G[j], j, ks, ah[0], al[0], NEED[0], part(NEED))
                if ks[-1] == HEADS - 1:
                    last_of[0].then_inc(block_done, 1)

            pe.wait_ge(con_loaded, 16)
            product(B_QKV, 1, x_ready, 0, xh, xl, ALL, 0, 0, lead=True)
            for s in range(1, TURNS):
                prev, cur = tiles(s - 1), tiles(s)
                if s % 3 == 0:
                    if cur:
                        turn_values(s // 3 - 1)
                    quarter(s, 0)
                    for n in cur:
                        scores(n)
                    quarter(s, 1)
                    quarter(s, 2)
                    for t in prev:
                        turn_weights(t)
                    if s < TURNS - 1:
                        quarter(s, 3)
                    for t in prev:
                        values(t)
                    if s == TURNS - 1:
                        pe.wait_ge(lo_ready, B_AO + 2)
                        pe.wait_ge(negs_ready, 10 * HEADS)
                        heads_out(0, [HEADS - 2])
                        heads_out(1, range(HEADS - 1))
                        turn_head(HEADS - 1, s)
                        for j in range(2):
                            heads_out(j, [HEADS - 1])
                else:
                    if s % 3 == 2 and turned_head(s) is not None:
                        turn_head(turned_head(s), s)
                    if s % 3 == 2:
                        quarter(s, 0)
                    for n in cur:
                        scores(n)
                    quarter(s, s % 3 - 1)
                    if prev:
                        turn_weights(prev[0])
                    if s % 3 == 1:
                        quarter(s, 1)
                    else:
                        quarter(s, 2)
                    if prev:
                        values(prev[0])
                        turn_weights(prev[1])
                    if s % 3 == 1:
                        quarter(s, 2)
                        if prev:
                            values(prev[1])
                        quarter(s, 3)
                    else:
                        quarter(s, 3)
                        if prev:
                            values(prev[1])

            product(B_AO, 8, a_ready, 0, ah[0], al[0], NEED, NEED[0], end=0, skip=2)

            def mlp(layer, cols, i):
                b0 = B_MLP[layer]
                for c in range(FF_CHUNKS + 1):
                    f = 5 * layer + c + 1
                    if c < FF_CHUNKS:
                        product(b0 + UP[c], 8, x_ready, 0, xh, xl, cols, 0, start=None if c else i)
                    if c >= 1:
                        product(b0 + DOWN[c - 1], 8, a_ready, 8 * (f - 1), ah[(f - 1) % 2], al[(f - 1) % 2], cols,
                                cols[0], end=i + 1 if c == FF_CHUNKS else None)

            mlp(0, NEED, 0)
            product(B_CI, 24, x_ready, 0, xh, xl, NEED, 0, start=1)
            product(B_CO, 8, a_ready, 40, ah[1], al[1], OUT, OUT[0], end=2)
            mlp(1, OUT, 2)

            blk = con[:, C_BLK:C_BLK + P]
            pe.wait_ge(con2_loaded, 16)
            pe.wait_ge(mat_loaded, 16)

            def mm(out_, lhsT, rhs, start=True, stop=True):
                return nc.tensor.matmul(out_, lhsT, rhs, start=start, stop=stop)

            for j in range(25):
                if j == 0:
                    first_blocks(3, B_IN2, x2h, x2l, OUT)
                elif j >= 2:
                    product(B_IN2 + j, 1, x_ready, 0, x2h, x2l, OUT, 0)
                p, i = feature_step(j)
                if i == 0 and p or j == 2 + 5 * PAIRS:
                    q = (j - 2) // 5 - 1
                    pe.wait_ge(S("rk_ready"), q + 1)
                    if q:
                        pe.wait_ge(S("bonus_ready"), q)
                    mm(bank(7), blk, sg[:]).then_inc(S("bonus_sum"), 1)
                if i == 0:
                    ps = slice(P * p, P * p + P)
                    if p == 0:
                        pe.wait_ge(S("tanh_ready"), 1)
                        pe.wait_ge(rms_ready, stat_count(8, 1))
                    else:
                        pe.wait_ge(S("av_ready"), p)
                    mm(bank(4), mat[0:HD, ps], tw[:]).then_inc(S("ww_ready"), 1)
                    mm(bank(5), mat[HD:P, ps], z[HD:P, 0, 1:]).then_inc(S("aa_ready"), 1)
                elif i == 1:
                    pe.wait_ge(S("ksq_ready"), p + 1)
                    if p:
                        pe.wait_ge(S("kn_ready"), p)
                    mm(bank(6), blk, kn[:]).then_inc(S("knorm_sum"), 1)

            def both(out_, lhsT, rhs, g):
                for c in range(4 * g, 4 * g + 4):
                    for x in range(2):
                        last = mm(out_(x, c), lhsT(x, c), rhs(x, c))
                return last

            def joint(out_, lhsT, rhs, g):
                for c in range(4 * g, 4 * g + 4):
                    last = mm(out_(c), lhsT[:, c, :], rhs[:, c, :])
                return last

            def of4(b):
                return lambda c: bank(b + c // 4)[:, CH * (c % 4):CH * (c % 4) + CH]

            def eye(x, c):
                return con[ROW[x], C_IDENT + HD * x:C_IDENT + HD * x + HD]

            def at4(b):
                return lambda x, c: bank(b + c // 4)[ROW[x], CH * (c % 4):CH * (c % 4) + CH]

            def at8(b, swap=False):
                return lambda x, c: bank(b)[ROW[1 - x if swap else x], CH * c:CH * c + CH]

            def of(t):
                return lambda x, c: t[ROW[x], c, :]

            def kind_of(t, kind):
                return lambda x, c: t[ROW[x], c // 4, kind, c % 4, :]

            def system(p, name, g):
                n2 = 2 * p + g + 1
                DT = lambda x, c: DL[x][ROW[x], c, :]
                LakT = lambda x, c: DL[x][ROW[1 - x], c, :]
                al = lambda x, c: alpha(p, x, c)
                halves = range(2)
                if name == "gram":
                    x, h = divmod(g, 2)
                    if p == 0 and g == 0:
                        pe.wait_ge(S("BK_ready"), 4 * PAIRS)
                        pe.wait_ge(tile_out, B_IN2 + 25)
                    elif p and x == 1:
                        pe.wait_ge(S(("q_out", "pt_out")[h]), p)
                    for c in range(4 * h, 4 * h + 4):
                        last = mm(bank(2 * (1 - x) + h)[:, 2 * CH * (c % 4):2 * CH * (c % 4 + 1)]
                                  .rearrange("p (k t) -> p k t", t=CH), BK[ROW[x], p, c].rearrange("p k t -> p (k t)"),
                                  z[ROW[x], 1 + p:6 + p:4, 1 + CH * c:1 + CH * c + CH])
                    last.then_inc(S("gram_ready"), 1)
                elif name == "lm":
                    both(at4(4), al, lambda x, c: BK[ROW[x], p, c, x, :], g).then_inc(S("lm_ready"), 1)
                elif name == "rv":
                    pe.wait_ge(S("gram_out"), 12 * p + 9)
                    pe.wait_ge(S("bonus_ready"), PAIRS)
                    for h in halves:
                        last = both(at8(0, True), lambda x, c: z[ROW[x], 9 + p, 1 + CH * c:1 + CH * c + CH], eye, h)
                    last.then_inc(S("rv_turned"), 1)
                elif name == "at":
                    pe.wait_ge(S("gram_out"), 12 * p + 12)
                    for h in halves:
                        last = both(at8(1), al, eye, h)
                    last.then_inc(S("at_turned"), 1)
                elif name == "D2":
                    pe.wait_ge(S("gram_out"), 12 * p + 9 + 3 * g)
                    pe.wait_ge(S("D_out"), n2)
                    both(lambda x, c: bank(2 + g)[ROW[x], CH * (c % 4):CH * (c % 4) + CH], DT, of(Dm), g)
                    both(lambda x, c: bank(2 + g)[ROW[x], CH * (4 + c % 4):CH * (5 + c % 4)], of(Dm), DT, g)\
                        .then_inc(S("d2_ready"), 1)
                elif name == "bk":
                    if g == 0:
                        pe.wait_ge(S("vt_out"), 2 * (p + 1))
                    else:
                        pe.wait_ge(S("at_out"), p + 1)
                    for c in range(NCH):
                        last = nc.tensor.transpose(bank(g)[:, CH * c:CH * c + CH],
                                                   BK[ROW[g], p, c].rearrange("p k t -> p (k t)"), eye(g, c))
                    last.then_inc(S("bk_turned"), 1)
                elif name == "w":
                    pe.wait_ge(S("bk_out"), 2 * p + 1)
                    for h in halves:
                        last = both(at8(0), LakT, lambda x, c: UV[p % 2][x][ROW[1 - x], c, :], h)
                    last.then_inc(S("w_ready"), 1)
                elif name == "D4":
                    pe.wait_ge(S("d2_out"), n2)
                    both(lambda x, c: bank(2 + g)[ROW[x], CH * (c % 4):CH * (c % 4) + CH], kind_of(PB2, 1), kind_of(PB2, 0), g)
                    both(lambda x, c: bank(2 + g)[ROW[x], CH * (4 + c % 4):CH * (5 + c % 4)], kind_of(PB2, 0),
                         kind_of(PB2, 1), g).then_inc(S("d4_ready"), 1)
                elif name == "y2":
                    pe.wait_ge(S("y1_out"), 2 * (p + 1))
                    both(at4(4), kind_of(PB2, 0), of(Ya), g).then_inc(S("y2_ready"), 1)
                elif name == "D8":
                    pe.wait_ge(S("d4_out"), n2)
                    joint(of4(2), BD, D4m, g).then_inc(S("d8_ready"), 1)
                elif name == "y3":
                    pe.wait_ge(S("y2_out"), n2)
                    both(at4(4), of(D4m), of(Yb), g).then_inc(S("y3_ready"), 1)
                elif name == "y4":
                    pe.wait_ge(S("y3_out"), n2)
                    pe.wait_ge(S("d8_out"), n2)
                    joint(of4(4), BD, Ya, g).then_inc(S("y4_ready"), 1)
                elif name == "td":
                    pe.wait_ge(S("y4_out"), n2)
                    both(at4(4), of(Yb), eye, g).then_inc(S("td_ready"), 1)
                elif name == "ht":
                    pe.wait_ge(S("td_out"), n2)
                    for c in range(4 * g, 4 * g + 4):
                        last = mm(of4(4)(c), ET[:, c, :], PB2[:, g, 0, c % 4, :])
                    last.then_inc(S("ht_ready"), 1)
                elif name in ("z1", "z2", "z3"):
                    need, src = {"z1": ("ht_out", Yb), "z2": ("z1_out", Ya), "z3": ("z2_out", D4m)}[name]
                    pe.wait_ge(S(need), n2)
                    joint(of4(4), BD, src, g).then_inc(S(name + "_ready"), 1)
                elif name == "q":
                    pe.wait_ge(S("z3_out"), 2 * p + 2)
                    pe.wait_ge(S("w_out"), p + 1)
                    for h in halves:
                        last = both(at8(0), of(Ya), of(Wm), h)
                    last.then_inc(S("q_ready"), 1)
                elif name == "pt":
                    pe.wait_ge(S("bk_out"), 2 * p + 2)
                    for h in halves:
                        last = joint(lambda c: bank(1)[:, CH * c:CH * c + CH], at_, Ya, h)
                    last.then_inc(S("pt_ready"), 1)

            def tail(p, name, c):
                U = UV[p % 2]
                if name == "u" and c:
                    if c == 1:
                        pe.wait_ge(S("pt_out"), p + 1)
                    pe.wait_ge(S("s_out"), (NCH - 1) * p + c)
                    for x in range(2):
                        last = mm(bank(6)[ROW[x], 0:CH], BK[ROW[x], p, c, 1, :], state(p, c)[ROW[x]])
                    last.then_inc(S("u_ready"), 1)
                elif name == "s":
                    if p == 0 and c == 0:
                        pe.wait_ge(S("ya_ready"), 3)
                    pe.wait_ge(S("u_out"), 2 * (NCH * p + c + 1))
                    for x in range(2):
                        last = mm(bank(6)[ROW[x], CH:2 * CH], BKt[p % 2][x][:, c, :], U[x][:, c, :])
                    last.then_inc(S("s_ready"), 1)
                elif name == "y":
                    x = c
                    if x == 0:
                        pe.wait_ge(S("u_out"), 2 * NCH * (p + 1))
                        if p == 0:
                            pe.wait_ge(S("ya_ready"), 4)
                        else:
                            pe.wait_ge(S("sd_ready"), p)
                    for c in range(NCH):
                        o = at8(7)(x, c)
                        last = mm(o, U[x][:, c, :], MR[p % 2][x][:, c, :], stop=c == 0)
                        if c >= 1:
                            last = mm(o, state(p, c)[ROW[x]], rcv(p, x, c), start=False)
                    if x == 1:
                        last.then_inc(S("y_ready"), 1)
                elif name == "mu":
                    pe.wait_ge(S("yt_out"), p + 1)
                    mm(bank(7), blk, gn_y).then_inc(S("mu_ready"), 1)
                elif name == "var":
                    pe.wait_ge(S("ysq_ready"), p + 1)
                    mm(bank(7), blk, gn_sd).then_inc(S("var_ready"), 1)

            def last_tile(i):
                o, k = O2_TILES[i]
                if i % KT == 0:
                    pe.wait_ge(lo_ready, B_O2 + i // KT + 1)
                if o == 0:
                    pe.wait_ge(x_ready, x_base(5) + k + 1)
                if (o, k) == (0, 0):
                    pe.wait_ge(S("q_out"), PAIRS)
                    pe.wait_ge(S("pt_out"), PAIRS)
                if (o, k) == (OPEN, 0):
                    pe.wait_ge(S("sd_ready"), PAIRS)
                w, ws = (B_O2 + i // KT) % 2, slice(P * (i % KT), P * (i % KT) + P)
                for q, (wt, xt) in enumerate(((whi, x2h), (whi, x2l), (wlo, x2h))):
                    last = mm(bank(o), wt[:, w, ws], xt[:, k, META:], k == 0 and q == 0, k == KT - 1 and q == 2)
                if i % KT == KT - 1:
                    last.then_inc(block_done, 1)
                elif k == KT - 1:
                    last.then_inc(S("sum_ready"), 1)

            for steps in (STEPS, ENDS):
                for kind, n, name, g in steps:
                    if kind == system_:
                        system(n, name, g)
                    elif kind == tail_:
                        tail(n, name, g)
                    elif kind == out_:
                        last_tile(n)
                    else:
                        pe.wait_ge(S("pooled"), n + 1)
                        if n >= 2:
                            pe.wait_ge(S("ya_ready"), n - 1)
                        mm(bank(6 + n % 2), mat[:, SEQ + P * n:SEQ + P * n + P], (Gt, Gi, cs, Gp)[n][:])\
                            .then_inc(S("mix_ready"), 1)

            for i in range(O2_EARLY, KT * KT):
                last_tile(i)
            post_stat(9, OUT)


def layout(v):
    return v.reshape(-1, P).T


def weight_blocks(w):
    n = w.shape[1] // P
    return w.reshape(KT, P, n, P).transpose(2, 1, 0, 3).reshape(n, P, KT * P)


def kernel(**inputs):
    import concourse.bacc as bacc
    from concourse.bass_utils import run_bass_kernel_spmd as run

    a = {k: np.asarray(v) for k, v in inputs.items()}
    xT = np.ascontiguousarray(np.concatenate([a["meta_tokens"], a["x"][0]], axis=0).T)
    lam = np.broadcast_to(a["lambda_params"].reshape(1, 256), (P, 256))
    conv = a["conv_w"][0].reshape(CW, KT, P).transpose(2, 1, 0).reshape(P, KT * CW)
    mu = layout(a["shift_mu_2"])[:, [12, *range(4, 8), *range(0, 4), *range(8, 12)]]
    second = [layout(a[n]) for n in ("w0_2", "a0_2", "k_k_2", "k_a_2", "r_k_2", "gn_gain_2", "gn_bias_2", "final_gain_2")]
    vecs = np.ascontiguousarray(np.concatenate([layout(a["norm_g"]), layout(a["subln_g"]), conv, lam,
                                                layout(a["norm_gain_2"]), layout(a["pool_scale_2"]), mu, *second], axis=1))
    mats = np.concatenate([np.concatenate([a["w_up_2"][0], a["a_up_2"][0]], axis=0),
                           a["pool_w_2"][0].transpose(1, 0, 2).reshape(P, SEQ)], axis=1)

    q = np.arange(P)[:, None]
    dist = np.arange(TOK)[None, :] - META - 3 * P - q
    dist = np.where(dist > 0, MASKED, dist)
    heads = np.kron(np.eye(2), np.ones((HD, HD)))
    i, j = np.arange(CH)[:, None], np.arange(CH)[None, :]
    near = i // SUB == j // SUB
    twice = lambda m: np.concatenate([m, m], axis=0)
    diag, strict = near & (i < j), i < j
    mdl = np.concatenate([np.concatenate([diag, strict]), np.concatenate([strict, diag])], axis=1)
    reset = np.broadcast_to(np.arange(SEQ) % CH != 0, (P, SEQ))
    pos = np.arange(16)
    fix = np.concatenate([w / np.minimum(pos + 1, w) for w in POOL_W])
    consts = np.concatenate([np.eye(P), np.ones((P, P)), dist, heads, mdl, twice(i <= j), twice(strict & ~near),
                             twice(near & (j < i)), reset, np.broadcast_to(fix, (P, 64))], axis=1).astype(np.float32)

    def interleave(w, n):
        b = weight_blocks(w)
        return b.reshape(n, KT, P, D).transpose(1, 0, 2, 3).reshape(n * KT, P, D)

    def mlp_blocks(up, down):
        u = weight_blocks(up).reshape(FF_CHUNKS, KT, P, D)
        d = [weight_blocks(down[c * D:(c + 1) * D]) for c in range(FF_CHUNKS)]
        return [u[0], u[1], d[0], u[2], d[1], u[3], d[2], d[3]]

    w = [interleave(a["w_in"][0], 3), weight_blocks(a["w_out"][0])]
    w += mlp_blocks(a["w_up"][0], a["w_down"][0])
    w += [interleave(a["w_in"][1], 3), weight_blocks(a["w_out"][1])]
    w += mlp_blocks(a["w_up"][1], a["w_down"][1])
    w2 = weight_blocks(a["w_in_2"][0])
    w += [w2[[20, *(i + p for p in range(PAIRS) for i in (12, 8, 16)), *range(0, 8), *range(21, 25)]]]
    last = weight_blocks(a["w_out_2"][0])
    last = np.stack([last[o, :, k * P:k * P + P] for o, k in O2_TILES])
    w += [last.reshape(KT, KT, P, P).transpose(0, 2, 1, 3).reshape(KT, P, D)]
    weights = np.concatenate(w, axis=0)

    nc = bacc.Bacc("TRN2", target_bir_lowering=False, num_devices=1)
    arrays, args = {}, []
    for name, v in (("xT", xT), ("vecs", vecs), ("consts", consts), ("mats", mats), ("weights", weights)):
        arrays[name + "_dram"] = v
        args.append(nc.dram_tensor(name + "_dram", v.shape, F32, kind="ExternalInput").ap())
    args.append(nc.dram_tensor("out_dram", (D, SEQ), F32, kind="ExternalOutput").ap())
    program(nc, *args)
    r = run(nc, [arrays], core_ids=[0])
    return np.ascontiguousarray(r.results[0]["out_dram"].T)[None]
```
